# Optimizing a Trainium2 kernel written in Bass

```python
import jax, jax.numpy as jnp
from jax import lax
import numpy as np

D_MODEL = 4096
BATCH = 1
SEQ = 256
DEPTH = 1
DEC_BATCH = 1
DEC_SEQ = 32
PAST_LEN = 128

CHUNK = 64
N_META = 16
EPS = 1e-6
V_HEAD = 128
QK_NOPE = 128
QK_ROPE = 64
Q_LORA = 1536
KV_LORA = 512
MLA_HEADS = (D_MODEL // 2) // V_HEAD
MLA_WIDTH = MLA_HEADS * V_HEAD
ATTN_SCALE = (QK_NOPE + QK_ROPE) ** -0.5
ROPE_THETA = 10000.0
Q_BLOCK = 128
ML_DV = 512
ML_DQK = 256
ML_HEADS = (D_MODEL // 2) // ML_DV
ML_WIDTH = ML_HEADS * ML_DV
ML_BLOCK = 16
D_MIX = MLA_WIDTH + ML_WIDTH
OFF_CQ = 0
OFF_CKV = OFF_CQ + Q_LORA
OFF_KPE = OFF_CKV + KV_LORA
OFF_MQ = OFF_KPE + QK_ROPE
OFF_MK = OFF_MQ + ML_HEADS * ML_DQK
OFF_MV = OFF_MK + ML_HEADS * ML_DQK
OFF_MO = OFF_MV + ML_WIDTH
OFF_MI = OFF_MO + ML_WIDTH
OFF_MF = OFF_MI + ML_HEADS
OFF_ZA = OFF_MF + ML_HEADS
OFF_ZB = OFF_ZA + MLA_WIDTH
IN_COLS = OFF_ZB + ML_WIDTH

kernel_name = 'hymba_mla_mlstm_streaming_step'

def rmsnorm(x, g):
    xf = x.astype(jnp.float32)
    y = xf * lax.rsqrt(jnp.mean(xf * xf, axis=-1, keepdims=True) + EPS)
    return (y * g.astype(jnp.float32)).astype(x.dtype)

def rope(x, pos):
    half = QK_ROPE // 2
    inv_freq = ROPE_THETA ** (-jnp.arange(half, dtype=jnp.float32) / half)
    ang = pos.astype(jnp.float32)[:, None] * inv_freq[None, :]
    cos = jnp.cos(ang)[None, :, None, :]
    sin = jnp.sin(ang)[None, :, None, :]
    xf = x.astype(jnp.float32)
    x1, x2 = xf[..., :half], xf[..., half:]
    return jnp.concatenate([x1 * cos - x2 * sin, x2 * cos + x1 * sin], axis=-1).astype(x.dtype)

def chunk_id(p):
    return jnp.where(p < N_META, 0, (p - N_META) // CHUNK + 1)

def project(h, w_in):
    p = h @ w_in
    return (p[..., OFF_CQ:OFF_CKV], p[..., OFF_CKV:OFF_KPE], p[..., OFF_KPE:OFF_MQ],
            p[..., OFF_MQ:OFF_MK], p[..., OFF_MK:OFF_MV], p[..., OFF_MV:OFF_MO],
            p[..., OFF_MO:OFF_MI], p[..., OFF_MI:OFF_MF], p[..., OFF_MF:OFF_ZA],
            p[..., OFF_ZA:OFF_ZB], p[..., OFF_ZB:IN_COLS])

def mla_latent(ckv_raw, kpe_raw, pos, kv_a_norm, k_rope_norm):
    ckv = rmsnorm(ckv_raw, kv_a_norm)
    kpe = rope(rmsnorm(kpe_raw, k_rope_norm)[:, :, None, :], pos)[:, :, 0, :]
    return ckv, kpe

def mla_queries(cq_raw, pos, q_a_norm, w_q_up, q_nope_norm, q_rope_norm):
    B, T, _ = cq_raw.shape
    q = (rmsnorm(cq_raw, q_a_norm) @ w_q_up).reshape(B, T, MLA_HEADS, QK_NOPE + QK_ROPE)
    q_nope = rmsnorm(q[..., :QK_NOPE], q_nope_norm)
    q_pe = rope(rmsnorm(q[..., QK_NOPE:], q_rope_norm), pos)
    return q_nope, q_pe

def mla_expand(ckv, w_kv_up, k_nope_norm):
    B, S, _ = ckv.shape
    kv = (ckv @ w_kv_up).reshape(B, S, MLA_HEADS, QK_NOPE + V_HEAD)
    return rmsnorm(kv[..., :QK_NOPE], k_nope_norm), kv[..., QK_NOPE:]

def mla_attend(q_nope, q_pe, k_nope, k_pe, v, mask):
    s = (jnp.einsum('bqhd,bshd->bhqs', q_nope, k_nope)
         + jnp.einsum('bqhd,bsd->bhqs', q_pe, k_pe)).astype(jnp.float32) * ATTN_SCALE
    if mask is not None:
        s = jnp.where(mask[None, None], s, -jnp.inf)
    p = jax.nn.softmax(s, axis=-1).astype(v.dtype)
    return jnp.einsum('bhqs,bshd->bqhd', p, v)

def mla_prompt_attention(q_nope, q_pe, k_nope, k_pe, v):
    B, T = q_nope.shape[:2]
    n_qb = -(-T // Q_BLOCK)
    pad = n_qb * Q_BLOCK - T
    qn = jnp.pad(q_nope, ((0, 0), (0, pad), (0, 0), (0, 0)))
    qp = jnp.pad(q_pe, ((0, 0), (0, pad), (0, 0), (0, 0)))
    cid_k = chunk_id(jnp.arange(T))

    def one_block(i):
        start = i * Q_BLOCK
        cid_q = chunk_id(start + jnp.arange(Q_BLOCK))
        mask = cid_q[:, None] >= cid_k[None, :]
        return mla_attend(lax.dynamic_slice_in_dim(qn, start, Q_BLOCK, 1),
                          lax.dynamic_slice_in_dim(qp, start, Q_BLOCK, 1), k_nope, k_pe, v, mask)

    out = lax.map(one_block, jnp.arange(n_qb))
    return jnp.moveaxis(out, 0, 1).reshape(B, n_qb * Q_BLOCK, MLA_HEADS, V_HEAD)[:, :T]

def mlstm_block(carry, blk):
    C0, n0, m0 = carry
    q, k, v, ig, lf = blk
    L = q.shape[2]
    b = jnp.cumsum(lf, axis=-1)
    a = b + m0[..., None]
    D = b[..., :, None] - b[..., None, :] + ig[..., None, :]
    D = jnp.where(jnp.tril(jnp.ones((L, L), dtype=bool)), D, -jnp.inf)
    m = jnp.maximum(a, D.max(axis=-1))
    w_inter = jnp.exp(a - m)
    qk = jnp.einsum('bhtd,bhsd->bhts', q, k) * jnp.exp(D - m[..., None])
    num = w_inter[..., None] * jnp.einsum('bhtd,bhde->bhte', q, C0) + jnp.einsum('bhts,bhse->bhte', qk, v)
    den = w_inter * jnp.einsum('bhtd,bhd->bht', q, n0) + qk.sum(axis=-1)
    h = num / jnp.maximum(jnp.abs(den), jnp.exp(-m))[..., None]
    bL = b[..., -1]
    g = bL[..., None] - b + ig
    mL = jnp.maximum(bL + m0, g.max(axis=-1))
    decay = jnp.exp(bL + m0 - mL)
    ws = jnp.exp(g - mL[..., None])
    C1 = decay[..., None, None] * C0 + jnp.einsum('bhs,bhsd,bhse->bhde', ws, k, v)
    n1 = decay[..., None] * n0 + jnp.einsum('bhs,bhsd->bhd', ws, k)
    return (C1, n1, mL), h

def mlstm_branch(mq, mk, mv, mo, mi, mf, b_igate, b_fgate, ml_out_norm, state, block):
    B, T, _ = mq.shape
    f32 = jnp.float32
    heads = lambda a, d: a.reshape(B, T, ML_HEADS, d).transpose(0, 2, 1, 3).astype(f32)
    q = heads(mq, ML_DQK)
    k = heads(mk, ML_DQK) * (ML_DQK ** -0.5)
    v = heads(mv, ML_DV)
    ig = (mi + b_igate).astype(f32).transpose(0, 2, 1)
    lf = jax.nn.log_sigmoid((mf + b_fgate).astype(f32)).transpose(0, 2, 1)
    nb = T // block
    to_blocks = lambda a: jnp.moveaxis(a.reshape(B, ML_HEADS, nb, block, *a.shape[3:]), 2, 0)
    state = tuple(s.astype(f32) for s in state)
    state, h = lax.scan(mlstm_block, state,
                        (to_blocks(q), to_blocks(k), to_blocks(v), to_blocks(ig), to_blocks(lf)))
    h = jnp.moveaxis(h, 0, 2).reshape(B, ML_HEADS, T, ML_DV).transpose(0, 2, 1, 3)
    h = jax.nn.sigmoid(mo.astype(f32)).reshape(B, T, ML_HEADS, ML_DV) * rmsnorm(h, ml_out_norm)
    return h.reshape(B, T, ML_WIDTH).astype(mq.dtype), state

def merge(x_res, attn, za, ml_h, zb, w_out):
    B, T, _ = x_res.shape
    a = attn.reshape(B, T, MLA_WIDTH) * jax.nn.silu(za)
    m = ml_h * jax.nn.silu(zb)
    return x_res + jnp.concatenate([a, m], axis=-1) @ w_out

def prompt_path(x, params):
    (meta_tokens, norm_gain, w_in, b_igate, b_fgate, q_a_norm, w_q_up, q_nope_norm, q_rope_norm,
     kv_a_norm, k_rope_norm, w_kv_up, k_nope_norm, ml_out_norm, w_out) = params
    B, S, _ = x.shape
    T = N_META + S
    seq = jnp.concatenate([jnp.broadcast_to(meta_tokens.astype(x.dtype)[None], (B, N_META, D_MODEL)), x], axis=1)
    pos = jnp.arange(T)
    cq, ckv_raw, kpe_raw, mq, mk, mv, mo, mi, mf, za, zb = project(rmsnorm(seq, norm_gain), w_in)
    ckv, kpe = mla_latent(ckv_raw, kpe_raw, pos, kv_a_norm, k_rope_norm)
    q_nope, q_pe = mla_queries(cq, pos, q_a_norm, w_q_up, q_nope_norm, q_rope_norm)
    k_nope, v = mla_expand(ckv, w_kv_up, k_nope_norm)
    attn = mla_prompt_attention(q_nope, q_pe, k_nope, kpe, v)
    state0 = (jnp.zeros((B, ML_HEADS, ML_DQK, ML_DV), jnp.float32),
              jnp.zeros((B, ML_HEADS, ML_DQK), jnp.float32),
              jnp.zeros((B, ML_HEADS), jnp.float32))
    ml_h, (C, n, m) = mlstm_branch(mq, mk, mv, mo, mi, mf, b_igate, b_fgate, ml_out_norm, state0, ML_BLOCK)
    y = merge(seq, attn, za, ml_h, zb, w_out)[:, N_META:]
    return y, ckv, kpe, C, n, m

def sample_path(x, cache_ckv, cache_kpe, state, params):
    (meta_tokens, norm_gain, w_in, b_igate, b_fgate, q_a_norm, w_q_up, q_nope_norm, q_rope_norm,
     kv_a_norm, k_rope_norm, w_kv_up, k_nope_norm, ml_out_norm, w_out) = params
    B, L, _ = x.shape
    P = cache_ckv.shape[1]
    mp = rmsnorm(meta_tokens.astype(x.dtype), norm_gain)[None] @ w_in[:, OFF_CKV:OFF_MQ]
    meta_ckv, meta_kpe = mla_latent(mp[..., :KV_LORA], mp[..., KV_LORA:], jnp.arange(N_META), kv_a_norm, k_rope_norm)
    pos = N_META + P + jnp.arange(L)
    cq, ckv_raw, kpe_raw, mq, mk, mv, mo, mi, mf, za, zb = project(rmsnorm(x, norm_gain), w_in)
    ckv_new, kpe_new = mla_latent(ckv_raw, kpe_raw, pos, kv_a_norm, k_rope_norm)
    q_nope, q_pe = mla_queries(cq, pos, q_a_norm, w_q_up, q_nope_norm, q_rope_norm)
    ckv_all = jnp.concatenate([jnp.broadcast_to(meta_ckv, (B, N_META, KV_LORA)),
                               cache_ckv.astype(ckv_new.dtype), ckv_new], axis=1)
    kpe_all = jnp.concatenate([jnp.broadcast_to(meta_kpe, (B, N_META, QK_ROPE)),
                               cache_kpe.astype(kpe_new.dtype), kpe_new], axis=1)
    k_nope, v = mla_expand(ckv_all, w_kv_up, k_nope_norm)
    attn = mla_attend(q_nope, q_pe, k_nope, kpe_all, v, None)
    ml_h, (C, n, m) = mlstm_branch(mq, mk, mv, mo, mi, mf, b_igate, b_fgate, ml_out_norm, state, L)
    y = merge(x, attn, za, ml_h, zb, w_out)
    return y, ckv_new, kpe_new, C, n, m

def setup_inputs(seed: int = 0) -> dict:
    key = jax.random.key(seed)
    ks = jax.random.split(key, 24)
    nrm = lambda k, shape, s=1.0: s * jax.random.normal(k, shape, jnp.float32)
    gain = lambda k, shape: 1.0 + 0.02 * jax.random.normal(k, shape, jnp.float32)
    return {
        'x_prompt': nrm(ks[0], (BATCH, SEQ, D_MODEL)),
        'x_sample': nrm(ks[1], (DEC_BATCH, DEC_SEQ, D_MODEL)),
        'cache_ckv': nrm(ks[2], (DEC_BATCH, PAST_LEN, KV_LORA)),
        'cache_kpe': nrm(ks[3], (DEC_BATCH, PAST_LEN, QK_ROPE)),
        'state_C': nrm(ks[4], (DEC_BATCH, ML_HEADS, ML_DQK, ML_DV), 0.1),
        'state_n': nrm(ks[5], (DEC_BATCH, ML_HEADS, ML_DQK), 0.5),
        'state_m': nrm(ks[6], (DEC_BATCH, ML_HEADS)),
        'meta_tokens': nrm(ks[7], (N_META, D_MODEL)),
        'norm_gain': gain(ks[8], (D_MODEL,)),
        'w_in': nrm(ks[9], (D_MODEL, IN_COLS), D_MODEL ** -0.5),
        'b_igate': nrm(ks[10], (ML_HEADS,), 0.1),
        'b_fgate': 3.0 + nrm(ks[11], (ML_HEADS,), 0.1),
        'q_a_norm': gain(ks[12], (Q_LORA,)),
        'w_q_up': nrm(ks[13], (Q_LORA, MLA_HEADS * (QK_NOPE + QK_ROPE)), Q_LORA ** -0.5),
        'q_nope_norm': gain(ks[14], (QK_NOPE,)),
        'q_rope_norm': gain(ks[15], (QK_ROPE,)),
        'kv_a_norm': gain(ks[16], (KV_LORA,)),
        'k_rope_norm': gain(ks[17], (QK_ROPE,)),
        'w_kv_up': nrm(ks[18], (KV_LORA, MLA_HEADS * (QK_NOPE + V_HEAD)), KV_LORA ** -0.5),
        'k_nope_norm': gain(ks[19], (QK_NOPE,)),
        'ml_out_norm': gain(ks[20], (ML_HEADS, ML_DV)),
        'w_out': nrm(ks[21], (D_MIX, D_MODEL), D_MIX ** -0.5),
    }

def reference(x_prompt, x_sample, cache_ckv, cache_kpe, state_C, state_n, state_m, meta_tokens, norm_gain,
              w_in, b_igate, b_fgate, q_a_norm, w_q_up, q_nope_norm, q_rope_norm, kv_a_norm, k_rope_norm,
              w_kv_up, k_nope_norm, ml_out_norm, w_out):
    params = (meta_tokens, norm_gain, w_in, b_igate, b_fgate, q_a_norm, w_q_up, q_nope_norm, q_rope_norm,
              kv_a_norm, k_rope_norm, w_kv_up, k_nope_norm, ml_out_norm, w_out)
    y_prompt, ckv_p, kpe_p, C_p, n_p, m_p = prompt_path(x_prompt, params)
    y_sample, ckv_s, kpe_s, C_s, n_s, m_s = sample_path(x_sample, cache_ckv, cache_kpe,
                                                        (state_C, state_n, state_m), params)
    return (y_prompt, y_sample, ckv_p, kpe_p, C_p, n_p, m_p, ckv_s, kpe_s, C_s, n_s, m_s)


_drawn_inputs = setup_inputs


def setup_inputs(seed=0):
    import zlib

    import numpy as np

    out = dict(_drawn_inputs(seed))
    spreads = {}
    factors = {'q_a_norm': 8.0,
     'q_nope_norm': 8.0,
     'q_rope_norm': 8.0,
     'kv_a_norm': 2.787,
     'k_rope_norm': 2.83,
     'k_nope_norm': 8.0,
     'ml_out_norm': 8.0}
    for name, (base, spread) in spreads.items():
        noise = np.random.default_rng([zlib.crc32(name.encode()), seed]).standard_normal(out[name].shape)
        drawn = base * np.exp(spread * noise) if base else spread * noise
        out[name] = __import__('jax').numpy.asarray(drawn.astype(out[name].dtype))
    for name, factor in factors.items():
        out[name] = (out[name] * factor).astype(out[name].dtype)
    return out
```

```python
from contextlib import ExitStack

import concourse.bass as bass
import numpy as np
from concourse import mybir

D_MODEL = 4096
SEQ, DEC, PAST, N_META = 256, 32, 128, 16
KV_LORA, Q_LORA, ROPE = 512, 1536, 64
MLA_HEADS, NOPE, V_HEAD = 16, 128, 128
ML_HEADS, DQK, DV = 4, 256, 512
OFF_CQ = 0
OFF_CKV = OFF_CQ + Q_LORA
OFF_KPE = OFF_CKV + KV_LORA
OFF_MQ = OFF_KPE + ROPE
OFF_MK = OFF_MQ + ML_HEADS * DQK
OFF_MV = OFF_MK + ML_HEADS * DQK
OFF_MO = OFF_MV + ML_HEADS * DV
OFF_MI = OFF_MO + ML_HEADS * DV
OFF_ZA = OFF_MI + 2 * ML_HEADS
OFF_ZB = OFF_ZA + MLA_HEADS * V_HEAD
EPS = 1e-6
ATTN_SCALE = (NOPE + ROPE) ** -0.5
CHUNK = 64
NEG = -1e30

P = 128
NT = N_META + SEQ + DEC
NQ = SEQ + DEC
NKV = NT + PAST
C_SAMPLE = N_META + SEQ
KT = D_MODEL // P
KQ = Q_LORA // P
KC = KV_LORA // P
TOK = [(0, 128), (128, 128), (256, 48)]
TAIL = C_SAMPLE - 256
QT = [(0, 128), (128, 128), (256, 32)]
MQT = [(0, 112), (112, 128), (240, 48)]
MLW = [(0, 288), (288, 176), (464, 48)]

RAW_SLOTS = 4
HL_SLOTS = 4
AHEAD = HL_SLOTS - 1
U_CQ = 0
U_CKV = U_CQ + 3 * KT
U_NAR = U_CKV + KT
NAR_UNITS = 8
U_PAIR = U_NAR + NAR_UNITS
PAIR_UNITS = KQ + KC
U_ML = U_PAIR + (MLA_HEADS // 2) * PAIR_UNITS
U_GATE = U_ML + ML_HEADS * 2 * KT
U_OUT = U_GATE + 12 * KT

PHASES = [
    ("gain", 1, (0, 0, 0, 0, 1, 0, 0, 0)),
    ("x", 1, (0, 0, 0, 0, 8, 8, 8, 8)),
    ("cq", 3, (1, 1, 1, 1, 0, 0, 0, 0)),
    ("ckv", 1, (1, 1, 1, 1, 1, 0, 0, 0)),
    ("narrow", 1, (1, 0, 0, 0, 0, 0, 0, 0)),
    ("latent", 1, (0, 0, 0, 0, 2, 2, 3, 3)),
    ("bulk0", 1, (2, 2, 2, 1, 1, 1, 1, 1)),
    ("step", 7, (2, 2, 2, 1, 3, 5, 4, 4)),
    ("ml0qk", 1, (1, 1, 1, 1, 2, 4, 3, 3)),
    ("rows", 1, (0, 0, 0, 0, 1, 1, 1, 1)),
    ("ml0v", 1, (1, 1, 1, 1, 0, 0, 0, 0)),
    ("ml", 3, (2, 2, 2, 2, 4, 5, 6, 5)),
    ("gate0", 1, (1, 1, 1, 1, 4, 5, 6, 5)),
    ("gate", 11, (1, 1, 1, 1, 0, 0, 0, 0)),
    ("nout", 1, (0, 0, 0, 0, 1, 0, 0, 0)),
    ("out0", 1, (1, 1, 1, 1, 0, 0, 0, 0)),
    ("out", 7, (1, 1, 1, 1, 1, 1, 1, 0)),
    ("outlast", 1, (0, 0, 0, 0, 1, 1, 1, 0)),
]


def bank_base():
    base, total = {}, [0] * 8
    for name, times, uses in PHASES:
        base[name] = (list(total), uses)
        total = [t + times * u for t, u in zip(total, uses)]
    return base


BASE = bank_base()


def use(phase, bank, nth=0, i=0):
    before, uses = BASE[phase]
    return before[bank] + nth + i * uses[bank]


CONST_PARTS = [("ident", 128), ("blockones", 128), ("ones", 128), ("rot", 128), ("dup", 128),
               ("cos", NT), ("sin", NT), ("causal_ind", 128), ("causal_neg", 64),
               ("rowmask", 4)]
CONST_AT = {}
_n = 0
for _name, _w in CONST_PARTS:
    CONST_AT[_name] = (_n, _w)
    _n += _w
CONST_COLS = _n
G_X, G_QA, G_KVA, G_MLO, G_QN, G_KN, G_QR, G_KR, G_N0 = 0, 32, 44, 48, 64, 65, 66, 67, 68
G_ROWS = 76


def shape_constants():
    t = np.zeros((P, CONST_COLS), np.float32)

    def part(name):
        a, w = CONST_AT[name]
        return t[:, a:a + w]

    part("ident")[:] = np.eye(P, dtype=np.float32)
    for b in range(2):
        part("blockones")[64 * b:64 * b + 64, 64 * b:64 * b + 64] = 1.0
        for f in range(32):
            part("rot")[64 * b + 32 + f, 64 * b + f] = -1.0
            part("rot")[64 * b + f, 64 * b + 32 + f] = 1.0
        for f in range(64):
            part("dup")[f, 64 * b + f] = 1.0
    part("ones")[:] = 1.0
    pos = np.concatenate([np.arange(C_SAMPLE), N_META + PAST + np.arange(DEC)]).astype(np.float32)
    inv = np.float32(10000.0) ** (-np.arange(32, dtype=np.float32) / np.float32(32))
    ang = (pos[None, :] * inv.astype(np.float32)[:, None]).astype(np.float32)
    part("cos")[:] = np.tile(np.cos(ang), (4, 1))
    part("sin")[:] = np.tile(np.sin(ang), (4, 1))
    part("causal_ind")[0, 0:CHUNK] = 1.0
    part("causal_neg")[0, :] = NEG
    part("rowmask")[:, 0:2] = 1.0
    part("rowmask")[0:TAIL, 2] = 1.0
    part("rowmask")[TAIL:48, 3] = 1.0
    mask = np.zeros((P, 512), np.float32)
    for (c0, rows), (at, width) in zip(TOK, MLW):
        s = c0 + np.arange(rows)
        q = NT - width + np.arange(width)
        same = (s[:, None] < C_SAMPLE) == (q[None, :] < C_SAMPLE)
        mask[:rows, at:at + width] = (s[:, None] <= q[None, :]) & same
    return t, mask


def hymba_step(nc, x_prompt, x_sample, cache_ckv, cache_kpe, state_C, state_n, state_m, meta, norm_gain,
               w_in, b_ig, b_fg, q_a, w_qu, q_nope, q_rope, kv_a, k_rope, w_kvu, k_nope, ml_out, w_out,
               consts, mlmask,
               y_p, y_s, ckv_p, kpe_p, C_p, n_p, m_p, ckv_s, kpe_s, C_s, n_s, m_s):
    f32, f32r = mybir.dt.float32, mybir.dt.float32r
    ALU, ACT, AX = mybir.AluOpType, mybir.ActivationFunctionType, mybir.AxisListType
    ds = bass.ds

    ctx = ExitStack()
    with ctx:
        def keep(stack):
            return lambda name, shape, dt=f32: stack.enter_context(nc.sbuf_tensor(name, shape, dt))

        def sem(name):
            return ctx.enter_context(nc.semaphore(name))

        sb = keep(ctx)
        raw = sb("raw", [P, RAW_SLOTS, 1024])
        whi = sb("whi", [P, HL_SLOTS, 512], f32r)
        wlo = sb("wlo", [P, HL_SLOTS, 512], f32r)
        con = sb("con", [P, CONST_COLS])
        G = sb("G", [P, G_ROWS])
        nraw = sb("nraw", [72, NT])
        epsc = sb("epsc", [P, 1])
        gate_b = sb("gate_b", [ML_HEADS, 3])
        attnT = sb("attnT", [P, MLA_HEADS, NQ])

        def c(name, rows=P):
            a, w = CONST_AT[name]
            return con[0:rows, a:a + w]

        ident, blockones, ones, rot, dup = c("ident"), c("blockones"), c("ones"), c("rot"), c("dup", 64)
        cosT, sinT = c("cos"), c("sin")

        px = ExitStack()
        xhi = keep(px)("xhi", [P, KT, NT], f32r)
        xlo = keep(px)("xlo", [P, KT, NT], f32r)

        p1 = ExitStack()
        xt = [keep(p1)(f"xt{t}", [P, D_MODEL]) for t in range(3)]
        Grows = keep(p1)("Grows", [G_ROWS, P])
        xss = keep(p1)("xss", [P, 3])
        xrs = keep(p1)("xrs", [P, 3])
        p1.close()

        p2 = ExitStack()
        sb2 = keep(p2)
        cqhi = sb2("cqhi", [P, KQ, NQ], f32r)
        cqlo = sb2("cqlo", [P, KQ, NQ], f32r)
        ckhi = sb2("ckhi", [P, KC, NKV], f32r)
        cklo = sb2("cklo", [P, KC, NKV], f32r)
        kpe2 = [sb2(f"kpe{h}", [P, NKV]) for h in range(2)]
        qn = sb2("qn", [P, 2, NQ])
        qp = sb2("qp", [P, NQ])
        kn = sb2("kn", [P, 2, NKV])
        vt = sb2("vt", [P, 4, 2 * V_HEAD])
        sqb = sb2("sqb", [P, 3 * NQ])
        rsb = sb2("rsb", [P, 3 * NQ])
        rope1 = sb2("rope1", [P, NT])
        rope2 = sb2("rope2", [P, NT])
        rotq = sb2("rotq", [P, P])
        nmax = sb2("nmax", [P, 3])
        psum_ = sb2("psumrow", [P, 3])
        pinv = sb2("pinv", [P, 3])
        gsc = sb2("gsc", [P, 2])
        pa = ExitStack()
        prob = keep(pa)("prob", [P, 608])
        probT = keep(pa)("probT", [P, 736])
        pa.close()
        ckvf = sb2("ckvf", [P, KC, NT])
        p2.close()
        cqraw = attnT
        sq3 = sqb[:, :].rearrange("p (t n) -> p t n", t=3)
        sq2 = sqb[:, :].rearrange("p (t n) -> p t n", t=2)
        rs3 = rsb[:, :].rearrange("p (t n) -> p t n", t=3)
        rs2 = rsb[:, :].rearrange("p (t n) -> p t n", t=2)
        kpr = kn[:, 0, 0:NT]
        kpe_n = kn[:, 1, 0:NT]
        orow = vt[:, :, :].rearrange("p a b -> p (a b)")
        cacher = orow[:, 0:640]
        kout = qn[:, 0, 0:192]
        sqk0 = sq2[:, 0, 0:NT]

        p3 = ExitStack()
        sb3 = keep(p3)
        hT = sb3("hT", [P, 16, NQ])
        mask = sb3("mask", [P, 512])
        kws = sb3("kws", [P, 4, DQK])
        vtok = sb3("vtok", [P, 3, DV])
        E = sb3("E", [P, 512])
        Pt = sb3("Pt", [P, 512])
        Mb = sb3("Mb", [P, NT + 1])
        Mh = sb3("Mh", [ML_HEADS, NT + 1])
        rows = {n: sb3(n, [ML_HEADS, NT + 1]) for n in ("ig", "xf", "lf", "bsum", "crow", "Mrow", "mrow")}
        ccol = sb3("ccol", [P, 3, ML_HEADS])
        emcol = sb3("emcol", [P, 3, ML_HEADS])
        wi = sb3("wi", [P, DEC])
        nML = sb3("nML", [P, 2])
        wtmp = sb3("wtmp", [P, 4])
        decay = sb3("decay", [P, 1])
        qw = sb3("qw", [P, 2, 48])
        C0 = sb3("C0", [P, 2, DV])
        Cout = sb3("Cout", [P, 4, DV])
        ncol = sb3("ncol", [P, 16])
        nrow = sb3("nrow", [16, P])
        dsb = sb3("dsb", [P, 3])
        dinv = sb3("dinv", [P, 3])
        hss = sb3("hss", [P, 3])
        hfac = sb3("hfac", [P, 3])
        hn = sb3("hn", [P, 3, DV])
        pm = ExitStack()
        mqT = keep(pm)("mqT", [P, 2, NT])
        mkT = keep(pm)("mkT", [P, 2, NT])
        mvT = keep(pm)("mvT", [P, 4, NT])
        pm.close()
        sg = sb3("sg", [P, 4, NQ])
        gt = sb3("gt", [P, 4, NQ])
        p3.close()
        p4 = ExitStack()
        keep(p4)("hT_", [P, 16, NQ])
        yT = keep(p4)("yT", [P, 4, NQ])
        ytok = keep(p4)("ytok", [P, 3, 512])
        xres = keep(p4)("xres", [P, 3, 512])
        p4.close()
        px.close()
        p5 = ExitStack()
        mhi = keep(p5)("mhi", [P, KT, NQ], f32r)
        mlo = keep(p5)("mlo", [P, KT, NQ], f32r)
        p5.close()

        bank = [ctx.enter_context(nc.psum_tensor(f"bank{b}", [P, 512], f32)) for b in range(8)]
        full = [sem(f"bank{b}_full") for b in range(8)]
        free = [sem(f"bank{b}_free") for b in range(8)]

        raw_in = [sem(f"raw{s}_in") for s in range(RAW_SLOTS)]
        hi_done = sem("hi_done")
        lo_done = sem("lo_done")
        unit_used = sem("unit_used")
        const_in, grows_in, eps_set = sem("const_in"), sem("grows_in"), sem("eps_set")
        xrow_in = [sem(f"xrow{t}_in") for t in range(3)]
        xsq, xln, xrstd, xscaled, xhi_d = (sem(n) for n in ("x_squares", "x_ln", "x_rstd", "x_scaled", "x_hi"))
        cq_sq, cq_ssm, cq_rs, cq_n, cq_hi, cq_lo = (sem(n) for n in (
            "cq_squares", "cq_summed", "cq_rstd", "cq_normed", "cq_hi", "cq_lo"))
        ck_sq, ck_ssm, ck_rs, ck_n, ck_hi, ck_lo = (sem(n) for n in (
            "ckv_squares", "ckv_summed", "ckv_rstd", "ckv_normed", "ckv_hi", "ckv_lo"))
        cache_in = sem("cache_in")
        kp_sq, kp_rs, kp_c, kp_a, kp_n = (sem(n) for n in (
            "kpe_squares", "kpe_rstd", "kpe_cos", "kpe_added", "kpe_normed"))
        kp_st, kp_zero, kp_rows, ck_out, ck_tail_out, kp_out = (sem(n) for n in (
            "kpe_stored", "kpe_zeroed", "kpe_rows", "ckv_out", "ckv_tail_out", "kpe_out"))
        gsc_d = sem("scaled_gains")
        q_sq, q_rs, q_fin = (sem(n) for n in ("q_squares", "q_rstd", "q_normed"))
        k_sq, k_rs, k_fin = (sem(n) for n in ("k_squares", "k_rstd", "k_normed"))
        qp_c, qp_a, qp_fin = (sem(n) for n in ("qpe_cos", "qpe_added", "qpe_normed"))
        v_ev = sem("v_evict")
        mx, ex, pn, pt_d = (sem(n) for n in ("neg_max", "exp_done", "probs_normed", "probT_minor"))
        mask_in, gb_in = sem("mask_in"), sem("gate_bias_in")
        r_v, r_abs, r_e, r_l, r_c, r_em = (sem(n) for n in ("row_vec", "row_abs", "row_exp", "row_ln", "ccol_done", "emcol_done"))
        m_out = sem("m_out")
        mh_d, e_d, e_x, e_m, p_d = (sem(n) for n in ("Mh_done", "E_diff", "E_exp", "E_masked", "Pt_done"))
        nml_s, nml_d, wt_p, wt_d, wt_x, wt_m, wi_d, dec_d, kws_d = (sem(n) for n in (
            "nML_prompt", "nML_sample", "wtmp_prompt", "wtmp_sample", "wtmp_exp", "wtmp_masked", "wi_done",
            "decay_done", "kws_done"))
        qw_z, qw_d = sem("qw_zero"), sem("qw_done")
        C0_in, Cp_out, Cs_out = sem("C0_in"), sem("C_prompt_out"), sem("C_sample_out")
        den_d, dab_d, dmx_d, din_d = (sem(n) for n in ("den_copied", "den_abs", "den_max", "den_inv"))
        hsq_d, hln_d, hrs_d, hf_d = (sem(n) for n in ("h_squares", "h_ln", "h_rstd", "h_factor"))
        n_d, n_out = sem("n_prompt_done"), sem("n_out")
        sg_d, gm_d = sem("sigmoid_done"), sem("gate_applied")
        mix_hi, mix_lo = sem("mix_hi"), sem("mix_lo")
        xres_in, y_out = sem("xres_in"), sem("y_out")
        passed_pe, passed_pool = sem("passed_pe"), sem("passed_pool")

        w_in_t = w_in.rearrange("(k p) c -> p k c", p=P)
        w_qu_t = w_qu.rearrange("(k p) c -> p k c", p=P)
        w_kvu_t = w_kvu.rearrange("(k p) c -> p k c", p=P)
        w_out_t = w_out.rearrange("(k p) c -> p k c", p=P)
        w_qk_t = w_in[:, OFF_MQ:OFF_MV].rearrange("(k p) (s c) -> p k s c", p=P, s=2)

        block = ctx.enter_context(nc.Block())

        @block.sync
        def _(sp):
            def load(b, slot, dst, src):
                if not isinstance(b, int) or b >= RAW_SLOTS:
                    sp.wait_ge(lo_done, 2 * b - 2 * RAW_SLOTS + 2)
                sp.dma_start(dst, src).then_inc(raw_in[slot], 16)

            def group(b0, col, src=w_in_t, blocks=KT // 2, width=512):
                for n in range(blocks):
                    s = n % RAW_SLOTS
                    dst = raw[:, s, 0:2 * width].rearrange("p (k c) -> p k c", k=2)
                    load(b0 + n, s, dst, src[:, 2 * n:2 * n + 2, ds(col, width)])

            group(0, OFF_CQ)
            with sp.Fori(1, 3) as i:
                group(i * (KT // 2), OFF_CQ + i * 512)
            group(U_CKV // 2, OFF_CKV)
            for n in range(NAR_UNITS // 2):
                b = U_NAR // 2 + n
                dst = raw[:, n % RAW_SLOTS, 0:8 * 72].rearrange("p (k c) -> p k c", k=8)
                load(b, n % RAW_SLOTS, dst[:, :, 0:ROPE], w_in_t[:, 8 * n:8 * n + 8, OFF_KPE:OFF_KPE + ROPE])
                load(b, n % RAW_SLOTS, dst[:, :, ROPE:72], w_in_t[:, 8 * n:8 * n + 8, OFF_MI:OFF_MI + 8])

            def pair(b0, n):
                for m in range(KQ // 2):
                    s = m % RAW_SLOTS
                    dst = raw[:, s, 0:768].rearrange("p (k c) -> p k c", k=2)
                    src = w_qu_t[:, 2 * m:2 * m + 2, ds(n * 384, 384)].rearrange("p k (h c) -> p k h c", h=2)
                    for q in range(2):
                        load(b0 + m, s, dst[:, q, 0:2 * NOPE].rearrange("p (h c) -> p h c", h=2),
                             src[:, q, :, 0:NOPE])
                        load(b0 + m, s, dst[:, q, 2 * NOPE:384].rearrange("p (h c) -> p h c", h=2),
                             src[:, q, :, NOPE:192])
                for m in range(KC // 2):
                    s = (KQ // 2 + m) % RAW_SLOTS
                    dst = raw[:, s, :].rearrange("p (k c) -> p k c", k=2)
                    load(b0 + KQ // 2 + m, s, dst, w_kvu_t[:, 2 * m:2 * m + 2, ds(n * 512, 512)])

            pair(U_PAIR // 2, 0)
            with sp.Fori(1, MLA_HEADS // 2) as n:
                pair(U_PAIR // 2 + n * (PAIR_UNITS // 2), n)

            def ml(b0, h):
                for n in range(KT // 2):
                    s = n % RAW_SLOTS
                    for q in range(2):
                        dst = raw[:, s, 512 * q:512 * q + 512].rearrange("p (s c) -> p s c", s=2)
                        load(b0 + n, s, dst, w_qk_t[:, 2 * n + q, :, ds(h * DQK, DQK)])
                group(b0 + KT // 2, OFF_MV + h * DV)

            with sp.Fori(0, ML_HEADS) as h:
                ml(U_ML // 2 + h * KT, h)
            for g, off in enumerate((OFF_ZA, OFF_MO, OFF_ZB)):
                with sp.Fori(0, 4) as i:
                    group(U_GATE // 2 + g * 2 * KT + i * (KT // 2), off + i * 512)
            with sp.Fori(0, 8) as i:
                group(U_OUT // 2 + i * (KT // 2), i * 512, w_out_t)

        turns = KT // (2 * RAW_SLOTS)
        PAIR_DMAS = [sum(4 if b < KQ // 2 else 1 for b in range(s, PAIR_UNITS // 2, RAW_SLOTS))
                     for s in range(RAW_SLOTS)]
        T_CQ = [0] * RAW_SLOTS
        T_CKV = [3 * turns] * RAW_SLOTS
        T_NAR = [4 * turns] * RAW_SLOTS
        T_PAIR = [4 * turns + 2] * RAW_SLOTS
        T_ML = [t + MLA_HEADS // 2 * d for t, d in zip(T_PAIR, PAIR_DMAS)]
        T_GATE = [t + ML_HEADS * 3 * turns for t in T_ML]
        T_OUT = [t + 12 * turns for t in T_GATE]

        def landed(before, local, extra=0, dmas=1):
            slot = (local // 2) % RAW_SLOTS
            return 16 * extra + 16 * (before[slot] + dmas * (local // (2 * RAW_SLOTS) + 1))

        def landed_pair(local, n):
            b = local // 2
            slot = b % RAW_SLOTS
            mine = sum(4 if x < KQ // 2 else 1 for x in range(slot, b + 1, RAW_SLOTS))
            return n * (16 * PAIR_DMAS[slot]) + 16 * (T_PAIR[slot] + mine)

        def raw_unit(local, width):
            return raw[:, (local // 2) % RAW_SLOTS, (local % 2) * width:(local % 2) * width + width]

        @block.scalar
        def _(act):
            nc.scalar.preload_act_table_set("natural_log_exp_and_others")
            act.dma_start(xt[0][0:N_META, :], meta).then_inc(xrow_in[0], 16)
            act.dma_start(xt[0][N_META:P, :], x_prompt[0, 0:P - N_META, :]).then_inc(xrow_in[0], 16)
            act.dma_start(xt[1][:, :], x_prompt[0, 112:240, :]).then_inc(xrow_in[1], 16)
            act.dma_start(xt[2][0:TAIL, :], x_prompt[0, 240:256, :]).then_inc(xrow_in[2], 16)
            act.dma_start(xt[2][TAIL:48, :], x_sample[0, :, :]).then_inc(xrow_in[2], 16)
            junk = attnT[:, :, :].rearrange("p a b -> p (a b)")

            def unit(u, local, t, width=512, first_dma=False):
                if local % 2 == 0:
                    act.wait_ge(raw_in[(local // 2) % RAW_SLOTS], t)
                if not (isinstance(u, int) and u < HL_SLOTS):
                    act.wait_ge(unit_used, u - HL_SLOTS + 2)
                nc.scalar.copy(whi[:, local % HL_SLOTS, 0:width], raw_unit(local, width)).then_inc(hi_done, 1)

            act.wait_ge(eps_set, 1)
            for t, (_, n) in enumerate(TOK):
                act.wait_ge(xrow_in[t], 16 if t == 1 else 32)
                if t:
                    act.wait_ge(xsq, t)
                nc.scalar.activation(junk[0:n, 0:D_MODEL], xt[t][0:n, :], ACT.Square,
                                     accum_out=xss[0:n, t:t + 1]).then_inc(xsq, 1)
                act.wait_ge(xsq, t + 1)
                nc.scalar.activation(xrs[0:n, t:t + 1], xss[0:n, t:t + 1], ACT.Ln, scale=1.0 / D_MODEL,
                                     bias=epsc[0:n, :]).then_inc(xln, 1)
                act.wait_ge(xln, t + 1)
                nc.scalar.activation(xrs[0:n, t:t + 1], xrs[0:n, t:t + 1], ACT.Exp, scale=-0.5).then_inc(xrstd, 1)
            act.wait_ge(free[4], use("gain", 4) + 1)
            for k in range(KT):
                b = 4 + k % 4
                act.wait_ge(full[b], use("x", b, k // 4) + 1)
                nc.scalar.activation(xhi[:, k, :], bank[b][:, 0:NT], ACT.Copy,
                                     scale=G[:, G_X + k:G_X + k + 1]).then_inc(xhi_d, 1)

            def cq_group(i):
                for k in range(KT):
                    unit(i * KT + k, k, landed(T_CQ, k, i * turns))
                for ct in (0, 2):
                    act.wait_ge(full[ct], use("cq", ct, 0, i) + 1)
                    nc.scalar.copy(cqraw[:, ds(i * 4 + ct, 1), :], bank[ct][:, 0:NQ]).then_inc(free[ct], 1)

            cq_group(0)
            with act.Fori(1, 3) as i:
                cq_group(i)

            for k in range(KT):
                unit(U_CKV + k, k, landed(T_CKV, k))
                if k == 16:
                    act.wait_ge(full[4], use("ckv", 4) + 1)
                    nc.scalar.activation(rs3[:, 0, :], bank[4][:, 0:NQ], ACT.Ln, scale=1.0 / Q_LORA,
                                         bias=epsc[:, :]).then_inc(free[4], 1)
                    act.wait_ge(free[4], use("ckv", 4) + 1)
                    nc.scalar.activation(rs3[:, 0, :], rs3[:, 0, :], ACT.Exp, scale=-0.5).then_inc(cq_rs, 1)
                if 18 <= k < 18 + KQ:
                    t = k - 18
                    act.wait_ge(cq_n, t + 1)
                    nc.scalar.copy(cqhi[:, t, :], cqraw[:, t, :]).then_inc(cq_hi, 1)
            for ct in (0, 2):
                act.wait_ge(full[ct], use("ckv", ct) + 1)
                nc.scalar.copy(ckvf[:, ct, :], bank[ct][:, 0:NT]).then_inc(free[ct], 1)
            for k in range(NAR_UNITS):
                unit(U_NAR + k, k, landed(T_NAR, k, 0, 2), 288)

            def rstd(dst, src, scale, bank_no, used, done):
                act.wait_ge(full[bank_no], used + 1)
                nc.scalar.activation(dst, src, ACT.Ln, scale=scale, bias=epsc[:, :]).then_inc(free[bank_no], 1)
                act.wait_ge(free[bank_no], used + 1)
                nc.scalar.activation(dst, dst, ACT.Exp, scale=-0.5).then_inc(done, 1)

            def q_units(n, hooks):
                for k in range(KQ):
                    unit(U_PAIR + n * PAIR_UNITS + k, k, landed_pair(k, n), 384)
                    hooks(k)

            def kv_units(n):
                for k in range(KC):
                    unit(U_PAIR + n * PAIR_UNITS + KQ + k, KQ + k, landed_pair(KQ + k, n))

            def q_rstd(phase, i, n):
                for t in range(3):
                    b = 4 + t
                    nth = (0, 0, 0)[t] if phase == "bulk0" else (2, 4, 3)[t]
                    rstd(rs3[:, t, :], bank[b][:, 0:NQ], 1.0 / (NOPE if t < 2 else ROPE), b,
                         use(phase, b, nth, i), q_rs)

            def v_evict(phase, i, n):
                for half, b in ((0, 1), (1, 2)):
                    act.wait_ge(full[b], use(phase, b, 1, i) + 1)
                    if half == 0:
                        nc.scalar.copy(vt[:, 0:2, :], bank[b][:, :].rearrange("p (a c) -> p a c", a=2))\
                          .then_inc(free[b], 1)
                    else:
                        nc.scalar.copy(vt[0:48, 2, :], bank[b][0:48, 0:256]).then_inc(v_ev, 1)
                        nc.scalar.copy(vt[:, 3, :], bank[b][:, 256:512]).then_inc(free[b], 1)

            def latent(k):
                if k == 3:
                    rstd(rs2[:, 0, 0:NT], bank[5][:, 0:NT], 1.0 / KV_LORA, 5, use("latent", 5), ck_rs)
                if k == 6:
                    for t in range(KC):
                        act.wait_ge(ck_n, t + 1)
                        nc.scalar.copy(ckhi[:, t, 0:NT], ckvf[:, t, :]).then_inc(ck_hi, 1)
                    act.wait_ge(full[4], use("latent", 4) + 1)
                    nc.scalar.copy(ckhi[:, :, NT:NKV], bank[4][:, :].rearrange("p (t n) -> p t n", t=KC))\
                      .then_inc(ck_hi, 1)
                if k == 7:
                    rstd(rs2[:, 1, 0:NT], bank[6][:, 0:NT], 1.0 / ROPE, 6, use("latent", 6, 1), kp_rs)
                if k == 10:
                    for t, b in ((0, 4), (1, 5)):
                        act.wait_ge(full[b], use("latent", b, 1) + 1)
                        nc.scalar.copy(orow[:, 512 * t:512 * t + 512], bank[b][:, :]).then_inc(free[b], 1)
                    act.wait_ge(free[4], use("latent", 4, 1) + 1)
                    act.dma_start(ckv_p[0, 0:128, :], orow[:, 0:512]).then_inc(ck_out, 16)
                    act.wait_ge(free[5], use("latent", 5, 1) + 1)
                    act.dma_start(ckv_p[0, 128:256, :], orow[:, 512:1024]).then_inc(ck_out, 16)

            q_units(0, latent)
            kv_units(0)
            q_rstd("bulk0", 0, 0)
            act.wait_ge(ck_out, 32)
            act.wait_ge(ck_tail_out, 32)
            v_evict("bulk0", 0, 0)

            def k_rstd(phase, i, j):
                for t in range(2):
                    b = 6 + t
                    if t == 0:
                        act.wait_ge(q_fin, 2 * j + 2)
                        act.wait_ge(qp_fin, j + 1)
                    rstd(rs2[:, t, :], bank[b][:, 0:NKV], 1.0 / NOPE, b, use(phase, b, 0, i), k_rs)

            def exps(phase, i, j, h):
                hh = 2 * j + h
                if not (isinstance(j, int) and j == 0 and h == 0):
                    act.wait_ge(full[7], use(phase, 7, h, i) + 1)
                for t, (a, w, rows_) in enumerate(((0, 144, P), (144, 272, P), (416, 192, DEC))):
                    act.wait_ge(mx, 3 * hh + (2, 2, 3)[t])
                    src = bank[4][:, a:a + w] if t < 2 else bank[5][0:DEC, 0:w]
                    ins = nc.scalar.activation(prob[0:rows_, a:a + w], src, ACT.Exp, bias=nmax[0:rows_, t:t + 1],
                                               accum_out=psum_[0:rows_, t:t + 1])
                    ins.then_inc(ex, 1)

            def pt_main(phase, i, j, h):
                hh = 2 * j + h
                act.wait_ge(full[6], use(phase, 6, 1 + h, i) + 1)
                nc.scalar.copy(probT[:, 0:416], bank[6][:, 0:416]).then_inc(free[6], 1)

            def attn_evict(phase, i, j, h):
                act.wait_ge(full[5], use(phase, 5, 2 + h, i) + 1)
                nc.scalar.copy(attnT[:, ds(2 * j + h, 1), :], bank[5][:, 0:NQ]).then_inc(free[5], 1)

            def attention(phase, i, j):
                def hooks(k):
                    if k == 1:
                        k_rstd(phase, i, j)
                    if k == 5:
                        exps(phase, i, j, 0)
                    if k == 7:
                        pt_main(phase, i, j, 0)
                    if k == 8:
                        exps(phase, i, j, 1)
                    if k == 9:
                        attn_evict(phase, i, j, 0)
                    if k == 10:
                        pt_main(phase, i, j, 1)
                return hooks

            with act.Fori(0, 7) as j:
                q_units(j + 1, attention("step", j, j))
                attn_evict("step", j, j, 1)
                kv_units(j + 1)
                q_rstd("step", j, j + 1)
                v_evict("step", j, j + 1)

            def big(u, before, extra=0, hooks=lambda k: None, dmas=1):
                for k in range(KT):
                    unit(u + k, k, landed(before, k, extra, dmas))
                    hooks(k)

            last = attention("ml0qk", 0, 7)

            def first_head(k):
                last(k)
                if k == 12:
                    attn_evict("ml0qk", 0, 7, 1)
            big(U_ML, T_ML, 0, first_head, 2)

            def qk_evict(phase, i, h):
                for ct in (0, 2):
                    act.wait_ge(full[ct], use(phase, ct, 0, i) + 1)
                    if ct == 0:
                        nc.scalar.copy(mqT[:, 0, :], bank[0][:, 0:NT]).then_inc(free[0], 1)
                    else:
                        nc.scalar.mul(mkT[:, 0, :], bank[2][:, 0:NT], DQK ** -0.5).then_inc(free[2], 1)

            def mv_evict(phase, nth, i, h):
                for ct in (0, 2):
                    act.wait_ge(full[ct], use(phase, ct, nth, i) + 1)
                    nc.scalar.copy(mvT[:, ct, :], bank[ct][:, 0:NT]).then_inc(free[ct], 1)

            qk_evict("ml0qk", 0, 0)

            def row_hooks(k):
                if k == 4:
                    act.wait_ge(free[5], use("rows", 5) + 1)
                    R = rows
                    nc.scalar.activation(R["mrow"][:, 0:NT], R["xf"][:, 0:NT], ACT.Abs).then_inc(r_abs, 1)
                    act.wait_ge(r_abs, 1)
                    nc.scalar.activation(R["mrow"][:, 0:NT], R["mrow"][:, 0:NT], ACT.Exp, scale=-1.0).then_inc(r_e, 1)
                    act.wait_ge(r_e, 1)
                    nc.scalar.activation(R["mrow"][:, 0:NT], R["mrow"][:, 0:NT], ACT.Ln, bias=1.0).then_inc(r_l, 1)
                if k == 12:
                    act.wait_ge(r_v, 11)
                    act.wait_ge(full[7], use("rows", 7) + 1)
                    for t, (_, n) in enumerate(MQT):
                        nc.scalar.activation(emcol[0:n, t, :], bank[7][0:n, 4 * t:4 * t + 4], ACT.Exp,
                                             scale=-1.0).then_inc(free[7] if t == 2 else r_em, 1)
            big(U_ML + KT, T_ML, 2 * turns, row_hooks)
            mv_evict("ml0v", 0, 0, 0)

            def mlstm(phase, i, h):
                def hooks(k):
                    if k == 3:
                        act.wait_ge(full[4], use(phase, 4, 0, i) + 1)
                        nc.scalar.copy(Mb[:, :], bank[4][:, 0:NT + 1]).then_inc(free[4], 1)
                        act.wait_ge(free[4], use(phase, 4, 0, i) + 1)
                        act.wait_ge(nml_d, h + 1)
                        nc.scalar.activation(wi[:, :], Mb[:, C_SAMPLE:NT], ACT.Exp, scale=-1.0,
                                             bias=Mb[:, NT:NT + 1]).then_inc(wi_d, 1)
                        nc.scalar.activation(decay[:, :], Mb[:, NT:NT + 1], ACT.Exp,
                                             bias=nML[:, 1:2]).then_inc(dec_d, 1)
                        act.wait_ge(wt_d, h + 1)
                        nc.scalar.activation(wtmp[:, :], wtmp[:, :], ACT.Exp).then_inc(wt_x, 1)
                    if k == 5:
                        act.wait_ge(e_d, 3 * h + 3)
                        nc.scalar.activation(E[:, 0:464], E[:, 0:464], ACT.Exp, scale=-1.0).then_inc(e_x, 1)
                        nc.scalar.activation(E[0:48, 464:512], E[0:48, 464:512], ACT.Exp, scale=-1.0).then_inc(e_x, 1)
                    if k == 8:
                        act.wait_ge(full[6], use(phase, 6, 1, i) + 1)
                        nc.scalar.copy(vtok[:, 0, :], bank[6][:, :]).then_inc(free[6], 1)
                        act.wait_ge(full[7], use(phase, 7, 1, i) + 1)
                        nc.scalar.copy(vtok[:, 1, :], bank[7][:, :]).then_inc(free[7], 1)
                    if k == 16:
                        act.wait_ge(din_d, h + 1)
                        for t, (_, n) in enumerate(MQT):
                            b = 5 + t
                            act.wait_ge(full[b], use(phase, b, (1, 2, 2)[t], i) + 1)
                            if t:
                                act.wait_ge(hsq_d, 3 * h + t)
                            nc.scalar.activation(E[0:n, :], bank[b][0:n, :], ACT.Square, scale=dinv[0:n, t:t + 1],
                                                 accum_out=hss[0:n, t:t + 1]).then_inc(hsq_d, 1)
                        act.wait_ge(hsq_d, 3 * h + 3)
                        nc.scalar.activation(hss[:, :], hss[:, :], ACT.Ln, scale=1.0 / DV, bias=epsc[:, :])\
                          .then_inc(hln_d, 1)
                        act.wait_ge(hln_d, h + 1)
                        nc.scalar.activation(hss[:, :], hss[:, :], ACT.Exp, scale=-0.5).then_inc(hrs_d, 1)
                    if k == 26:
                        for d in range(2):
                            b = 5 + d
                            act.wait_ge(full[b], use(phase, b, 3 + d, i) + 1)
                            nc.scalar.copy(Cout[:, d, :], bank[b][:, :]).then_inc(free[b], 1)
                            act.wait_ge(free[b], use(phase, b, 3 + d, i) + 1)
                        act.dma_start(C_p[0, ds(h, 1), :, :].rearrange("a (d p) e -> p (a d) e", p=P),
                                      Cout[:, 0:2, :]).then_inc(Cp_out, 16)
                return hooks

            with act.Fori(0, 3) as h:
                big(U_ML + 2 * KT + h * (2 * KT), T_ML, (h + 1) * (3 * turns), mlstm("ml", h, h), 2)
                qk_evict("ml", h, h + 1)
                big(U_ML + 3 * KT + h * (2 * KT), T_ML, (h + 1) * (3 * turns) + 2 * turns)
                mv_evict("ml", 1, h, h + 1)
                act.wait_ge(Cp_out, 16 * h + 16)

            def gate(phase, i, g, silu):
                for ct in range(4):
                    act.wait_ge(full[ct], use(phase, ct, 0, i) + 1)
                    if not (isinstance(g, int) and g == 0):
                        act.wait_ge(gm_d, 4 * g - 3 + ct)
                    ins = nc.scalar.activation(sg[:, ct, :], bank[ct][:, 0:NQ], ACT.Sigmoid)
                    ins.then_inc(sg_d, 1)

            big(U_GATE, T_GATE, 0, mlstm("gate0", 0, 3))
            gate("gate0", 0, 0, True)
            with act.Fori(0, 11) as g:
                big(U_GATE + KT + g * KT, T_GATE, (g + 1) * turns)
                gate("gate", g, g + 1, True)

            for k in range(AHEAD):
                unit(U_OUT + k, k, landed(T_OUT, k))
            for t in range(KT):
                if t == 0:
                    act.wait_ge(full[3], use("out0", 3))
                act.wait_ge(gm_d, 4 * 12)
                src = attnT[:, t, :] if t < 16 else hT[:, t - 16, :]
                nc.scalar.copy(mhi[:, t, :], src).then_inc(mix_hi, 1)
                if t + AHEAD < KT:
                    unit(U_OUT + AHEAD + t, AHEAD + t, landed(T_OUT, AHEAD + t))

            def y_evict(phase, i, g):
                for ct in (0, 2):
                    act.wait_ge(full[ct], use(phase, ct, 0, i) + 1)
                    if not (isinstance(g, int) and g == 0):
                        act.wait_ge(full[6], use("out", 6, 0, i) + 1)
                    nc.scalar.copy(yT[:, ct, :], bank[ct][:, 0:NQ]).then_inc(free[ct], 1)

            y_evict("out0", 0, 0)
            with act.Fori(0, 7) as g:
                big(U_OUT + KT + g * KT, T_OUT, (g + 1) * turns)
                y_evict("out", g, g + 1)

        @block.vector
        def _(dve):
            tt, ts_, stt = nc.vector.tensor_tensor, nc.vector.tensor_scalar, nc.vector.scalar_tensor_tensor
            nc.vector.memset(epsc[:, :], EPS).then_inc(eps_set, 1)

            def unit(u, local, width=512):
                dve.wait_ge(hi_done, u + 1)
                tt(wlo[:, local % HL_SLOTS, 0:width], raw_unit(local, width),
                   whi[:, local % HL_SLOTS, 0:width].bitcast(f32), ALU.subtract).then_inc(lo_done, 1)

            dve.wait_ge(full[4], use("gain", 4) + 1)
            nc.vector.tensor_copy(G[:, :], bank[4][:, 0:G_ROWS]).then_inc(free[4], 1)
            for t, (_, n) in enumerate(TOK):
                dve.wait_ge(xrstd, t + 1)
                ts_(xt[t][0:n, :], xt[t][0:n, :], xrs[0:n, t:t + 1], None, ALU.mult).then_inc(xscaled, 1)
            for k in range(KT):
                b = 4 + k % 4
                dve.wait_ge(xhi_d, k + 1)
                stt(xlo[:, k, :], bank[b][:, 0:NT], G[:, G_X + k:G_X + k + 1], xhi[:, k, :].bitcast(f32),
                    ALU.mult, ALU.subtract).then_inc(free[b], 1)

            with dve.Fori(0, 3) as i:
                for k in range(KT):
                    unit(i * KT + k, k)
                for ct in (1, 3):
                    dve.wait_ge(full[ct], use("cq", ct, 0, i) + 1)
                    nc.vector.tensor_copy(cqraw[:, ds(i * 4 + ct, 1), :], bank[ct][:, 0:NQ]).then_inc(free[ct], 1)

            ts_(gsc[:, 0:1], G[:, G_QN:G_QN + 1], ATTN_SCALE, None, ALU.mult).then_inc(gsc_d, 1)
            ts_(gsc[:, 1:2], G[:, G_QR:G_QR + 1], ATTN_SCALE, None, ALU.mult).then_inc(gsc_d, 1)
            dve.wait_ge(gsc_d, 2)
            ts_(rotq[:, :], rot, gsc[:, 1:2], None, ALU.mult).then_inc(gsc_d, 1)
            nc.vector.memset(kpe2[0][64:P, :], 0.0).then_inc(kp_zero, 1)
            nc.vector.memset(kpe2[1][0:64, :], 0.0).then_inc(kp_zero, 1)
            ts_(rope1[:, 0:P], rot, G[:, G_KR:G_KR + 1], None, ALU.mult).then_inc(gsc_d, 1)

            for k in range(KT):
                unit(U_CKV + k, k)
                if 17 <= k < 17 + KQ + 1:
                    t = k - 17
                    if t == 0:
                        dve.wait_ge(cq_rs, 1)
                    if t < KQ:
                        stt(cqraw[:, t, :], cqraw[:, t, :], G[:, G_QA + t:G_QA + t + 1], rs3[:, 0, :],
                            ALU.mult, ALU.mult).then_inc(cq_n, 1)
                    if t > 0:
                        dve.wait_ge(cq_hi, t)
                        tt(cqlo[:, t - 1, :], cqraw[:, t - 1, :], cqhi[:, t - 1, :].bitcast(f32),
                           ALU.subtract).then_inc(cq_lo, 1)
            for ct in (1, 3):
                dve.wait_ge(full[ct], use("ckv", ct) + 1)
                nc.vector.tensor_copy(ckvf[:, ct, :], bank[ct][:, 0:NT]).then_inc(free[ct], 1)
            for k in range(NAR_UNITS):
                unit(U_NAR + k, k, 288)
            dve.wait_ge(full[0], use("narrow", 0) + 1)
            nc.vector.tensor_copy(nraw[:, :], bank[0][0:72, 0:NT]).then_inc(free[0], 1)

            def q_units(n, hooks):
                for k in range(KQ):
                    unit(U_PAIR + n * PAIR_UNITS + k, k, 384)
                    hooks(k)

            def kv_units(n, hooks=lambda k: None):
                for k in range(KC):
                    unit(U_PAIR + n * PAIR_UNITS + KQ + k, KQ + k)
                    hooks(k)

            def latent(k):
                if k == 2:
                    dve.wait_ge(full[6], use("latent", 6) + 1)
                    nc.vector.tensor_copy(kpr, bank[6][:, 0:NT]).then_inc(free[6], 1)
                if k == 4:
                    dve.wait_ge(ck_rs, 1)
                    for t in range(KC):
                        stt(ckvf[:, t, :], ckvf[:, t, :], G[:, G_KVA + t:G_KVA + t + 1], rs2[:, 0, 0:NT],
                            ALU.mult, ALU.mult).then_inc(ck_n, 1)
                if k == 6:
                    for t in range(KC):
                        dve.wait_ge(ck_hi, t + 1)
                        tt(cklo[:, t, 0:NT], ckvf[:, t, :], ckhi[:, t, 0:NT].bitcast(f32),
                           ALU.subtract).then_inc(ck_lo, 1)
                    dve.wait_ge(ck_hi, KC + 1)
                    tt(cklo[:, :, NT:NKV], bank[4][:, :].rearrange("p (t n) -> p t n", t=KC),
                       ckhi[:, :, NT:NKV].bitcast(f32), ALU.subtract).then_inc(free[4], 1)
                if k == 7:
                    dve.wait_ge(full[7], use("latent", 7, 1) + 1)
                    tt(rope2[:, :], bank[7][:, 0:NT], sinT, ALU.mult).then_inc(free[7], 1)
                    stt(rope1[:, :], kpr, G[:, G_KR:G_KR + 1], cosT, ALU.mult, ALU.mult).then_inc(kp_c, 1)
                if k == 9:
                    dve.wait_ge(kp_n, 1)
                    dve.wait_ge(kp_zero, 2)
                    nc.vector.tensor_copy(kpe2[0][0:64, 0:NT], kpe_n[0:64, :]).then_inc(kp_st, 1)
                    nc.vector.tensor_copy(kpe2[1][64:P, 0:NT], kpe_n[64:P, :]).then_inc(kp_st, 1)
                if k == 11:
                    dve.wait_ge(full[7], use("latent", 7, 2) + 1)
                    nc.vector.tensor_copy(kout[:, 0:128], bank[7][:, 0:128]).then_inc(kp_rows, 1)
                    nc.vector.tensor_copy(kout[0:48, 128:192], bank[7][0:48, 128:192]).then_inc(free[7], 1)

            def q_evict(phase, i, n):
                if phase == "bulk0":
                    dve.wait_ge(kp_out, 64)
                for t in range(3):
                    dve.wait_ge(full[t], use(phase, t, 0, i) + 1)
                    dst = qn[:, t, :] if t < 2 else qp[:, :]
                    nc.vector.tensor_copy(dst, bank[t][:, 0:NQ]).then_inc(free[t], 1)

            def q_norm(phase, i, n):
                nth = 0 if phase == "bulk0" else 3
                dve.wait_ge(full[7], use(phase, 7, nth, i) + 1)
                tt(rope2[:, 0:NQ], bank[7][:, 0:NQ], sinT[:, N_META:NT], ALU.mult).then_inc(free[7], 1)
                stt(rope1[:, 0:NQ], qp[:, :], gsc[:, 1:2], cosT[:, N_META:NT], ALU.mult, ALU.mult).then_inc(qp_c, 1)
                for t in range(2):
                    dve.wait_ge(q_rs, 3 * n + t + 1)
                    stt(qn[:, t, :], qn[:, t, :], gsc[:, 0:1], rs3[:, t, :], ALU.mult, ALU.mult).then_inc(q_fin, 1)

            def k_evict(phase, i, n, t):
                b = (3, 0)[t]
                dve.wait_ge(full[b], use(phase, b, (0, 1)[t], i) + 1)
                nc.vector.tensor_copy(kn[:, t, :], bank[b][:, 0:NKV]).then_inc(free[b], 1)

            def latent_cache(k):
                latent(k)
                if k == 5:
                    dve.wait_ge(full[7], use("latent", 7) + 1)
                    nc.vector.tensor_copy(kpe2[0][0:64, NT:NKV], bank[7][0:64, 0:PAST]).then_inc(kp_st, 1)
                    nc.vector.tensor_copy(kpe2[1][64:P, NT:NKV], bank[7][64:P, 0:PAST]).then_inc(free[7], 1)
            q_units(0, latent_cache)
            dve.wait_ge(full[6], use("latent", 6, 2) + 1)
            dve.wait_ge(ck_out, 32)
            nc.vector.tensor_copy(orow[0:48, 0:512], bank[6][0:48, :]).then_inc(free[6], 1)
            q_evict("bulk0", 0, 0)
            kv_units(0)
            for t in range(2):
                k_evict("bulk0", 0, 0, t)
            q_norm("bulk0", 0, 0)

            def k_norm(j, t):
                dve.wait_ge(k_rs, 2 * j + t + 1)
                stt(kn[:, t, :], kn[:, t, :], G[:, G_KN:G_KN + 1], rs2[:, t, :], ALU.mult, ALU.mult)\
                    .then_inc(k_fin, 1)

            def maxima(phase, i, j, h):
                dve.wait_ge(full[4], use(phase, 4, h, i) + 1)
                nc.vector.tensor_reduce(nmax[:, 0:1], bank[4][:, 0:144], AX.X, ALU.max, negate=True).then_inc(mx, 1)
                nc.vector.tensor_reduce(nmax[:, 1:2], bank[4][:, 144:416], AX.X, ALU.max, negate=True).then_inc(mx, 1)
                dve.wait_ge(full[5], use(phase, 5, h, i) + 1)
                nc.vector.tensor_reduce(nmax[0:DEC, 2:3], bank[5][0:DEC, 0:192], AX.X, ALU.max, negate=True)\
                    .then_inc(mx, 1)

            def inverse(phase, i, j, h):
                dve.wait_ge(ex, 6 * j + 3 * h + 3)
                nc.vector.reciprocal(pinv[:, 0:2], psum_[:, 0:2]).then_inc(free[4], 1)
                nc.vector.reciprocal(pinv[0:DEC, 2:3], psum_[0:DEC, 2:3]).then_inc(free[5], 1)

            def pt_minor(phase, i, j, h):
                dve.wait_ge(full[7], use(phase, 7, 1 + h, i) + 1)
                nc.vector.tensor_copy(probT[0:TAIL, 416:704], bank[7][0:TAIL, 0:288]).then_inc(pt_d, 1)
                nc.vector.tensor_copy(probT[0:48, 704:736], bank[7][0:48, 288:320]).then_inc(free[7], 1)

            def attention(phase, i, j):
                def hooks(k):
                    if k in (2, 3):
                        k_norm(j, k - 2)
                    if k == 5:
                        maxima(phase, i, j, 0)
                    if k == 6:
                        inverse(phase, i, j, 0)
                    if k == 7:
                        pt_minor(phase, i, j, 0)
                    if k == 8:
                        maxima(phase, i, j, 1)
                    if k == 9:
                        inverse(phase, i, j, 1)
                    if k == 10:
                        pt_minor(phase, i, j, 1)
                return hooks

            with dve.Fori(0, 7) as j:
                q_units(j + 1, attention("step", j, j))
                q_evict("step", j, j + 1)
                kv_units(j + 1)
                for t in range(2):
                    k_evict("step", j, j + 1, t)
                q_norm("step", j, j + 1)

            def big(u, hooks=lambda k: None):
                for k in range(KT):
                    unit(u + k, k)
                    hooks(k)

            big(U_ML, attention("ml0qk", 0, 7))

            def qk_evict(phase, i, h):
                for ct in (1, 3):
                    dve.wait_ge(full[ct], use(phase, ct, 0, i) + 1)
                    if ct == 1:
                        nc.vector.tensor_copy(mqT[:, 1, :], bank[1][:, 0:NT]).then_inc(free[1], 1)
                    else:
                        ts_(mkT[:, 1, :], bank[3][:, 0:NT], DQK ** -0.5, None, ALU.mult).then_inc(free[3], 1)

            def mv_evict(phase, nth, i, h):
                for ct in (1, 3):
                    dve.wait_ge(full[ct], use(phase, ct, nth, i) + 1)
                    nc.vector.tensor_copy(mvT[:, ct, :], bank[ct][:, 0:NT]).then_inc(free[ct], 1)

            qk_evict("ml0qk", 0, 0)
            R = rows

            def scan(dst, data, a, b, init, op, other):
                return nc.vector.tensor_tensor_scan(dst[:, a:b], data[:, a:b], other[:, a:b], init, op[0], op[1])

            def row_hooks(k):
                if k == 3:
                    dve.wait_ge(gb_in, 48)
                    dve.wait_ge(full[4], use("rows", 4) + 1)
                    ts_(R["ig"][:, 0:NT], bank[4][0:ML_HEADS, 0:NT], gate_b[:, 0:1], None, ALU.add).then_inc(free[4], 1)
                    dve.wait_ge(full[5], use("rows", 5) + 1)
                    ts_(R["xf"][:, 0:NT], bank[5][0:ML_HEADS, 0:NT], gate_b[:, 1:2], None, ALU.add).then_inc(free[5], 1)
                    nc.vector.memset(R["crow"][:, :], 0.0).then_inc(r_v, 1)
                if k == 5:
                    dve.wait_ge(free[5], use("rows", 5) + 1)
                    dve.wait_ge(r_l, 1)
                    stt(R["lf"][:, 0:NT], R["xf"][:, 0:NT], 0.0, R["mrow"][:, 0:NT], ALU.min, ALU.subtract)\
                        .then_inc(r_v, 1)
                    dve.wait_ge(r_v, 2)
                    scan(R["bsum"], R["lf"], 0, C_SAMPLE, 0.0, (ALU.add, ALU.add), R["crow"]).then_inc(r_v, 1)
                    scan(R["bsum"], R["lf"], C_SAMPLE, NT, 0.0, (ALU.add, ALU.add), R["crow"]).then_inc(r_v, 1)
                if k == 6:
                    dve.wait_ge(r_v, 4)
                    tt(R["crow"][:, 0:NT], R["ig"][:, 0:NT], R["bsum"][:, 0:NT], ALU.subtract).then_inc(r_v, 1)
                    dve.wait_ge(r_v, 5)
                    scan(R["Mrow"], R["crow"], 0, C_SAMPLE, 0.0, (ALU.max, ALU.max), R["crow"]).then_inc(r_v, 1)
                    scan(R["Mrow"], R["crow"], C_SAMPLE, NT, gate_b[:, 2:3], (ALU.max, ALU.max), R["crow"])\
                        .then_inc(r_v, 1)
                    nc.vector.tensor_copy(R["Mrow"][:, NT:NT + 1], gate_b[:, 2:3]).then_inc(r_v, 1)
                if k == 7:
                    dve.wait_ge(r_v, 8)
                    tt(R["mrow"][:, 0:NT], R["bsum"][:, 0:NT], R["Mrow"][:, 0:NT], ALU.add).then_inc(r_v, 1)
                    nc.vector.memset(ccol[:, :, :], 0.0).then_inc(r_v, 1)
                    nc.vector.memset(emcol[:, :, :], 1.0).then_inc(r_v, 1)
                    nc.vector.memset(dsb[:, :], 1.0).then_inc(r_v, 1)
                    nc.vector.memset(hss[:, :], 1.0).then_inc(r_v, 1)
                    nc.vector.memset(qw[:, :, :], 0.0).then_inc(qw_z, 1)
                if k == 13:
                    dve.wait_ge(r_v, 13)
                    dve.wait_ge(full[6], use("rows", 6) + 1)
                    for t, (_, n) in enumerate(TOK):
                        nc.vector.tensor_copy(ccol[0:n, t, :], bank[6][0:n, 4 * t:4 * t + 4])\
                            .then_inc(free[6] if t == 2 else r_c, 1)
            big(U_ML + KT, row_hooks)
            mv_evict("ml0v", 0, 0, 0)

            def mlstm(phase, i, h):
                first = isinstance(h, int) and h == 0

                def hooks(k):
                    if k == 0:
                        dve.wait_ge(free[6], use("rows", 6) + 1)
                        ts_(Mh[:, :], R["Mrow"][:, :], ident[0:ML_HEADS, ds(h, 1)], None, ALU.mult).then_inc(mh_d, 1)
                    if k == 3:
                        dve.wait_ge(free[4], use(phase, 4, 0, i) + 1)
                        ts_(nML[:, 0:1], Mb[:, C_SAMPLE - 1:C_SAMPLE], -1.0, None, ALU.mult).then_inc(nml_s, 1)
                        ts_(nML[:, 1:2], Mb[:, NT - 1:NT], -1.0, None, ALU.mult).then_inc(nml_d, 1)
                        dve.wait_ge(nml_s, h + 1)
                        dve.wait_ge(nml_d, h + 1)
                        ts_(wtmp[:, 0:3], ccol[:, :, ds(h, 1)].rearrange("p t a -> p (t a)"), nML[:, 0:1], 0.0,
                            ALU.add, ALU.min).then_inc(wt_p, 1)
                        ts_(wtmp[:, 3:4], ccol[:, 2, ds(h, 1)], nML[:, 1:2], 0.0, ALU.add, ALU.min).then_inc(wt_d, 1)
                        for t, (at, w) in enumerate(MLW):
                            n = TOK[t][1]
                            ts_(E[0:n, at:at + w], Mb[0:n, NT - w:NT], ccol[0:n, t, ds(h, 1)], 0.0,
                                ALU.subtract, ALU.max).then_inc(e_d, 1)
                    if k == 5:
                        dve.wait_ge(wt_x, h + 1)
                        tt(wtmp[:, :], wtmp[:, :], c("rowmask"), ALU.mult).then_inc(wt_m, 1)
                        dve.wait_ge(wt_m, h + 1)
                        dve.wait_ge(full[6], use(phase, 6, 0, i) + 1)
                        ts_(kws[:, 0, :], bank[6][:, 0:256], wtmp[:, 0:1], None, ALU.mult).then_inc(kws_d, 1)
                        ts_(kws[:, 1, :], bank[6][:, 256:512], wtmp[:, 1:2], None, ALU.mult).then_inc(free[6], 1)
                        dve.wait_ge(full[7], use(phase, 7, 0, i) + 1)
                        ts_(kws[0:48, 2, :], bank[7][0:48, 0:256], wtmp[0:48, 2:3], None, ALU.mult).then_inc(kws_d, 1)
                        ts_(kws[0:48, 3, :], bank[7][0:48, 0:256], wtmp[0:48, 3:4], None, ALU.mult).then_inc(free[7], 1)
                        dve.wait_ge(wi_d, h + 1)
                        dve.wait_ge(qw_z, 1)
                        for d in range(2):
                            tt(qw[:, d, TAIL:48], mqT[:, d, C_SAMPLE:NT], wi[:, :], ALU.mult).then_inc(qw_d, 1)
                    if k == 7:
                        dve.wait_ge(full[5], use(phase, 5, 0, i) + 1)
                        dve.wait_ge(e_m, 2 * h + 2)
                        tt(Pt[:, 0:464], bank[5][:, 0:464], E[:, 0:464], ALU.mult).then_inc(p_d, 1)
                        tt(Pt[0:48, 464:512], bank[5][0:48, 464:512], E[0:48, 464:512], ALU.mult).then_inc(free[5], 1)
                        dve.wait_ge(full[4], use(phase, 4, 1, i) + 1)
                        nc.vector.tensor_copy(vtok[0:48, 2, :], bank[4][0:48, :]).then_inc(free[4], 1)
                    if k == 14:
                        dve.wait_ge(full[4], use(phase, 4, 2, i) + 1)
                        nc.vector.tensor_copy(dsb[:, 0:2], bank[4][:, 0:2]).then_inc(den_d, 1)
                        nc.vector.tensor_copy(dsb[0:48, 2:3], bank[4][0:48, 2:3]).then_inc(free[4], 1)
                        dve.wait_ge(den_d, h + 1)
                        dve.wait_ge(free[4], use(phase, 4, 2, i) + 1)
                        stt(dinv[:, :], dsb[:, :], -1.0, dsb[:, :], ALU.mult, ALU.max).then_inc(dab_d, 1)
                        dve.wait_ge(dab_d, h + 1)
                        tt(dinv[:, :], dinv[:, :], emcol[:, :, ds(h, 1)].rearrange("p t a -> p (t a)"),
                           ALU.max).then_inc(dmx_d, 1)
                        dve.wait_ge(dmx_d, h + 1)
                        nc.vector.reciprocal(dinv[:, :], dinv[:, :]).then_inc(din_d, 1)
                    if k == 19:
                        dve.wait_ge(hrs_d, h + 1)
                        tt(hfac[:, :], dinv[:, :], hss[:, :], ALU.mult).then_inc(hf_d, 1)
                        dve.wait_ge(hf_d, h + 1)
                        for t, (_, n) in enumerate(MQT):
                            b = 5 + t
                            ts_(hn[0:n, t, :], bank[b][0:n, :], hfac[0:n, t:t + 1], None, ALU.mult)\
                                .then_inc(free[b], 1)
                    if k == 24:
                        for e in range(4):
                            b = 4 + e
                            dve.wait_ge(full[b], use(phase, b, (3, 2, 3, 3)[e], i) + 1)
                            ts_(hT[:, ds(4 * h + e, 1), :], bank[b][:, 0:NQ], G[:, ds(G_MLO + 4 * h + e, 1)], None,
                                ALU.mult).then_inc(free[b], 1)
                    if k == 30:
                        dve.wait_ge(C0_in, 16 * (h + 1))
                        dve.wait_ge(dec_d, h + 1)
                        for d in range(2):
                            b = 5 + d
                            dve.wait_ge(full[b], use(phase, b, 4 + d, i) + 1)
                            stt(Cout[:, 2 + d, :], C0[:, d, :], decay[:, :], bank[b][:, :], ALU.mult, ALU.add)\
                                .then_inc(free[b], 1)
                        dve.wait_ge(full[7], use(phase, 7, 4, i) + 1)
                        nc.vector.tensor_copy(ncol[:, ds(2 * h, 2)], bank[7][:, 0:2]).then_inc(n_d, 1)
                        stt(ncol[:, ds(8 + 2 * h, 2)], G[:, ds(G_N0 + 2 * h, 2)], decay[:, :], bank[7][:, 2:4],
                            ALU.mult, ALU.add).then_inc(free[7], 1)
                return hooks

            with dve.Fori(0, 3) as h:
                big(U_ML + 2 * KT + h * (2 * KT), mlstm("ml", h, h))
                qk_evict("ml", h, h + 1)
                big(U_ML + 3 * KT + h * (2 * KT))
                mv_evict("ml", 1, h, h + 1)
                dve.wait_ge(Cs_out, 16 * h + 16)

            def silu(phase, i, g):
                for ct in range(4):
                    dve.wait_ge(sg_d, 4 * g + ct + 1)
                    tt(gt[:, ct, :], bank[ct][:, 0:NQ], sg[:, ct, :], ALU.mult).then_inc(free[ct], 1)

            big(U_GATE, mlstm("gate0", 0, 3))
            silu("gate0", 0, 0)
            with dve.Fori(0, 11) as g:
                big(U_GATE + KT + g * KT)
                silu("gate", g, g + 1)
            dve.wait_ge(full[4], use("nout", 4) + 1)
            nc.vector.tensor_copy(nrow[:, :], bank[4][0:16, 0:P]).then_inc(free[4], 1)

            for k in range(AHEAD):
                unit(U_OUT + k, k)
            for t in range(KT):
                dve.wait_ge(mix_hi, t + 1)
                src = attnT[:, t, :] if t < 16 else hT[:, t - 16, :]
                tt(mlo[:, t, :], src, mhi[:, t, :].bitcast(f32), ALU.subtract).then_inc(mix_lo, 1)
                if t + AHEAD < KT:
                    unit(U_OUT + AHEAD + t, AHEAD + t)

            def y_evict(phase, i, g):
                for ct in (1, 3):
                    dve.wait_ge(full[ct], use(phase, ct, 0, i) + 1)
                    if not (isinstance(g, int) and g == 0):
                        dve.wait_ge(full[6], use("out", 6, 0, i) + 1)
                    nc.vector.tensor_copy(yT[:, ct, :], bank[ct][:, 0:NQ]).then_inc(free[ct], 1)

            def add_rows(phase, i, g):
                for t, (_, n) in enumerate(QT):
                    b = 4 + t
                    dve.wait_ge(full[b], use(phase, b, 0, i) + 1)
                    tt(ytok[0:n, t, :], bank[b][0:n, :], xres[0:n, t, :], ALU.add).then_inc(free[b], 1)

            y_evict("out0", 0, 0)
            with dve.Fori(0, 7) as g:
                def hooks(k):
                    if k == 4:
                        dve.wait_ge(xres_in, g * 48 + 48)
                        add_rows("out", g, g)
                big(U_OUT + KT + g * KT, hooks)
                y_evict("out", g, g + 1)
                dve.wait_ge(y_out, g * 48 + 48)
            dve.wait_ge(xres_in, 8 * 48)
            add_rows("outlast", 0, 7)

        @block.tensor
        def _(pe):
            mm, tr = nc.tensor.matmul, nc.tensor.transpose

            def mm3(out, w_hi, w_lo, m_hi, m_lo, start, stop, opens=False, **kw):
                ins = mm(out, w_hi, m_hi, start=start, stop=False, **kw)
                if opens:
                    ins.then_inc(unit_used, 1)
                mm(out, w_hi, m_lo, start=False, stop=False, **kw)
                return mm(out, w_lo, m_hi, start=False, stop=stop, **kw)

            def apart():
                pe.sem_inc(passed_pe, 1)

            def fill(phase, b, nth=0, i=0):
                before = use(phase, b, nth, i)
                if not (isinstance(before, int) and before == 0):
                    pe.wait_ge(free[b], before)

            pe.wait_ge(const_in, 16)
            pe.wait_ge(grows_in, 16 * 11)
            tr(bank[4][:, 0:G_ROWS], Grows[:, :], ident[0:G_ROWS, 0:G_ROWS]).then_inc(full[4], 1)
            for k in range(KT):
                b = 4 + k % 4
                fill("x", b, k // 4)
                for t, (c0, n) in enumerate(TOK):
                    if k == 0:
                        pe.wait_ge(xscaled, t + 1)
                    ins = tr(bank[b][:, c0:c0 + n], xt[t][0:n, k * P:(k + 1) * P], ident[0:n, 0:n])
                ins.then_inc(full[b], 1)

            def group(u, phase, nth, i, c0, hooks=lambda k: None, a_hi=xhi, a_lo=xlo, ready=None):
                n = NT - c0
                for k in range(KT):
                    pe.wait_ge(lo_done, u + k + 1)
                    if ready is not None:
                        pe.wait_ge(ready, k + 1)
                    for ct in range(4):
                        if k == 0:
                            fill(phase, ct, nth, i)
                        s = slice(ct * P, ct * P + P)
                        mc = slice(0, NQ) if a_hi is mhi else slice(c0, NT)
                        ins = mm3(bank[ct][:, 0:n], whi[:, k % HL_SLOTS, s], wlo[:, k % HL_SLOTS, s],
                                  a_hi[:, k, mc], a_lo[:, k, mc], k == 0, k == KT - 1, k == 0 and ct == 0)
                        if k == KT - 1:
                            ins.then_inc(full[ct], 1)
                    if k < KT - 1:
                        ins.then_inc(unit_used, 1)
                    hooks(k)

            pe.wait_ge(free[7], use("cq", 7))
            pe.wait_ge(free[4], use("cq", 4))
            pe.wait_ge(free[5], use("cq", 5))
            pe.wait_ge(free[6], use("cq", 6))
            with pe.Fori(0, 3) as i:
                group(i * KT, "cq", 0, i, N_META)

            def cq_squares(k):
                if 2 <= k < 2 + KQ:
                    t = k - 2
                    if t == 0:
                        fill("ckv", 4)
                    pe.wait_ge(cq_sq, t + 1)
                    ins = mm(bank[4][:, 0:NQ], ones, sq3[:, t % 3, :], start=t == 0, stop=t == KQ - 1)
                    ins.then_inc(full[4] if t == KQ - 1 else cq_ssm, 1)
            group(U_CKV, "ckv", 0, 0, 0, cq_squares)

            for k in range(NAR_UNITS):
                pe.wait_ge(lo_done, U_NAR + k + 1)
                if k == 0:
                    fill("narrow", 0)
                for q in range(4):
                    s = slice(72 * q, 72 * q + 72)
                    kk = 4 * k + q
                    ins = mm3(bank[0][0:72, 0:NT], whi[:, k % HL_SLOTS, s], wlo[:, k % HL_SLOTS, s],
                              xhi[:, kk, :], xlo[:, kk, :], kk == 0, kk == KT - 1, kk == 0)
                ins.then_inc(full[0] if k == NAR_UNITS - 1 else unit_used, 1)

            def q_units(n, phase, i, hooks):
                for k in range(KQ):
                    pe.wait_ge(lo_done, U_PAIR + n * PAIR_UNITS + k + 1)
                    if isinstance(n, int):
                        pe.wait_ge(cq_lo, k + 1)
                    for t in range(3):
                        if k == 0:
                            fill(phase, t, 0, i)

                        def cols(w):
                            return w[:, k % HL_SLOTS, P * t:P * t + P]
                        ins = mm3(bank[t][:, 0:NQ], cols(whi), cols(wlo), cqhi[:, k, :], cqlo[:, k, :],
                                  k == 0, k == KQ - 1, k == 0 and t == 0)
                        if k == KQ - 1:
                            ins.then_inc(full[t], 1)
                    if k < KQ - 1:
                        ins.then_inc(unit_used, 1)
                    hooks(k)

            def kv_units(n, phase, i, hook):
                for k in range(KC):
                    slot = (KQ + k) % HL_SLOTS
                    pe.wait_ge(lo_done, U_PAIR + n * PAIR_UNITS + KQ + k + 1)
                    last = k == KC - 1
                    for h, b in ((0, 3), (1, 0)):
                        if k == 0:
                            fill(phase, b, (0, 1)[h], i)
                        s = slice(256 * h, 256 * h + P)
                        ins = mm3(bank[b][:, 0:NKV], whi[:, slot, s], wlo[:, slot, s], ckhi[:, k, :], cklo[:, k, :],
                                  k == 0, last, k == 0 and h == 0)
                        if last:
                            ins.then_inc(full[b], 1)

                    def vcols(w):
                        return w[:, slot, :].rearrange("p (h c) -> p h c", h=2)[:, :, NOPE:256]
                    for t, c0 in enumerate((0, P, 2 * P, NT)):
                        m = P
                        b, half = 1 + t // 2, t % 2
                        if k == 0 and half == 0:
                            fill(phase, b, 1, i)
                        out = bank[b][0:m, 256 * half:256 * half + 256].rearrange("p (h c) -> p h c", h=2)
                        cs = slice(c0, c0 + m)
                        mm(out, ckhi[:, k, cs], vcols(whi), start=k == 0 and half == 0, stop=False,
                           skip_group_check=True)
                        mm(out, cklo[:, k, cs], vcols(whi), start=False, stop=False, skip_group_check=True)
                        ins = mm(out, ckhi[:, k, cs], vcols(wlo), start=False, stop=last, skip_group_check=True)
                        if last and half == 1:
                            ins.then_inc(full[b], 1)
                    if not last:
                        ins.then_inc(unit_used, 1)
                    if k == 1:
                        hook()

            def q_squares(phase, i, n):
                first = phase == "bulk0"
                for t in range(3):
                    b = 4 + t
                    pe.wait_ge(q_sq, 3 * n + t + 1)
                    fill(phase, b, 0 if first else (2, 4, 3)[t], i)
                    mm(bank[b][:, 0:NQ], ones if t < 2 else blockones, sq3[:, t, :], start=True, stop=True)\
                        .then_inc(full[b], 1)
                pe.wait_ge(gsc_d, 3)
                fill(phase, 7, 0 if first else 3, i)
                mm(bank[7][:, 0:NQ], rotq[:, :], qp[:, :], start=True, stop=True).then_inc(full[7], 1)

            def latent(k):
                if k == 1:
                    fill("latent", 5)
                    for t in range(KC):
                        pe.wait_ge(ck_sq, t + 1)
                        ins = mm(bank[5][:, 0:NT], ones, sq2[:, t % 2, 0:NT], start=t == 0, stop=t == KC - 1)
                        ins.then_inc(full[5] if t == KC - 1 else ck_ssm, 1)
                    pe.wait_ge(free[0], use("narrow", 0) + 1)
                    fill("latent", 6)
                    mm(bank[6][:, 0:NT], dup, nraw[0:64, :], start=True, stop=True).then_inc(full[6], 1)
                if k == 3:
                    pe.wait_ge(cache_in, 48)
                    fill("latent", 4)
                    for t in range(KC):
                        ins = tr(bank[4][:, t * P:t * P + P], cacher[:, t * P:t * P + P], ident)
                    ins.then_inc(full[4], 1)
                    fill("latent", 7)
                    tr(bank[7][:, 0:P], cacher[:, 512:640], ident).then_inc(full[7], 1)
                if k == 5:
                    pe.wait_ge(kp_sq, 1)
                    fill("latent", 6, 1)
                    mm(bank[6][:, 0:NT], blockones, sqk0, start=True, stop=True).then_inc(full[6], 1)
                    fill("latent", 7, 1)
                    pe.wait_ge(gsc_d, 4)
                    mm(bank[7][:, 0:NT], rope1[:, 0:P], kpr, start=True, stop=True).then_inc(full[7], 1)
                if k == 8:
                    pe.wait_ge(ck_n, KC)
                    for t, (c0, n) in enumerate(TOK):
                        b = 4 + t
                        fill("latent", b, (1, 1, 2)[t])
                        for f in range(KC):
                            ins = tr(bank[b][0:n, f * P:f * P + P], ckvf[:, f, c0:c0 + n], ident)
                        ins.then_inc(full[b], 1)
                if k == 10:
                    pe.wait_ge(kp_n, 1)
                    fill("latent", 7, 2)
                    for t, (c0, n) in enumerate(TOK):
                        ins = tr(bank[7][0:n, 64 * t:64 * t + 64], kpe_n[0:64, c0:c0 + n], ident[0:64, 0:64])
                    ins.then_inc(full[7], 1)
            q_units(0, "bulk0", 0, latent)
            pe.wait_ge(ck_lo, KC)
            pe.wait_ge(free[4], use("latent", 4) + 1)
            kv_units(0, "bulk0", 0, lambda: q_squares("bulk0", 0, 0))

            def k_squares(phase, i, j):
                for t in range(2):
                    b = 6 + t
                    pe.wait_ge(k_sq, 2 * j + t + 1)
                    fill(phase, b, 0, i)
                    mm(bank[b][:, 0:NKV], ones, sq2[:, t, :], start=True, stop=True).then_inc(full[b], 1)

            def scores(phase, i, j, h):
                if h == 0:
                    pe.wait_ge(q_fin, 2 * j + 2)
                    pe.wait_ge(qp_fin, j + 1)
                    pe.wait_ge(kp_st, 3)
                    pe.wait_ge(free[7], use("latent", 7) + 1)
                pe.wait_ge(k_fin, 2 * j + h + 1)
                fill(phase, 4, h, i)
                ind, neg = c("causal_ind"), c("causal_neg")
                for q0, at, keys in ((0, 0, N_META + P), (P, 144, C_SAMPLE)):
                    out = bank[4][:, at:at + keys]
                    mm(out, qn[:, h, q0:q0 + P], kn[:, h, 0:keys], start=True, stop=False)
                    mm(bank[4][:, at + keys - CHUNK:at + keys], ind, neg, start=False, stop=False)
                    ins = mm(out, qp[:, q0:q0 + P], kpe2[h][:, 0:keys], start=False, stop=True)
                ins.then_inc(full[4], 1)
                fill(phase, 5, h, i)
                for a, k0, w in ((0, 0, N_META), (N_META, 256, NKV - 256)):
                    out = bank[5][0:DEC, a:a + w]
                    mm(out, qn[:, h, SEQ:NQ], kn[:, h, k0:k0 + w], start=True, stop=False)
                    if a:
                        mm(bank[5][0:DEC, a:a + TAIL], ind[:, 0:DEC], neg[:, 0:TAIL], start=False, stop=False)
                    ins = mm(out, qp[:, SEQ:NQ], kpe2[h][:, k0:k0 + w], start=False, stop=True)
                ins.then_inc(full[5], 1)

            def transposes(phase, i, j, h):
                pe.wait_ge(pn, 6 * j + 3 * h + 3)
                fill(phase, 6, 1 + h, i)
                for at, a, m in ((0, 0, P), (128, 144, P), (256, 272, P)):
                    tr(bank[6][:, at:at + m], prob[:, a:a + P], ident)
                tr(bank[6][:, 384:416], prob[0:DEC, 480:608], ident[0:DEC, 0:DEC]).then_inc(full[6], 1)
                fill(phase, 7, 1 + h, i)
                tr(bank[7][0:TAIL, 0:128], prob[:, 128:144], ident)
                tr(bank[7][0:TAIL, 128:256], prob[:, 400:416], ident)
                tr(bank[7][0:TAIL, 256:288], prob[0:DEC, 416:432], ident[0:DEC, 0:DEC])
                tr(bank[7][0:48, 288:320], prob[0:DEC, 432:480], ident[0:DEC, 0:DEC]).then_inc(full[7], 1)

            def weighted(phase, i, j, h):
                pe.wait_ge(v_ev, j + 1)
                pe.wait_ge(free[6], use(phase, 6, 1 + h, i) + 1)
                pe.wait_ge(free[7], use(phase, 7, 1 + h, i) + 1)
                fill(phase, 5, 2 + h, i)
                vh = slice(P * h, P * h + P)
                for cols, parts in (
                        (slice(0, 128), ((0, P, 0), (1, TAIL, 416))),
                        (slice(128, 256), ((0, P, 128), (1, P, 256), (2, TAIL, 544))),
                        (slice(256, 288), ((0, TAIL, 672), (2, 48, 704), (3, P, 384)))):
                    w = cols.stop - cols.start
                    for n, (t, k, at) in enumerate(parts):
                        ins = mm(bank[5][:, cols], vt[0:k, t, vh], probT[0:k, at:at + w], start=n == 0,
                                 stop=n == len(parts) - 1)
                ins.then_inc(full[5], 1)

            def attention(phase, i, j):
                def hooks(k):
                    if k == 1:
                        k_squares(phase, i, j)
                    if k == 4:
                        scores(phase, i, j, 0)
                    if k == 6:
                        transposes(phase, i, j, 0)
                        scores(phase, i, j, 1)
                    if k == 8:
                        weighted(phase, i, j, 0)
                    if k == 9:
                        transposes(phase, i, j, 1)
                    if k == 11:
                        weighted(phase, i, j, 1)
                return hooks

            with pe.Fori(0, 7) as j:
                q_units(j + 1, "step", j, attention("step", j, j))
                kv_units(j + 1, "step", j, lambda: q_squares("step", j, j + 1))
            group(U_ML, "ml0qk", 0, 0, 0, attention("ml0qk", 0, 7))

            def row_hooks(k):
                if k == 1:
                    for b, a in ((4, 64), (5, 68)):
                        fill("rows", b)
                        mm(bank[b][0:ML_HEADS, 0:NT], ident[0:72, a:a + 4], nraw[:, :], start=True, stop=True)\
                            .then_inc(full[b], 1)
                if k == 9:
                    pe.wait_ge(r_v, 9)
                    fill("rows", 6)
                    for t, (c0, n) in enumerate(TOK):
                        ins = tr(bank[6][0:n, 4 * t:4 * t + 4], R4["crow"][:, c0:c0 + n], ident[0:4, 0:4])
                    ins.then_inc(full[6], 1)
                    fill("rows", 7)
                    for t, (q0, n) in enumerate(MQT):
                        ins = tr(bank[7][0:n, 4 * t:4 * t + 4], R4["mrow"][:, N_META + q0:N_META + q0 + n],
                                 ident[0:4, 0:4])
                    ins.then_inc(full[7], 1)
            R4 = rows
            group(U_ML + KT, "ml0v", 0, 0, 0, row_hooks)

            def mlstm(phase, i, h):
                blocks = [slice(at, at + w) for at, w in MLW]

                def hooks(k):
                    if k == 1:
                        pe.wait_ge(mh_d, h + 1)
                        fill(phase, 4, 0, i)
                        mm(bank[4][:, 0:NT + 1], ones[0:ML_HEADS, :], Mh[:, :], start=True, stop=True)\
                            .then_inc(full[4], 1)
                        qk_ready(h)
                        fill(phase, 6, 0, i)
                        for t in range(2):
                            for d in range(2):
                                ins = tr(bank[6][:, 256 * t + P * d:256 * t + P * d + P],
                                         mkT[:, d, TOK[t][0]:TOK[t][0] + P], ident)
                        ins.then_inc(full[6], 1)
                        fill(phase, 7, 0, i)
                        apart()
                        for d in range(2):
                            ins = tr(bank[7][0:48, P * d:P * d + P], mkT[:, d, 256:NT], ident)
                        ins.then_inc(full[7], 1)
                    if k == 3:
                        fill(phase, 5, 0, i)
                        for t, (c0, n) in enumerate(TOK):
                            for d in range(2):
                                ins = mm(bank[5][0:n, blocks[t]], mkT[:, d, c0:c0 + n],
                                         mqT[:, d, NT - MLW[t][1]:NT], start=d == 0, stop=d == 1)
                        ins.then_inc(full[5], 1)
                    if k == 6:
                        for t, b, nth in ((0, 6, 1), (1, 7, 1), (2, 4, 1)):
                            c0, n = TOK[t]
                            fill(phase, b, nth, i)
                            apart()
                            for e in range(4):
                                ins = tr(bank[b][0:n, P * e:P * e + P], mvT[:, e, c0:c0 + n], ident)
                            ins.then_inc(full[b], 1)
                    if k == 12:
                        pe.wait_ge(p_d, h + 1)
                        pe.wait_ge(free[5], use(phase, 5, 0, i) + 1)
                        pe.wait_ge(free[4], use(phase, 4, 1, i) + 1)
                        pe.wait_ge(free[6], use(phase, 6, 1, i) + 1)
                        pe.wait_ge(free[7], use(phase, 7, 1, i) + 1)
                        pe.wait_ge(qw_d, 2 * h + 2)
                        pe.wait_ge(C0_in, 16 * (h + 1))
                        for q, (q0, m) in enumerate(MQT):
                            b = 5 + q
                            fill(phase, b, (1, 2, 2)[q], i)
                            for t in range(q + 1):
                                at = MLW[t][0] + q0 - (NQ - MLW[t][1])
                                n = TOK[t][1]
                                ins = mm(bank[b][0:m, :], Pt[0:n, at:at + m], vtok[0:n, t, :], start=t == 0,
                                         stop=t == q and q < 2)
                            if q == 2:
                                for d in range(2):
                                    ins = mm(bank[b][0:m, :], qw[:, d, :], C0[:, d, :], start=False, stop=d == 1)
                            ins.then_inc(full[b], 1)
                        fill(phase, 4, 2, i)
                        for q, (q0, m) in enumerate(MQT):
                            m = P if q == 0 else m
                            for t in range(q + 1):
                                at = MLW[t][0] + q0 - (NQ - MLW[t][1])
                                n = TOK[t][1]
                                ins = mm(bank[4][0:m, q:q + 1], Pt[0:n, at:at + m], ones[0:n, 0:1], start=t == 0,
                                         stop=t == q and q < 2)
                            if q == 2:
                                for d in range(2):
                                    ins = mm(bank[4][0:m, q:q + 1], qw[:, d, :], G[:, ds(G_N0 + 2 * h + d, 1)],
                                             start=False, stop=d == 1)
                        ins.then_inc(full[4], 1)
                    if k == 22:
                        for q in range(3):
                            pe.wait_ge(free[5 + q], use(phase, 5 + q, (1, 2, 2)[q], i) + 1)
                        for e in range(4):
                            b = 4 + e
                            fill(phase, b, (3, 2, 3, 3)[e], i)
                            for q, (q0, m) in enumerate(MQT):
                                ins = tr(bank[b][:, q0:q0 + m], hn[0:m, q, P * e:P * e + P], ident[0:m, 0:m])
                            ins.then_inc(full[b], 1)
                    if k == 25:
                        pe.wait_ge(kws_d, 2 * h + 2)
                        for d in range(2):
                            b = 5 + d
                            fill(phase, b, 3 + d, i)
                            for t in range(3):
                                n = TOK[t][1]
                                ins = mm(bank[b][:, :], kws[0:n, t, P * d:P * d + P], vtok[0:n, t, :],
                                         start=t == 0, stop=t == 2)
                            ins.then_inc(full[b], 1)
                    if k == 28:
                        for d in range(2):
                            b = 5 + d
                            fill(phase, b, 4 + d, i)
                            mm(bank[b][:, :], kws[0:48, 3, P * d:P * d + P], vtok[0:48, 2, :], start=True, stop=True)\
                                .then_inc(full[b], 1)
                        fill(phase, 7, 4, i)
                        for d in range(2):
                            for t in range(3):
                                n = TOK[t][1]
                                mm(bank[7][:, d:d + 1], kws[0:n, t, P * d:P * d + P], ones[0:n, 0:1],
                                   start=t == 0, stop=t == 2)
                        for d in range(2):
                            ins = mm(bank[7][:, 2 + d:3 + d], kws[0:48, 3, P * d:P * d + P], ones[0:48, 0:1],
                                     start=True, stop=True)
                        ins.then_inc(full[7], 1)
                return hooks

            def qk_ready(h):
                for b in range(4):
                    pe.wait_ge(free[b], use("ml0v", b) + 1 + 2 * h)

            with pe.Fori(0, 3) as h:
                group(U_ML + 2 * KT + h * (2 * KT), "ml", 0, h, 0, mlstm("ml", h, h))
                group(U_ML + 3 * KT + h * (2 * KT), "ml", 1, h, 0)
            group(U_GATE, "gate0", 0, 0, N_META, mlstm("gate0", 0, 3))
            with pe.Fori(0, 11) as g:
                group(U_GATE + KT + g * KT, "gate", 0, g, N_META)
            fill("nout", 4)
            pe.wait_ge(free[7], use("nout", 7))
            tr(bank[4][0:16, 0:P], ncol[:, :], ident).then_inc(full[4], 1)
            group(U_OUT, "out0", 0, 0, N_META, a_hi=mhi, a_lo=mlo, ready=mix_lo)

            def y_rows(phase, i):
                for b in range(4):
                    pe.wait_ge(free[b], use(phase, b, 0, i) if phase == "out" else use("outlast", b))
                for t, (q0, m) in enumerate(QT):
                    b = 4 + t
                    fill(phase, b, 0, i)
                    for ct in range(4):
                        ins = tr(bank[b][0:m, ct * P:ct * P + P], yT[:, ct, q0:q0 + m], ident)
                    ins.then_inc(full[b], 1)

            with pe.Fori(0, 7) as g:
                group(U_OUT + KT + g * KT, "out", 0, g, N_META,
                      lambda k: y_rows("out", g) if k == 2 else None, a_hi=mhi, a_lo=mlo)
            y_rows("outlast", 0)

        @block.gpsimd
        def _(pool):
            tt, ts_ = nc.gpsimd.tensor_tensor, nc.gpsimd.tensor_scalar

            def apart():
                pool.sem_inc(passed_pool, 1)

            pool.dma_start(con[:, :], consts).then_inc(const_in, 16)

            def rows_of(v, n):
                return v.rearrange("(r c) -> r c", c=P) if n > 1 else v.rearrange("(a c) -> a c", a=1)
            pool.dma_start(Grows[G_X:G_X + 32, :], rows_of(norm_gain, 32)).then_inc(grows_in, 16)
            pool.dma_start(Grows[G_QA:G_QA + 12, :], rows_of(q_a, 12)).then_inc(grows_in, 16)
            pool.dma_start(Grows[G_KVA:G_KVA + 4, :], rows_of(kv_a, 4)).then_inc(grows_in, 16)
            pool.dma_start(Grows[G_MLO:G_MLO + 16, :], ml_out.rearrange("h (r c) -> (h r) c", c=P)).then_inc(grows_in, 16)
            pool.dma_start(Grows[G_QN:G_QN + 1, :], rows_of(q_nope, 1)).then_inc(grows_in, 16)
            pool.dma_start(Grows[G_KN:G_KN + 1, :], rows_of(k_nope, 1)).then_inc(grows_in, 16)
            for half in range(2):
                s = slice(64 * half, 64 * half + 64)
                pool.dma_start(Grows[G_QR:G_QR + 1, s], rows_of(q_rope, 1)).then_inc(grows_in, 16)
                pool.dma_start(Grows[G_KR:G_KR + 1, s], rows_of(k_rope, 1)).then_inc(grows_in, 16)
            pool.dma_start(Grows[G_N0:G_N0 + 8, :], state_n[0].rearrange("h (r c) -> (h r) c", c=P)).then_inc(grows_in, 16)
            pool.dma_start(gate_b[:, 0:1], b_ig.rearrange("(h a) -> h a", a=1)).then_inc(gb_in, 16)
            pool.dma_start(gate_b[:, 1:2], b_fg.rearrange("(h a) -> h a", a=1)).then_inc(gb_in, 16)
            pool.dma_start(gate_b[:, 2:3], state_m.rearrange("a h -> h a")).then_inc(gb_in, 16)
            for b in range(4, 8):
                pool.wait_ge(full[b], use("cq", b))
            pool.dma_start(cacher[:, 0:512], cache_ckv[0]).then_inc(cache_in, 16)
            pool.dma_start(cacher[:, 512:576], cache_kpe[0]).then_inc(cache_in, 16)
            pool.dma_start(cacher[:, 576:640], cache_kpe[0]).then_inc(cache_in, 16)

            for ct in range(4):
                pool.wait_ge(free[ct], use("ckv", ct))
            for t in range(KQ):
                if t >= 3:
                    pool.wait_ge(cq_ssm, t - 2)
                tt(sq3[:, t % 3, :], cqraw[:, t, :], cqraw[:, t, :], ALU.mult).then_inc(cq_sq, 1)
            for ct in range(4):
                pool.wait_ge(free[ct], use("narrow", ct) if ct else use("ckv", 0) + 1)
            pool.wait_ge(full[4], use("ckv", 4) + 1)
            for t in range(KC):
                if t >= 2:
                    pool.wait_ge(ck_ssm, t - 1)
                tt(sq2[:, t % 2, 0:NT], ckvf[:, t, :], ckvf[:, t, :], ALU.mult).then_inc(ck_sq, 1)
            pool.wait_ge(free[6], use("latent", 6) + 1)
            pool.wait_ge(full[5], use("latent", 5) + 1)
            tt(sqk0, kpr, kpr, ALU.mult).then_inc(kp_sq, 1)
            pool.wait_ge(kp_c, 1)
            pool.wait_ge(free[7], use("latent", 7, 1) + 1)
            tt(rope1[:, :], rope1[:, :], rope2[:, :], ALU.add).then_inc(kp_a, 1)
            pool.wait_ge(kp_a, 1)
            pool.wait_ge(kp_rs, 1)
            tt(kpe_n, rope1[:, :], rs2[:, 1, 0:NT], ALU.mult).then_inc(kp_n, 1)
            pool.wait_ge(kp_rows, 1)
            pool.wait_ge(free[7], use("latent", 7, 2) + 1)
            pool.dma_start(kpe_p[0, 0:128, :], kout[:, 0:64]).then_inc(kp_out, 16)
            pool.dma_start(kpe_p[0, 128:256, :], kout[:, 64:128]).then_inc(kp_out, 16)
            pool.dma_start(kpe_p[0, 256:272, :], kout[0:TAIL, 128:192]).then_inc(kp_out, 16)
            pool.dma_start(kpe_s[0, :, :], kout[TAIL:48, 128:192]).then_inc(kp_out, 16)
            pool.wait_ge(free[6], use("latent", 6, 2) + 1)
            pool.dma_start(ckv_p[0, 256:272, :], orow[0:TAIL, 0:512]).then_inc(ck_tail_out, 16)
            pool.dma_start(ckv_s[0, :, :], orow[TAIL:48, 0:512]).then_inc(ck_tail_out, 16)

            def q_square(phase, i, n):
                for t in range(3):
                    pool.wait_ge(free[t], use(phase, t, 0, i) + 1)
                    src = qn[:, t, :] if t < 2 else qp[:, :]
                    tt(sq3[:, t, :], src, src, ALU.mult).then_inc(q_sq, 1)

            def k_square(phase, i, n):
                for t, b in ((0, 3), (1, 0)):
                    pool.wait_ge(free[b], use(phase, b, (0, 1)[t], i) + 1)
                    for q in range(3):
                        pool.wait_ge(full[4 + q], use(phase, 4 + q, (0 if phase == "bulk0" else (2, 4, 3)[q]), i) + 1)
                    tt(sq2[:, t, :], kn[:, t, :], kn[:, t, :], ALU.mult).then_inc(k_sq, 1)

            def q_turn(phase, i, n):
                pool.wait_ge(qp_c, n + 1)
                pool.wait_ge(free[7], use(phase, 7, 0 if phase == "bulk0" else 3, i) + 1)
                tt(rope1[:, 0:NQ], rope1[:, 0:NQ], rope2[:, 0:NQ], ALU.add).then_inc(qp_a, 1)
                pool.wait_ge(qp_a, n + 1)
                pool.wait_ge(q_rs, 3 * n + 3)
                tt(qp[:, :], rope1[:, 0:NQ], rs3[:, 2, :], ALU.mult).then_inc(qp_fin, 1)

            def norm_probs(phase, i, j, h):
                pool.wait_ge(free[4], use(phase, 4, h, i) + 1)
                apart()
                ts_(prob[:, 0:144], prob[:, 0:144], pinv[:, 0:1], None, ALU.mult).then_inc(pn, 1)
                ts_(prob[:, 144:416], prob[:, 144:416], pinv[:, 1:2], None, ALU.mult).then_inc(pn, 1)
                pool.wait_ge(free[5], use(phase, 5, h, i) + 1)
                apart()
                ts_(prob[0:DEC, 416:608], prob[0:DEC, 416:608], pinv[0:DEC, 2:3], None, ALU.mult).then_inc(pn, 1)

            q_square("bulk0", 0, 0)
            k_square("bulk0", 0, 0)
            q_turn("bulk0", 0, 0)
            with pool.Fori(0, 7) as j:
                norm_probs("step", j, j, 0)
                norm_probs("step", j, j, 1)
                q_square("step", j, j + 1)
                k_square("step", j, j + 1)
                q_turn("step", j, j + 1)
            norm_probs("ml0qk", 0, 7, 0)
            norm_probs("ml0qk", 0, 7, 1)

            for h in range(2):
                pool.wait_ge(free[5], use("ml0qk", 5, 2 + h) + 1)
            pool.dma_start(mask[:, :], mlmask).then_inc(mask_in, 16)
            pool.wait_ge(r_v, 9)
            pool.dma_start(m_p.rearrange("a h -> h a"), rows["mrow"][:, C_SAMPLE - 1:C_SAMPLE]).then_inc(m_out, 16)
            pool.dma_start(m_s.rearrange("a h -> h a"), rows["mrow"][:, NT - 1:NT]).then_inc(m_out, 16)

            def mlstm(phase, i, h):
                pool.dma_start(C0[:, :, :], state_C[0, ds(h, 1), :, :].rearrange("a (d p) e -> p (a d) e", p=P))\
                    .then_inc(C0_in, 16)
                pool.wait_ge(mask_in, 16)
                pool.wait_ge(e_x, 2 * h + 2)
                tt(E[:, 0:464], E[:, 0:464], mask[:, 0:464], ALU.mult).then_inc(e_m, 1)
                tt(E[0:48, 464:512], E[0:48, 464:512], mask[0:48, 464:512], ALU.mult).then_inc(e_m, 1)
                for d in range(2):
                    pool.wait_ge(free[5 + d], use(phase, 5 + d, 4 + d, i) + 1)
                    apart()
                pool.dma_start(C_s[0, ds(h, 1), :, :].rearrange("a (d p) e -> p (a d) e", p=P),
                               Cout[:, 2:4, :]).then_inc(Cs_out, 16)

            with pool.Fori(0, 3) as h:
                mlstm("ml", h, h)
                pool.wait_ge(Cs_out, 16 * h + 16)
                apart()
            mlstm("gate0", 0, 3)

            def apply(phase, i, dst, at, src):
                for ct in range(4):
                    pool.wait_ge(free[ct], use(phase, ct, 0, i) + 1)
                    tt(dst[:, ds(at + ct, 1), :], dst[:, ds(at + ct, 1), :], src[:, ct:ct + 1, :], ALU.mult)\
                        .then_inc(gm_d, 1)

            apply("gate0", 0, attnT, 0, gt)
            with pool.Fori(1, 4) as g:
                apply("gate", g - 1, attnT, 4 * g, gt)
            with pool.Fori(0, 4) as g:
                apply("gate", g + 3, hT, 4 * g, sg)
            with pool.Fori(0, 4) as g:
                apply("gate", g + 7, hT, 4 * g, gt)

            pool.wait_ge(free[4], use("nout", 4) + 1)
            pool.dma_start(n_p[0].rearrange("h (r c) -> (h r) c", c=P), nrow[0:8, :]).then_inc(n_out, 16)
            pool.dma_start(n_s[0].rearrange("h (r c) -> (h r) c", c=P), nrow[8:16, :]).then_inc(n_out, 16)

            def fetch_x(g):
                cs = ds(g * 512, 512)
                pool.dma_start(xres[:, 0, :], x_prompt[0, 0:128, cs]).then_inc(xres_in, 16)
                pool.dma_start(xres[:, 1, :], x_prompt[0, 128:256, cs]).then_inc(xres_in, 16)
                pool.dma_start(xres[0:DEC, 2, :], x_sample[0, :, cs]).then_inc(xres_in, 16)

            def store_y(phase, i, g):
                cs = ds(g * 512, 512)
                for t, dst in enumerate((y_p[0, 0:128, cs], y_p[0, 128:256, cs], y_s[0, :, cs])):
                    pool.wait_ge(free[4 + t], use(phase, 4 + t, 0, i) + 1)
                    apart()
                    pool.dma_start(dst, ytok[0:QT[t][1], t, :]).then_inc(y_out, 16)

            pool.wait_ge(n_out, 32)
            fetch_x(0)
            with pool.Fori(0, 7) as g:
                store_y("out", g, g)
                fetch_x(g + 1)
            store_y("outlast", 0, 7)
            pool.wait_ge(y_out, 8 * 48)
            pool.wait_ge(Cp_out, 4 * 16)
            pool.wait_ge(Cs_out, 4 * 16)
            pool.wait_ge(m_out, 32)
            pool.wait_ge(ck_out, 32)
            pool.wait_ge(ck_tail_out, 32)
            pool.wait_ge(kp_out, 4 * 16)


_INS = ["x_prompt", "x_sample", "cache_ckv", "cache_kpe", "state_C", "state_n", "state_m", "meta_tokens",
        "norm_gain", "w_in", "b_igate", "b_fgate", "q_a_norm", "w_q_up", "q_nope_norm", "q_rope_norm",
        "kv_a_norm", "k_rope_norm", "w_kv_up", "k_nope_norm", "ml_out_norm", "w_out"]
_OUTS = [(1, SEQ, D_MODEL), (1, DEC, D_MODEL), (1, N_META + SEQ, KV_LORA), (1, N_META + SEQ, ROPE),
         (1, ML_HEADS, DQK, DV), (1, ML_HEADS, DQK), (1, ML_HEADS), (1, DEC, KV_LORA), (1, DEC, ROPE),
         (1, ML_HEADS, DQK, DV), (1, ML_HEADS, DQK), (1, ML_HEADS)]


def kernel(**inputs):
    import concourse.bacc as bacc
    from concourse.bass_utils import run_bass_kernel_spmd

    nc = bacc.Bacc("TRN2", target_bir_lowering=False, num_devices=1)
    arrays, args = {}, []
    table, mask = shape_constants()
    for name, a in [(n, inputs[n]) for n in _INS] + [("shape_table", table), ("mlstm_mask", mask)]:
        a = np.ascontiguousarray(a)
        arrays[f"in_{name}_dram"] = a
        args.append(nc.dram_tensor(f"in_{name}_dram", a.shape, mybir.dt.from_np(a.dtype),
                                   kind="ExternalInput").ap())
    for i, shape in enumerate(_OUTS):
        args.append(nc.dram_tensor(f"out_{i}_dram", shape, mybir.dt.float32, kind="ExternalOutput").ap())
    hymba_step(nc, *args)
    r = run_bass_kernel_spmd(nc, [arrays], core_ids=[0])
    return tuple(r.results[0][f"out_{i}_dram"] for i in range(len(_OUTS)))
```

```python
from contextlib import ExitStack

import concourse.bass as bass
import numpy as np
from concourse import mybir

D_MODEL = 4096
SEQ, DEC, PAST, N_META = 256, 32, 128, 16
KV_LORA, Q_LORA, ROPE = 512, 1536, 64
MLA_HEADS, NOPE, V_HEAD = 16, 128, 128
ML_HEADS, DQK, DV = 4, 256, 512
OFF_CQ = 0
OFF_CKV = OFF_CQ + Q_LORA
OFF_KPE = OFF_CKV + KV_LORA
OFF_MQ = OFF_KPE + ROPE
OFF_MK = OFF_MQ + ML_HEADS * DQK
OFF_MV = OFF_MK + ML_HEADS * DQK
OFF_MO = OFF_MV + ML_HEADS * DV
OFF_MI = OFF_MO + ML_HEADS * DV
OFF_ZA = OFF_MI + 2 * ML_HEADS
OFF_ZB = OFF_ZA + MLA_HEADS * V_HEAD
EPS = 1e-6
ATTN_SCALE = (NOPE + ROPE) ** -0.5
CHUNK = 64
NEG = -1e30

P = 128
NT = N_META + SEQ + DEC
NQ = SEQ + DEC
NKV = NT + PAST
C_SAMPLE = N_META + SEQ
KT = D_MODEL // P
KQ = Q_LORA // P
KC = KV_LORA // P
TOK = [(0, 128), (128, 128), (256, 48)]
TAIL = C_SAMPLE - 256
QT = [(0, 128), (128, 128), (256, 32)]
MQT = [(0, 112), (112, 128), (240, 48)]
MLW = [(0, 288), (288, 176), (464, 48)]

RAW_SLOTS = 4
HL_SLOTS = 4
AHEAD = HL_SLOTS - 1
X_ORDER = (2, 0, 1)
XH = (slice(0, D_MODEL // 2), slice(D_MODEL // 2, D_MODEL))
X_PARTS = 4
U_CQ = 0
U_CKV = U_CQ + 3 * KT
U_NAR = U_CKV + KT
NAR_UNITS = 8
U_PAIR = U_NAR + NAR_UNITS
PAIR_UNITS = KQ + KC
U_ML = U_PAIR + (MLA_HEADS // 2) * PAIR_UNITS
U_GATE = U_ML + ML_HEADS * 2 * KT
U_OUT = U_GATE + 12 * KT

PHASES = [
    ("gain", 1, (0, 0, 0, 0, 1, 0, 0, 0)),
    ("x", 1, (0, 0, 0, 0, 8, 8, 8, 8)),
    ("cq", 3, (1, 1, 1, 1, 0, 0, 0, 0)),
    ("ckv", 1, (1, 1, 1, 1, 1, 0, 0, 0)),
    ("narrow", 1, (1, 0, 0, 0, 0, 0, 0, 0)),
    ("latent", 1, (0, 0, 0, 0, 2, 2, 3, 3)),
    ("bulk0", 1, (2, 2, 2, 1, 1, 1, 1, 1)),
    ("step", 7, (2, 2, 2, 1, 3, 5, 4, 4)),
    ("ml0qk", 1, (1, 1, 1, 1, 2, 4, 3, 3)),
    ("rows", 1, (0, 0, 0, 0, 1, 1, 1, 1)),
    ("ml0v", 1, (1, 1, 1, 1, 0, 0, 0, 0)),
    ("ml", 3, (2, 2, 2, 2, 4, 5, 6, 5)),
    ("gate0", 1, (1, 1, 1, 1, 4, 5, 6, 5)),
    ("gates", 5, (1, 1, 1, 1, 1, 1, 1, 1)),
    ("nout", 1, (1, 0, 0, 0, 0, 0, 0, 0)),
    ("gate11", 1, (0, 0, 0, 0, 1, 1, 1, 1)),
    ("out0", 1, (1, 1, 1, 1, 0, 0, 0, 0)),
    ("out", 7, (1, 1, 1, 1, 1, 1, 1, 0)),
    ("outlast", 1, (0, 0, 0, 0, 1, 1, 1, 0)),
]


def bank_base():
    base, total = {}, [0] * 8
    for name, times, uses in PHASES:
        base[name] = (list(total), uses)
        total = [t + times * u for t, u in zip(total, uses)]
    return base


BASE = bank_base()


def use(phase, bank, nth=0, i=0):
    before, uses = BASE[phase]
    return before[bank] + nth + i * uses[bank]


CONST_PARTS = [("ident", 128), ("blockones", 128), ("ones", 128), ("rot", 128), ("dup", 128),
               ("cos", NT), ("sin", NT), ("causal_ind", 128), ("causal_neg", 64),
               ("rowmask", 4)]
CONST_AT = {}
_n = 0
for _name, _w in CONST_PARTS:
    CONST_AT[_name] = (_n, _w)
    _n += _w
CONST_COLS = _n
G_X, G_QA, G_KVA, G_MLO, G_QN, G_KN, G_QR, G_KR, G_N0 = 0, 32, 44, 48, 64, 65, 66, 67, 68
G_ROWS = 76


def shape_constants():
    t = np.zeros((P, CONST_COLS), np.float32)

    def part(name):
        a, w = CONST_AT[name]
        return t[:, a:a + w]

    part("ident")[:] = np.eye(P, dtype=np.float32)
    for b in range(2):
        part("blockones")[64 * b:64 * b + 64, 64 * b:64 * b + 64] = 1.0
        for f in range(32):
            part("rot")[64 * b + 32 + f, 64 * b + f] = -1.0
            part("rot")[64 * b + f, 64 * b + 32 + f] = 1.0
        for f in range(64):
            part("dup")[f, 64 * b + f] = 1.0
    part("ones")[:] = 1.0
    pos = np.concatenate([np.arange(C_SAMPLE), N_META + PAST + np.arange(DEC)]).astype(np.float32)
    inv = np.float32(10000.0) ** (-np.arange(32, dtype=np.float32) / np.float32(32))
    ang = (pos[None, :] * inv.astype(np.float32)[:, None]).astype(np.float32)
    part("cos")[:] = np.tile(np.cos(ang), (4, 1))
    part("sin")[:] = np.tile(np.sin(ang), (4, 1))
    part("causal_ind")[0, 0:CHUNK] = 1.0
    part("causal_neg")[0, :] = NEG
    part("rowmask")[:, 0:2] = 1.0
    part("rowmask")[0:TAIL, 2] = 1.0
    part("rowmask")[TAIL:48, 3] = 1.0
    mask = np.zeros((P, 512), np.float32)
    for (c0, rows), (at, width) in zip(TOK, MLW):
        s = c0 + np.arange(rows)
        q = NT - width + np.arange(width)
        same = (s[:, None] < C_SAMPLE) == (q[None, :] < C_SAMPLE)
        mask[:rows, at:at + width] = (s[:, None] <= q[None, :]) & same
    return t, mask


def hymba_step(nc, x_prompt, x_sample, cache_ckv, cache_kpe, state_C, state_n, state_m, meta, norm_gain,
               w_in, b_ig, b_fg, q_a, w_qu, q_nope, q_rope, kv_a, k_rope, w_kvu, k_nope, ml_out, w_out,
               consts, mlmask,
               y_p, y_s, ckv_p, kpe_p, C_p, n_p, m_p, ckv_s, kpe_s, C_s, n_s, m_s):
    f32, f32r = mybir.dt.float32, mybir.dt.float32r
    ALU, ACT, AX = mybir.AluOpType, mybir.ActivationFunctionType, mybir.AxisListType
    ds = bass.ds

    ctx = ExitStack()
    with ctx:
        def keep(stack):
            return lambda name, shape, dt=f32: stack.enter_context(nc.sbuf_tensor(name, shape, dt))

        def sem(name):
            return ctx.enter_context(nc.semaphore(name))

        sb = keep(ctx)
        raw = sb("raw", [P, RAW_SLOTS, 1024])
        whi = sb("whi", [P, HL_SLOTS, 512], f32r)
        wlo = sb("wlo", [P, HL_SLOTS, 512], f32r)
        con = sb("con", [P, CONST_COLS])
        G = sb("G", [P, G_ROWS])
        nraw = sb("nraw", [72, NT])
        epsc = sb("epsc", [P, 1])
        gate_b = sb("gate_b", [ML_HEADS, 3])
        attnT = sb("attnT", [P, MLA_HEADS, NQ])

        def c(name, rows=P):
            a, w = CONST_AT[name]
            return con[0:rows, a:a + w]

        ident, blockones, ones, rot, dup = c("ident"), c("blockones"), c("ones"), c("rot"), c("dup", 64)
        cosT, sinT = c("cos"), c("sin")

        px = ExitStack()
        xhi = keep(px)("xhi", [P, KT, NT], f32r)
        xlo = keep(px)("xlo", [P, KT, NT], f32r)

        p1 = ExitStack()
        xt = [keep(p1)(f"xt{t}", [P, D_MODEL]) for t in range(3)]
        Grows = keep(p1)("Grows", [G_ROWS, P])
        xss = keep(p1)("xss", [P, 4])
        xbias = keep(p1)("xbias", [P, 1])
        xrs = keep(p1)("xrs", [P, 3])
        p1.close()

        p2 = ExitStack()
        sb2 = keep(p2)
        cqhi = sb2("cqhi", [P, KQ, NQ], f32r)
        cqlo = sb2("cqlo", [P, KQ, NQ], f32r)
        ckhi = sb2("ckhi", [P, KC, NKV], f32r)
        cklo = sb2("cklo", [P, KC, NKV], f32r)
        kpe2 = [sb2(f"kpe{h}", [P, NKV]) for h in range(2)]
        qn = sb2("qn", [P, 2, NQ])
        qp = sb2("qp", [P, NQ])
        kn = sb2("kn", [P, 2, NKV])
        vt = sb2("vt", [P, 4, 2 * V_HEAD])
        sqb = sb2("sqb", [P, 3 * NQ])
        rsb = sb2("rsb", [P, 3 * NQ])
        rope1 = sb2("rope1", [P, NT])
        rope2 = sb2("rope2", [P, NT])
        rotq = sb2("rotq", [P, P])
        nmax = sb2("nmax", [P, 3])
        psum_ = sb2("psumrow", [P, 3])
        pinv = sb2("pinv", [P, 3])
        gsc = sb2("gsc", [P, 2])
        pa = ExitStack()
        prob = keep(pa)("prob", [P, 608])
        probT = keep(pa)("probT", [P, 736])
        pa.close()
        ckvf = sb2("ckvf", [P, KC, NT])
        p2.close()
        cqraw = attnT
        sq3 = sqb[:, :].rearrange("p (t n) -> p t n", t=3)
        sq2 = sqb[:, :].rearrange("p (t n) -> p t n", t=2)
        rs3 = rsb[:, :].rearrange("p (t n) -> p t n", t=3)
        rs2 = rsb[:, :].rearrange("p (t n) -> p t n", t=2)
        kpr = kn[:, 0, 0:NT]
        kpe_n = kn[:, 1, 0:NT]
        orow = vt[:, :, :].rearrange("p a b -> p (a b)")
        cacher = orow[:, 0:640]
        kout = rope2[:, 0:192]
        sqk0 = sq2[:, 0, 0:NT]

        p3 = ExitStack()
        sb3 = keep(p3)
        hT = sb3("hT", [P, 16, NQ])
        mask = sb3("mask", [P, 512])
        kws = sb3("kws", [P, 4, DQK])
        vtok = sb3("vtok", [P, 3, DV])
        E = sb3("E", [P, 512])
        Pt = sb3("Pt", [P, 512])
        Mb = sb3("Mb", [P, NT + 1])
        Mh = sb3("Mh", [ML_HEADS, NT + 1])
        rows = {n: sb3(n, [ML_HEADS, NT + 1]) for n in ("ig", "xf", "lf", "bsum", "crow", "Mrow", "mrow")}
        ccol = sb3("ccol", [P, 3, ML_HEADS])
        emcol = sb3("emcol", [P, 3, ML_HEADS])
        wi = sb3("wi", [P, DEC])
        nML = sb3("nML", [P, 2])
        wtmp = sb3("wtmp", [P, 4])
        decay = sb3("decay", [P, 1])
        qw = sb3("qw", [P, 2, 48])
        C0 = sb3("C0", [P, 2, DV])
        Cout = sb3("Cout", [P, 4, DV])
        ncol = sb3("ncol", [P, 16])
        nrow = sb3("nrow", [16, P])
        dsb = sb3("dsb", [P, 3])
        dinv = sb3("dinv", [P, 3])
        hss = sb3("hss", [P, 3])
        hfac = sb3("hfac", [P, 3])
        hn = sb3("hn", [P, 3, DV])
        pm = ExitStack()
        mqT = keep(pm)("mqT", [P, 2, NT])
        mkT = keep(pm)("mkT", [P, 2, NT])
        mvT = keep(pm)("mvT", [P, 4, NT])
        pm.close()
        sg = sb3("sg", [P, 4, NQ])
        gt = sb3("gt", [P, 4, NQ])
        p3.close()
        p4 = ExitStack()
        keep(p4)("hT_", [P, 16, NQ])
        yT = keep(p4)("yT", [P, 4, NQ])
        ytok = keep(p4)("ytok", [P, 3, 512])
        xres = keep(p4)("xres", [P, 3, 512])
        p4.close()
        px.close()
        p5 = ExitStack()
        mhi = keep(p5)("mhi", [P, KT, NQ], f32r)
        keep(p5)("meta_gap", [P, KT * N_META])
        mlo = keep(p5)("mlo", [P, KT, NQ], f32r)
        p5.close()

        bank = [ctx.enter_context(nc.psum_tensor(f"bank{b}", [P, 512], f32)) for b in range(8)]
        full = [sem(f"bank{b}_full") for b in range(8)]
        free = [sem(f"bank{b}_free") for b in range(8)]

        raw_in = [sem(f"raw{s}_in") for s in range(RAW_SLOTS)]
        hi_done = sem("hi_done")
        lo_done = sem("lo_done")
        unit_used = sem("unit_used")
        const_in, grows_in, eps_set = sem("const_in"), sem("grows_in"), sem("eps_set")
        xrow_in = [sem(f"xrow{t}_in") for t in (0, "1_left", 2, "1_right")]
        xbias_d = sem("x_bias_done")
        xsq, xln, xrstd, xscaled, xhi_d = (sem(n) for n in ("x_squares", "x_ln", "x_rstd", "x_scaled", "x_hi"))
        cq_sq, cq_ssm, cq_rs, cq_n, cq_hi, cq_lo = (sem(n) for n in (
            "cq_squares", "cq_summed", "cq_rstd", "cq_normed", "cq_hi", "cq_lo"))
        ck_sq, ck_ssm, ck_rs, ck_n, ck_hi, ck_lo = (sem(n) for n in (
            "ckv_squares", "ckv_summed", "ckv_rstd", "ckv_normed", "ckv_hi", "ckv_lo"))
        cache_in = sem("cache_in")
        kp_sq, kp_rs, kp_c, kp_a, kp_n = (sem(n) for n in (
            "kpe_squares", "kpe_rstd", "kpe_cos", "kpe_added", "kpe_normed"))
        kp_st, kp_zero, kp_rows, ck_out, ck_tail_out, kp_out = (sem(n) for n in (
            "kpe_stored", "kpe_zeroed", "kpe_rows", "ckv_out", "ckv_tail_out", "kpe_out"))
        gsc_d = sem("scaled_gains")
        q_sq, q_rs, q_fin = (sem(n) for n in ("q_squares", "q_rstd", "q_normed"))
        k_sq, k_rs, k_fin = (sem(n) for n in ("k_squares", "k_rstd", "k_normed"))
        qp_c, qp_a, qp_fin = (sem(n) for n in ("qpe_cos", "qpe_added", "qpe_normed"))
        v_ev = sem("v_evict")
        mx, ex, pn, pt_d = (sem(n) for n in ("neg_max", "exp_done", "probs_normed", "probT_minor"))
        mask_in, gb_in = sem("mask_in"), sem("gate_bias_in")
        r_v, r_abs, r_e, r_l, r_c, r_em = (sem(n) for n in ("row_vec", "row_abs", "row_exp", "row_ln", "ccol_done", "emcol_done"))
        m_out = sem("m_out")
        mh_d, e_d, e_x, e_m, p_d = (sem(n) for n in ("Mh_done", "E_diff", "E_exp", "E_masked", "Pt_done"))
        nml_s, nml_d, wt_p, wt_d, wt_x, wt_m, wi_d, dec_d, kws_d = (sem(n) for n in (
            "nML_prompt", "nML_sample", "wtmp_prompt", "wtmp_sample", "wtmp_exp", "wtmp_masked", "wi_done",
            "decay_done", "kws_done"))
        qw_z, qw_d = sem("qw_zero"), sem("qw_done")
        C0_in, Cp_out, Cs_out = sem("C0_in"), sem("C_prompt_out"), sem("C_sample_out")
        den_d, dab_d, dmx_d, din_d = (sem(n) for n in ("den_copied", "den_abs", "den_max", "den_inv"))
        hsq_d, hln_d, hrs_d, hf_d = (sem(n) for n in ("h_squares", "h_ln", "h_rstd", "h_factor"))
        n_d, n_out = sem("n_prompt_done"), sem("n_out")
        sg_d, gm_d = sem("sigmoid_done"), sem("gate_applied")
        mix_hi, mix_lo = sem("mix_hi"), sem("mix_lo")
        xres_in, y_out = sem("xres_in"), sem("y_out")
        passed_pe, passed_pool = sem("passed_pe"), sem("passed_pool")

        w_in_t = w_in.rearrange("(k p) c -> p k c", p=P)
        w_qu_t = w_qu.rearrange("(k p) c -> p k c", p=P)
        w_kvu_t = w_kvu.rearrange("(k p) c -> p k c", p=P)
        w_out_t = w_out.rearrange("(k p) c -> p k c", p=P)
        w_qk_t = w_in[:, OFF_MQ:OFF_MV].rearrange("(k p) (s c) -> p k s c", p=P, s=2)

        block = ctx.enter_context(nc.Block())

        @block.sync
        def _(sp):
            def load(b, slot, dst, src):
                if not isinstance(b, int) or b >= RAW_SLOTS:
                    sp.wait_ge(lo_done, 2 * b - 2 * RAW_SLOTS + 2)
                sp.dma_start(dst, src).then_inc(raw_in[slot], 16)

            def group(b0, col, src=w_in_t, blocks=KT // 2, width=512, first=0):
                for n in range(first, blocks):
                    s = n % RAW_SLOTS
                    dst = raw[:, s, 0:2 * width].rearrange("p (k c) -> p k c", k=2)
                    load(b0 + n, s, dst, src[:, 2 * n:2 * n + 2, ds(col, width)])

            for t in (1, 3):
                sp.wait_ge(xrow_in[t], 16)
            group(0, OFF_CQ)
            with sp.Fori(1, 3) as i:
                group(i * (KT // 2), OFF_CQ + i * 512)
            group(U_CKV // 2, OFF_CKV)
            for n in range(NAR_UNITS // 2):
                b = U_NAR // 2 + n
                dst = raw[:, n % RAW_SLOTS, 0:8 * 72].rearrange("p (k c) -> p k c", k=8)
                load(b, n % RAW_SLOTS, dst[:, :, 0:ROPE], w_in_t[:, 8 * n:8 * n + 8, OFF_KPE:OFF_KPE + ROPE])
                load(b, n % RAW_SLOTS, dst[:, :, ROPE:72], w_in_t[:, 8 * n:8 * n + 8, OFF_MI:OFF_MI + 8])

            def pair(b0, n):
                for m in range(KQ // 2):
                    s = m % RAW_SLOTS
                    dst = raw[:, s, 0:768].rearrange("p (k c) -> p k c", k=2)
                    load(b0 + m, s, dst, w_qu_t[:, 2 * m:2 * m + 2, ds(n * 384, 384)])
                for m in range(KC // 2):
                    s = (KQ // 2 + m) % RAW_SLOTS
                    dst = raw[:, s, :].rearrange("p (k c) -> p k c", k=2)
                    load(b0 + KQ // 2 + m, s, dst, w_kvu_t[:, 2 * m:2 * m + 2, ds(n * 512, 512)])

            pair(U_PAIR // 2, 0)
            with sp.Fori(1, MLA_HEADS // 2) as n:
                pair(U_PAIR // 2 + n * (PAIR_UNITS // 2), n)

            def ml(b0, h):
                for n in range(KT // 2):
                    s = n % RAW_SLOTS
                    for q in range(2):
                        dst = raw[:, s, 512 * q:512 * q + 512].rearrange("p (s c) -> p s c", s=2)
                        load(b0 + n, s, dst, w_qk_t[:, 2 * n + q, :, ds(h * DQK, DQK)])
                group(b0 + KT // 2, OFF_MV + h * DV)

            with sp.Fori(0, ML_HEADS) as h:
                ml(U_ML // 2 + h * KT, h)
            for n in range(RAW_SLOTS):
                for q in range(2):
                    load(U_GATE // 2 + n, n, raw[:, n, 512 * q:512 * q + 512], w_in_t[:, 2 * n + q, OFF_ZA:OFF_ZA + 512])
            group(U_GATE // 2, OFF_ZA, first=RAW_SLOTS)
            for g, off in enumerate((OFF_ZA, OFF_MO, OFF_ZB)):
                with sp.Fori(0 if g else 1, 4) as i:
                    group(U_GATE // 2 + g * 2 * KT + i * (KT // 2), off + i * 512)
            with sp.Fori(0, 8) as i:
                group(U_OUT // 2 + i * (KT // 2), i * 512, w_out_t)

        turns = KT // (2 * RAW_SLOTS)
        pair_turns = PAIR_UNITS // (2 * RAW_SLOTS)
        T_CQ = [0] * RAW_SLOTS
        T_CKV = [3 * turns] * RAW_SLOTS
        T_NAR = [4 * turns] * RAW_SLOTS
        T_PAIR = [4 * turns + 2] * RAW_SLOTS
        T_ML = [t + MLA_HEADS // 2 * pair_turns for t in T_PAIR]
        T_GATE = [t + ML_HEADS * 3 * turns + 1 for t in T_ML]
        T_OUT = [t + 12 * turns for t in T_GATE]

        def landed(before, local, extra=0, dmas=1):
            slot = (local // 2) % RAW_SLOTS
            return 16 * extra + 16 * (before[slot] + dmas * (local // (2 * RAW_SLOTS) + 1))

        def raw_unit(local, width):
            return raw[:, (local // 2) % RAW_SLOTS, (local % 2) * width:(local % 2) * width + width]

        def parts(local, width):
            src, hi, lo = raw_unit(local, width), whi[:, local % HL_SLOTS, 0:width], wlo[:, local % HL_SLOTS, 0:width]
            if width != 2 * (NOPE + ROPE):
                return [(src, hi, lo)]
            heads = src.rearrange("p (h c) -> p h c", h=2)
            return [(heads[:, :, a:z], hi[:, 2 * a:2 * z].rearrange("p (h c) -> p h c", h=2),
                     lo[:, 2 * a:2 * z].rearrange("p (h c) -> p h c", h=2)) for a, z in ((0, NOPE), (NOPE, NOPE + ROPE))]

        def steps(n, now, after, hooks=lambda k: None):
            for k in range(n):
                if k + AHEAD < n:
                    now(k + AHEAD)
                elif after is not None:
                    after(k + AHEAD - n)
                hooks(k)

        @block.scalar
        def _(act):
            nc.scalar.preload_act_table_set("natural_log_exp_and_others")
            act.dma_start(xt[2][0:TAIL, :], x_prompt[0, 240:256, :]).then_inc(xrow_in[2], 16)
            act.dma_start(xt[2][TAIL:48, :], x_sample[0, :, :]).then_inc(xrow_in[2], 16)
            act.dma_start(xt[0][0:N_META, :], meta).then_inc(xrow_in[0], 16)
            act.dma_start(xt[0][N_META:P, :], x_prompt[0, 0:P - N_META, :]).then_inc(xrow_in[0], 16)
            for half, t in enumerate((1, 3)):
                act.dma_start(xt[1][:, XH[half]], x_prompt[0, 112:240, XH[half]]).then_inc(xrow_in[t], 16)
            junk = attnT[:, :, :].rearrange("p a b -> p (a b)")

            def unit(u, local, t, width=512):
                if local % 2 == 0:
                    act.wait_ge(raw_in[(local // 2) % RAW_SLOTS], t)
                if not (isinstance(u, int) and u < HL_SLOTS):
                    act.wait_ge(unit_used, u - HL_SLOTS + 2)
                for src, hi, _ in parts(local, width):
                    ins = nc.scalar.copy(hi, src)
                ins.then_inc(hi_done, 1)

            act.wait_ge(eps_set, 1)
            for done, t in enumerate(X_ORDER):
                n = TOK[t][1]
                if t == 1:
                    act.wait_ge(xrow_in[1], 16)
                    act.wait_ge(xsq, 2)
                    nc.scalar.activation(junk[:, 0:D_MODEL // 2], xt[1][:, XH[0]], ACT.Square,
                                         accum_out=xss[:, 3:4]).then_inc(xsq, 1)
                    act.wait_ge(xrow_in[3], 16)
                    act.wait_ge(xsq, 3)
                    nc.scalar.activation(junk[:, 0:D_MODEL // 2], xt[1][:, XH[1]], ACT.Square,
                                         accum_out=xss[:, 1:2]).then_inc(xsq, 1)
                    act.wait_ge(xsq, 4)
                    act.wait_ge(xbias_d, 1)
                else:
                    act.wait_ge(xrow_in[t], 32)
                    if done:
                        act.wait_ge(xsq, done)
                    nc.scalar.activation(junk[0:n, 0:D_MODEL], xt[t][0:n, :], ACT.Square,
                                         accum_out=xss[0:n, t:t + 1]).then_inc(xsq, 1)
                    act.wait_ge(xsq, done + 1)
                nc.scalar.activation(xrs[0:n, t:t + 1], xss[0:n, t:t + 1], ACT.Ln, scale=1.0 / D_MODEL,
                                     bias=(xbias if t == 1 else epsc)[0:n, :]).then_inc(xln, 1)
                act.wait_ge(xln, done + 1)
                nc.scalar.activation(xrs[0:n, t:t + 1], xrs[0:n, t:t + 1], ACT.Exp, scale=-0.5).then_inc(xrstd, 1)

            def cq_units(i):
                return lambda k: unit(i * KT + k, k, landed(T_CQ, k, i * turns))

            for k in range(AHEAD - 1):
                cq_units(0)(k)
            act.wait_ge(free[4], use("gain", 4) + 1)

            def x_tile(k):
                b = 4 + k % 4
                act.wait_ge(full[b], use("x", b, k // 4) + 1)
                nc.scalar.activation(xhi[:, k, :], bank[b][:, 0:NT], ACT.Copy,
                                     scale=G[:, G_X + k:G_X + k + 1]).then_inc(xhi_d, 1)

            def cq_evict(i):
                for ct in (0, 2):
                    act.wait_ge(full[ct], use("cq", ct, 0, i) + 1)
                    nc.scalar.copy(cqraw[:, ds(i * 4 + ct, 1), :], bank[ct][:, 0:NQ]).then_inc(free[ct], 1)

            for k in range(4):
                x_tile(k)
                if k == 1:
                    cq_units(0)(AHEAD - 1)
            steps(KT, cq_units(0), cq_units(1), lambda k: x_tile(k + 4) if k + 4 < KT else None)
            cq_evict(0)
            with act.Fori(1, 3) as i:
                steps(KT, cq_units(i), cq_units(i + 1))
                cq_evict(i)

            def ckv_hooks(k):
                if k == 16:
                    act.wait_ge(full[4], use("ckv", 4) + 1)
                    nc.scalar.activation(rs3[:, 0, :], bank[4][:, 0:NQ], ACT.Ln, scale=1.0 / Q_LORA,
                                         bias=epsc[:, :]).then_inc(free[4], 1)
                    act.wait_ge(free[4], use("ckv", 4) + 1)
                    nc.scalar.activation(rs3[:, 0, :], rs3[:, 0, :], ACT.Exp, scale=-0.5).then_inc(cq_rs, 1)
                if 18 <= k < 18 + KQ:
                    t = k - 18
                    act.wait_ge(cq_n, t + 1)
                    nc.scalar.copy(cqhi[:, t, :], cqraw[:, t, :]).then_inc(cq_hi, 1)

            def narrow_units(k):
                unit(U_NAR + k, k, landed(T_NAR, k, 0, 2), 288)

            def pair_units(n):
                def split(k):
                    unit(U_PAIR + n * PAIR_UNITS + k, k, landed(T_PAIR, k, n * pair_turns), 384 if k < KQ else 512)
                return split

            steps(KT, lambda k: unit(U_CKV + k, k, landed(T_CKV, k)), narrow_units, ckv_hooks)
            for ct in (0, 2):
                act.wait_ge(full[ct], use("ckv", ct) + 1)
                nc.scalar.copy(ckvf[:, ct, :], bank[ct][:, 0:NT]).then_inc(free[ct], 1)

            def rstd(dst, src, scale, bank_no, used, done):
                act.wait_ge(full[bank_no], used + 1)
                nc.scalar.activation(dst, src, ACT.Ln, scale=scale, bias=epsc[:, :]).then_inc(free[bank_no], 1)
                act.wait_ge(free[bank_no], used + 1)
                nc.scalar.activation(dst, dst, ACT.Exp, scale=-0.5).then_inc(done, 1)

            def latent_norm(k):
                if k == 4:
                    rstd(rs2[:, 0, 0:NT], bank[5][:, 0:NT], 1.0 / KV_LORA, 5, use("latent", 5), ck_rs)
                if k == 6:
                    act.wait_ge(full[4], use("latent", 4) + 1)
                    nc.scalar.copy(ckhi[:, :, NT:NKV], bank[4][:, :].rearrange("p (t n) -> p t n", t=KC))\
                      .then_inc(ck_hi, 1)
                if k == 7:
                    for t in range(KC):
                        act.wait_ge(ck_n, t + 1)
                        nc.scalar.copy(ckhi[:, t, 0:NT], ckvf[:, t, :]).then_inc(ck_hi, 1)
            steps(NAR_UNITS, narrow_units, pair_units(0), latent_norm)

            def q_rstd(phase, i, n):
                for t in range(3):
                    b = 4 + t
                    nth = (0, 0, 0)[t] if phase == "bulk0" else (2, 4, 3)[t]
                    rstd(rs3[:, t, :], bank[b][:, 0:NQ], 1.0 / (NOPE if t < 2 else ROPE), b,
                         use(phase, b, nth, i), q_rs)

            def v_evict(phase, i, n):
                for half, b in ((0, 1), (1, 2)):
                    act.wait_ge(full[b], use(phase, b, 1, i) + 1)
                    if half == 0:
                        nc.scalar.copy(vt[:, 0:2, :], bank[b][:, :].rearrange("p (a c) -> p a c", a=2))\
                          .then_inc(free[b], 1)
                    else:
                        nc.scalar.copy(vt[0:48, 2, :], bank[b][0:48, 0:256]).then_inc(v_ev, 1)
                        nc.scalar.copy(vt[:, 3, :], bank[b][:, 256:512]).then_inc(free[b], 1)

            def latent(k):
                if k == 7:
                    rstd(rs2[:, 1, 0:NT], bank[6][:, 0:NT], 1.0 / ROPE, 6, use("latent", 6, 1), kp_rs)
                if k == 10:
                    for t, b in ((0, 4), (1, 5)):
                        act.wait_ge(full[b], use("latent", b, 1) + 1)
                        nc.scalar.copy(orow[:, 512 * t:512 * t + 512], bank[b][:, :]).then_inc(free[b], 1)
                    act.wait_ge(free[4], use("latent", 4, 1) + 1)
                    act.dma_start(ckv_p[0, 0:128, :], orow[:, 0:512]).then_inc(ck_out, 16)
                    act.wait_ge(free[5], use("latent", 5, 1) + 1)
                    act.dma_start(ckv_p[0, 128:256, :], orow[:, 512:1024]).then_inc(ck_out, 16)

            steps(PAIR_UNITS, pair_units(0), pair_units(1), latent)
            q_rstd("bulk0", 0, 0)
            act.wait_ge(ck_out, 32)
            act.wait_ge(ck_tail_out, 32)
            v_evict("bulk0", 0, 0)

            def k_rstd(phase, i, j):
                for t in range(2):
                    b = 6 + t
                    if t == 0:
                        act.wait_ge(q_fin, 2 * j + 2)
                        act.wait_ge(qp_fin, j + 1)
                    rstd(rs2[:, t, :], bank[b][:, 0:NKV], 1.0 / NOPE, b, use(phase, b, 0, i), k_rs)

            def exps(phase, i, j, h):
                hh = 2 * j + h
                if not (isinstance(j, int) and j == 0 and h == 0):
                    act.wait_ge(full[7], use(phase, 7, h, i) + 1)
                for t, (a, w, rows_) in enumerate(((0, 144, P), (144, 272, P), (416, 192, DEC))):
                    act.wait_ge(mx, 3 * hh + (2, 2, 3)[t])
                    src = bank[4][:, a:a + w] if t < 2 else bank[5][0:DEC, 0:w]
                    ins = nc.scalar.activation(prob[0:rows_, a:a + w], src, ACT.Exp, bias=nmax[0:rows_, t:t + 1],
                                               accum_out=psum_[0:rows_, t:t + 1])
                    ins.then_inc(ex, 1)

            def pt_main(phase, i, j, h):
                act.wait_ge(full[6], use(phase, 6, 1 + h, i) + 1)
                nc.scalar.copy(probT[:, 0:416], bank[6][:, 0:416]).then_inc(free[6], 1)

            def attn_evict(phase, i, j, h):
                act.wait_ge(full[5], use(phase, 5, 2 + h, i) + 1)
                nc.scalar.copy(attnT[:, ds(2 * j + h, 1), :], bank[5][:, 0:NQ]).then_inc(free[5], 1)

            def attention(phase, i, j):
                def hooks(k):
                    if k == 1:
                        k_rstd(phase, i, j)
                    if k == 6:
                        exps(phase, i, j, 0)
                    if k == 10:
                        pt_main(phase, i, j, 0)
                        exps(phase, i, j, 1)
                    if k == 12:
                        attn_evict(phase, i, j, 0)
                        pt_main(phase, i, j, 1)
                    if k == 13:
                        attn_evict(phase, i, j, 1)
                    if k == 15 and phase == "step":
                        q_rstd(phase, i, j + 1)
                return hooks

            def big_units(u, before, extra=0, dmas=1):
                return lambda k: unit(u + k, k, landed(before, k, extra, dmas))

            with act.Fori(0, 6) as j:
                steps(PAIR_UNITS, pair_units(j + 1), pair_units(j + 2), attention("step", j, j))
                v_evict("step", j, j + 1)
            steps(PAIR_UNITS, pair_units(7), big_units(U_ML, T_ML, 0, 2), attention("step", 6, 6))
            v_evict("step", 6, 7)

            steps(KT, big_units(U_ML, T_ML, 0, 2), big_units(U_ML + KT, T_ML, 2 * turns), attention("ml0qk", 0, 7))

            def qk_evict(phase, i, h):
                for ct in (0, 2):
                    act.wait_ge(full[ct], use(phase, ct, 0, i) + 1)
                    if ct == 0:
                        nc.scalar.copy(mqT[:, 0, N_META:NT], bank[0][:, N_META:NT]).then_inc(free[0], 1)
                    else:
                        nc.scalar.mul(mkT[:, 0, :], bank[2][:, 0:NT], DQK ** -0.5).then_inc(free[2], 1)

            def mv_evict(phase, nth, i, h):
                for ct in (0, 2):
                    act.wait_ge(full[ct], use(phase, ct, nth, i) + 1)
                    nc.scalar.copy(mvT[:, ct, :], bank[ct][:, 0:NT]).then_inc(free[ct], 1)

            qk_evict("ml0qk", 0, 0)

            def row_hooks(k):
                if k == 4:
                    act.wait_ge(free[5], use("rows", 5) + 1)
                    R = rows
                    nc.scalar.activation(R["mrow"][:, 0:NT], R["xf"][:, 0:NT], ACT.Abs).then_inc(r_abs, 1)
                    act.wait_ge(r_abs, 1)
                    nc.scalar.activation(R["mrow"][:, 0:NT], R["mrow"][:, 0:NT], ACT.Exp, scale=-1.0).then_inc(r_e, 1)
                    act.wait_ge(r_e, 1)
                    nc.scalar.activation(R["mrow"][:, 0:NT], R["mrow"][:, 0:NT], ACT.Ln, bias=1.0).then_inc(r_l, 1)
                if k == 12:
                    act.wait_ge(r_v, 11)
                    act.wait_ge(full[7], use("rows", 7) + 1)
                    for t, (_, n) in enumerate(MQT):
                        nc.scalar.activation(emcol[0:n, t, :], bank[7][0:n, 4 * t:4 * t + 4], ACT.Exp,
                                             scale=-1.0).then_inc(free[7] if t == 2 else r_em, 1)
            steps(KT, big_units(U_ML + KT, T_ML, 2 * turns), big_units(U_ML + 2 * KT, T_ML, 3 * turns, 2), row_hooks)
            mv_evict("ml0v", 0, 0, 0)

            def mlstm(phase, i, h):
                def hooks(k):
                    if k == 3:
                        act.wait_ge(full[4], use(phase, 4, 0, i) + 1)
                        nc.scalar.copy(Mb[:, :], bank[4][:, 0:NT + 1]).then_inc(free[4], 1)
                        act.wait_ge(free[4], use(phase, 4, 0, i) + 1)
                        act.wait_ge(nml_d, h + 1)
                        nc.scalar.activation(wi[:, :], Mb[:, C_SAMPLE:NT], ACT.Exp, scale=-1.0,
                                             bias=Mb[:, NT:NT + 1]).then_inc(wi_d, 1)
                        nc.scalar.activation(decay[:, :], Mb[:, NT:NT + 1], ACT.Exp,
                                             bias=nML[:, 1:2]).then_inc(dec_d, 1)
                        act.wait_ge(wt_d, h + 1)
                        nc.scalar.activation(wtmp[:, :], wtmp[:, :], ACT.Exp).then_inc(wt_x, 1)
                    if k == 5:
                        act.wait_ge(e_d, 3 * h + 3)
                        nc.scalar.activation(E[:, 0:464], E[:, 0:464], ACT.Exp, scale=-1.0).then_inc(e_x, 1)
                        nc.scalar.activation(E[0:48, 464:512], E[0:48, 464:512], ACT.Exp, scale=-1.0).then_inc(e_x, 1)
                    if k == 8:
                        act.wait_ge(full[6], use(phase, 6, 1, i) + 1)
                        nc.scalar.copy(vtok[:, 0, :], bank[6][:, :]).then_inc(free[6], 1)
                        act.wait_ge(full[7], use(phase, 7, 1, i) + 1)
                        nc.scalar.copy(vtok[:, 1, :], bank[7][:, :]).then_inc(free[7], 1)
                    if k == 16:
                        act.wait_ge(din_d, h + 1)
                        for t, (_, n) in enumerate(MQT):
                            b = 5 + t
                            act.wait_ge(full[b], use(phase, b, (1, 2, 2)[t], i) + 1)
                            if t:
                                act.wait_ge(hsq_d, 3 * h + t)
                            nc.scalar.activation(E[0:n, :], bank[b][0:n, :], ACT.Square, scale=dinv[0:n, t:t + 1],
                                                 accum_out=hss[0:n, t:t + 1]).then_inc(hsq_d, 1)
                        act.wait_ge(hsq_d, 3 * h + 3)
                        nc.scalar.activation(hss[:, :], hss[:, :], ACT.Ln, scale=1.0 / DV, bias=epsc[:, :])\
                          .then_inc(hln_d, 1)
                        act.wait_ge(hln_d, h + 1)
                        nc.scalar.activation(hss[:, :], hss[:, :], ACT.Exp, scale=-0.5).then_inc(hrs_d, 1)
                    if k == 26:
                        for d in range(2):
                            b = 5 + d
                            act.wait_ge(full[b], use(phase, b, 3 + d, i) + 1)
                            nc.scalar.copy(Cout[:, d, :], bank[b][:, :]).then_inc(free[b], 1)
                            act.wait_ge(free[b], use(phase, b, 3 + d, i) + 1)
                        act.dma_start(C_p[0, ds(h, 1), :, :].rearrange("a (d p) e -> p (a d) e", p=P),
                                      Cout[:, 0:2, :]).then_inc(Cp_out, 16)
                return hooks

            with act.Fori(0, 3) as h:
                qk = big_units(U_ML + 2 * KT + h * (2 * KT), T_ML, (h + 1) * (3 * turns), 2)
                v = big_units(U_ML + 3 * KT + h * (2 * KT), T_ML, (h + 1) * (3 * turns) + 2 * turns)
                steps(KT, qk, v, mlstm("ml", h, h))
                qk_evict("ml", h, h + 1)
                steps(KT, v, big_units(U_ML + 4 * KT + h * (2 * KT), T_ML, (h + 2) * (3 * turns), 2))
                mv_evict("ml", 1, h, h + 1)
                act.wait_ge(Cp_out, 16 * h + 16)

            def gate(phase, i, g, b0=0):
                for ct in range(4):
                    act.wait_ge(full[b0 + ct], use(phase, b0 + ct, 0, i) + 1)
                    if not (isinstance(g, int) and g == 0):
                        act.wait_ge(gm_d, 4 * g - 3 + ct)
                    ins = nc.scalar.activation(sg[:, ct, :], bank[b0 + ct][:, 0:NQ], ACT.Sigmoid)
                    ins.then_inc(sg_d, 1)

            def gate_units(g):
                return big_units(U_GATE + g * KT, T_GATE, g * turns)

            steps(KT, gate_units(0), gate_units(1), mlstm("gate0", 0, 3))
            gate("gate0", 0, 0)
            with act.Fori(0, 5) as g:
                steps(KT, gate_units(2 * g + 1), gate_units(2 * g + 2))
                gate("gates", g, 2 * g + 1, 4)
                steps(KT, gate_units(2 * g + 2), gate_units(2 * g + 3))
                gate("gates", g, 2 * g + 2)

            def mix(t):
                src = attnT[:, t, :] if t < 16 else hT[:, t - 16, :]
                nc.scalar.copy(mhi[:, t, :], src).then_inc(mix_hi, 1)

            def mix_attention(k):
                if k == 0:
                    act.wait_ge(gm_d, 4 * 4)
                if 1 <= k <= 16:
                    act.wait_ge(unit_used, U_GATE + 11 * KT + (k - 1) + 2)
                    mix(k - 1)
            steps(KT, gate_units(11), gate_units(12), mix_attention)
            gate("gate11", 0, 11, 4)

            def out_units(g):
                return big_units(U_OUT + g * KT, T_OUT, g * turns)

            def mix_mlstm(k):
                if k < 16:
                    act.wait_ge(gm_d, 4 * 8 + k + 1)
                    mix(16 + k)
            steps(KT, out_units(0), out_units(1), mix_mlstm)

            def y_evict(phase, i, g):
                for ct in (0, 2):
                    act.wait_ge(full[ct], use(phase, ct, 0, i) + 1)
                    if not (isinstance(g, int) and g == 0):
                        act.wait_ge(full[6], use("out", 6, 0, i) + 1)
                    nc.scalar.copy(yT[:, ct, :], bank[ct][:, 0:NQ]).then_inc(free[ct], 1)

            y_evict("out0", 0, 0)
            with act.Fori(0, 6) as g:
                steps(KT, out_units(g + 1), out_units(g + 2))
                y_evict("out", g, g + 1)
            steps(KT, out_units(7), None)
            y_evict("out", 6, 7)

        @block.vector
        def _(dve):
            tt, ts_, stt = nc.vector.tensor_tensor, nc.vector.tensor_scalar, nc.vector.scalar_tensor_tensor
            nc.vector.memset(epsc[:, :], EPS).then_inc(eps_set, 1)

            def unit(u, local, width=512):
                dve.wait_ge(hi_done, u + 1)
                for src, hi, lo in parts(local, width):
                    ins = tt(lo, src, hi.bitcast(f32), ALU.subtract)
                ins.then_inc(lo_done, 1)

            for done, t in enumerate(X_ORDER):
                n = TOK[t][1]
                if done == 2:
                    dve.wait_ge(full[4], use("gain", 4) + 1)
                    nc.vector.tensor_copy(G[:, :], bank[4][:, 0:G_ROWS]).then_inc(free[4], 1)
                    dve.wait_ge(xsq, 3)
                    ts_(xbias[:, :], xss[:, 3:4], 1.0 / D_MODEL, EPS, ALU.mult, ALU.add).then_inc(xbias_d, 1)
                dve.wait_ge(xrstd, done + 1)
                for q in range(X_PARTS if done == 2 else 1):
                    s = slice(q * D_MODEL // X_PARTS, (q + 1) * D_MODEL // X_PARTS) if done == 2 else slice(0, D_MODEL)
                    ts_(xt[t][0:n, s], xt[t][0:n, s], xrs[0:n, t:t + 1], None, ALU.mult).then_inc(xscaled, 1)

            def cq_units(i):
                return lambda k: unit(i * KT + k, k)

            def x_tile(k):
                b = 4 + k % 4
                dve.wait_ge(xhi_d, k + 1)
                stt(xlo[:, k, :], bank[b][:, 0:NT], G[:, G_X + k:G_X + k + 1], xhi[:, k, :].bitcast(f32),
                    ALU.mult, ALU.subtract).then_inc(free[b], 1)

            def cq_evict(i):
                for ct in (1, 3):
                    dve.wait_ge(full[ct], use("cq", ct, 0, i) + 1)
                    nc.vector.tensor_copy(cqraw[:, ds(i * 4 + ct, 1), :], bank[ct][:, 0:NQ]).then_inc(free[ct], 1)

            for k in range(4):
                x_tile(k)
                if k < AHEAD:
                    cq_units(0)(k)
            steps(KT, cq_units(0), cq_units(1), lambda k: x_tile(k + 4) if k + 4 < KT else None)
            cq_evict(0)
            with dve.Fori(1, 3) as i:
                steps(KT, cq_units(i), cq_units(i + 1))
                cq_evict(i)

            ts_(gsc[:, 0:1], G[:, G_QN:G_QN + 1], ATTN_SCALE, None, ALU.mult).then_inc(gsc_d, 1)
            ts_(gsc[:, 1:2], G[:, G_QR:G_QR + 1], ATTN_SCALE, None, ALU.mult).then_inc(gsc_d, 1)
            dve.wait_ge(gsc_d, 2)
            ts_(rotq[:, :], rot, gsc[:, 1:2], None, ALU.mult).then_inc(gsc_d, 1)
            nc.vector.memset(kpe2[0][64:P, :], 0.0).then_inc(kp_zero, 1)
            nc.vector.memset(kpe2[1][0:64, :], 0.0).then_inc(kp_zero, 1)
            ts_(rope1[:, 0:P], rot, G[:, G_KR:G_KR + 1], None, ALU.mult).then_inc(gsc_d, 1)

            def ckv_hooks(k):
                if 17 <= k < 17 + KQ + 1:
                    t = k - 17
                    if t == 0:
                        dve.wait_ge(cq_rs, 1)
                    if t < KQ:
                        stt(cqraw[:, t, :], cqraw[:, t, :], G[:, G_QA + t:G_QA + t + 1], rs3[:, 0, :],
                            ALU.mult, ALU.mult).then_inc(cq_n, 1)
                    if t > 0:
                        dve.wait_ge(cq_hi, t)
                        tt(cqlo[:, t - 1, :], cqraw[:, t - 1, :], cqhi[:, t - 1, :].bitcast(f32),
                           ALU.subtract).then_inc(cq_lo, 1)

            def narrow_units(k):
                unit(U_NAR + k, k, 288)

            def pair_units(n):
                return lambda k: unit(U_PAIR + n * PAIR_UNITS + k, k, 384 if k < KQ else 512)

            steps(KT, lambda k: unit(U_CKV + k, k), narrow_units, ckv_hooks)
            for ct in (1, 3):
                dve.wait_ge(full[ct], use("ckv", ct) + 1)
                nc.vector.tensor_copy(ckvf[:, ct, :], bank[ct][:, 0:NT]).then_inc(free[ct], 1)
            def latent_norm(k):
                if k == 5:
                    dve.wait_ge(ck_rs, 1)
                    for t in range(KC):
                        stt(ckvf[:, t, :], ckvf[:, t, :], G[:, G_KVA + t:G_KVA + t + 1], rs2[:, 0, 0:NT],
                            ALU.mult, ALU.mult).then_inc(ck_n, 1)
                if k == 6:
                    dve.wait_ge(ck_hi, 1)
                    tt(cklo[:, :, NT:NKV], bank[4][:, :].rearrange("p (t n) -> p t n", t=KC),
                       ckhi[:, :, NT:NKV].bitcast(f32), ALU.subtract).then_inc(free[4], 1)
                    dve.wait_ge(full[7], use("latent", 7) + 1)
                    nc.vector.tensor_copy(kpe2[0][0:64, NT:NKV], bank[7][0:64, 0:PAST]).then_inc(kp_st, 1)
                    nc.vector.tensor_copy(kpe2[1][64:P, NT:NKV], bank[7][64:P, 0:PAST]).then_inc(free[7], 1)
            steps(NAR_UNITS, narrow_units, pair_units(0), latent_norm)
            dve.wait_ge(full[0], use("narrow", 0) + 1)
            nc.vector.tensor_copy(nraw[:, :], bank[0][0:72, 0:NT]).then_inc(free[0], 1)

            def latent(k):
                if k == 0:
                    for t in range(KC):
                        dve.wait_ge(ck_hi, t + 2)
                        tt(cklo[:, t, 0:NT], ckvf[:, t, :], ckhi[:, t, 0:NT].bitcast(f32),
                           ALU.subtract).then_inc(ck_lo, 1)
                if k == 2:
                    dve.wait_ge(full[6], use("latent", 6) + 1)
                    nc.vector.tensor_copy(kpr, bank[6][:, 0:NT]).then_inc(free[6], 1)
                if k == 7:
                    dve.wait_ge(full[7], use("latent", 7, 1) + 1)
                    tt(rope2[:, :], bank[7][:, 0:NT], sinT, ALU.mult).then_inc(free[7], 1)
                    stt(rope1[:, :], kpr, G[:, G_KR:G_KR + 1], cosT, ALU.mult, ALU.mult).then_inc(kp_c, 1)
                if k == 9:
                    dve.wait_ge(kp_n, 1)
                    dve.wait_ge(kp_zero, 2)
                    nc.vector.tensor_copy(kpe2[0][0:64, 0:NT], kpe_n[0:64, :]).then_inc(kp_st, 1)
                    nc.vector.tensor_copy(kpe2[1][64:P, 0:NT], kpe_n[64:P, :]).then_inc(kp_st, 1)
                if k == 11:
                    dve.wait_ge(full[7], use("latent", 7, 2) + 1)
                    nc.vector.tensor_copy(kout[:, 0:128], bank[7][:, 0:128]).then_inc(kp_rows, 1)
                    nc.vector.tensor_copy(kout[0:48, 128:192], bank[7][0:48, 128:192]).then_inc(free[7], 1)

            def q_evict(phase, i, n):
                for t in range(3):
                    dve.wait_ge(full[t], use(phase, t, 0, i) + 1)
                    dst = qn[:, t, :] if t < 2 else qp[:, :]
                    nc.vector.tensor_copy(dst, bank[t][:, 0:NQ]).then_inc(free[t], 1)

            def q_norm(phase, i, n):
                nth = 0 if phase == "bulk0" else 3
                if phase == "bulk0":
                    dve.wait_ge(kp_out, 64)
                dve.wait_ge(full[7], use(phase, 7, nth, i) + 1)
                tt(rope2[:, 0:NQ], bank[7][:, 0:NQ], sinT[:, N_META:NT], ALU.mult).then_inc(free[7], 1)
                stt(rope1[:, 0:NQ], qp[:, :], gsc[:, 1:2], cosT[:, N_META:NT], ALU.mult, ALU.mult).then_inc(qp_c, 1)
                for t in range(2):
                    dve.wait_ge(q_rs, 3 * n + t + 1)
                    stt(qn[:, t, :], qn[:, t, :], gsc[:, 0:1], rs3[:, t, :], ALU.mult, ALU.mult).then_inc(q_fin, 1)

            def k_evict(phase, i, n, t):
                b = (3, 0)[t]
                dve.wait_ge(full[b], use(phase, b, (0, 1)[t], i) + 1)
                nc.vector.tensor_copy(kn[:, t, :], bank[b][:, 0:NKV]).then_inc(free[b], 1)

            def first_pair(k):
                latent(k)
                if k == KQ - 1:
                    q_evict("bulk0", 0, 0)
                    dve.wait_ge(full[6], use("latent", 6, 2) + 1)
                    dve.wait_ge(ck_out, 32)
                    nc.vector.tensor_copy(orow[0:48, 0:512], bank[6][0:48, :]).then_inc(free[6], 1)
            steps(PAIR_UNITS, pair_units(0), pair_units(1), first_pair)
            for t in range(2):
                k_evict("bulk0", 0, 0, t)
            q_norm("bulk0", 0, 0)

            def k_norm(j, t):
                dve.wait_ge(k_rs, 2 * j + t + 1)
                stt(kn[:, t, :], kn[:, t, :], G[:, G_KN:G_KN + 1], rs2[:, t, :], ALU.mult, ALU.mult)\
                    .then_inc(k_fin, 1)

            def maxima(phase, i, j, h):
                dve.wait_ge(full[4], use(phase, 4, h, i) + 1)
                nc.vector.tensor_reduce(nmax[:, 0:1], bank[4][:, 0:144], AX.X, ALU.max, negate=True).then_inc(mx, 1)
                nc.vector.tensor_reduce(nmax[:, 1:2], bank[4][:, 144:416], AX.X, ALU.max, negate=True).then_inc(mx, 1)
                dve.wait_ge(full[5], use(phase, 5, h, i) + 1)
                nc.vector.tensor_reduce(nmax[0:DEC, 2:3], bank[5][0:DEC, 0:192], AX.X, ALU.max, negate=True)\
                    .then_inc(mx, 1)

            def inverse(phase, i, j, h):
                dve.wait_ge(ex, 6 * j + 3 * h + 3)
                nc.vector.reciprocal(pinv[:, 0:2], psum_[:, 0:2]).then_inc(free[4], 1)
                nc.vector.reciprocal(pinv[0:DEC, 2:3], psum_[0:DEC, 2:3]).then_inc(free[5], 1)

            def pt_minor(phase, i, j, h):
                dve.wait_ge(full[7], use(phase, 7, 1 + h, i) + 1)
                nc.vector.tensor_copy(probT[0:TAIL, 416:704], bank[7][0:TAIL, 0:288]).then_inc(pt_d, 1)
                nc.vector.tensor_copy(probT[0:48, 704:736], bank[7][0:48, 288:320]).then_inc(free[7], 1)

            def attention(phase, i, j):
                def hooks(k):
                    if k in (2, 3):
                        k_norm(j, k - 2)
                    if k == 5:
                        maxima(phase, i, j, 0)
                    if k == 7:
                        inverse(phase, i, j, 0)
                    if k == 8:
                        maxima(phase, i, j, 1)
                    if k == 10:
                        pt_minor(phase, i, j, 0)
                        inverse(phase, i, j, 1)
                    if k == KQ - 1 and phase == "step":
                        q_evict(phase, i, j + 1)
                    if k == 12:
                        pt_minor(phase, i, j, 1)
                return hooks

            def pair_end(i, n):
                for t in range(2):
                    k_evict("step", i, n, t)
                q_norm("step", i, n)

            def big_units(u):
                return lambda k: unit(u + k, k)

            with dve.Fori(0, 6) as j:
                steps(PAIR_UNITS, pair_units(j + 1), pair_units(j + 2), attention("step", j, j))
                pair_end(j, j + 1)
            steps(PAIR_UNITS, pair_units(7), big_units(U_ML), attention("step", 6, 6))
            pair_end(6, 7)

            steps(KT, big_units(U_ML), big_units(U_ML + KT), attention("ml0qk", 0, 7))

            def qk_evict(phase, i, h):
                for ct in (1, 3):
                    dve.wait_ge(full[ct], use(phase, ct, 0, i) + 1)
                    if ct == 1:
                        nc.vector.tensor_copy(mqT[:, 1, N_META:NT], bank[1][:, N_META:NT]).then_inc(free[1], 1)
                    else:
                        ts_(mkT[:, 1, :], bank[3][:, 0:NT], DQK ** -0.5, None, ALU.mult).then_inc(free[3], 1)

            def mv_evict(phase, nth, i, h):
                for ct in (1, 3):
                    dve.wait_ge(full[ct], use(phase, ct, nth, i) + 1)
                    nc.vector.tensor_copy(mvT[:, ct, :], bank[ct][:, 0:NT]).then_inc(free[ct], 1)

            qk_evict("ml0qk", 0, 0)
            R = rows

            def scan(dst, data, a, b, init, op, other):
                return nc.vector.tensor_tensor_scan(dst[:, a:b], data[:, a:b], other[:, a:b], init, op[0], op[1])

            def row_hooks(k):
                if k == 3:
                    dve.wait_ge(gb_in, 48)
                    dve.wait_ge(full[4], use("rows", 4) + 1)
                    ts_(R["ig"][:, 0:NT], bank[4][0:ML_HEADS, 0:NT], gate_b[:, 0:1], None, ALU.add).then_inc(free[4], 1)
                    dve.wait_ge(full[5], use("rows", 5) + 1)
                    ts_(R["xf"][:, 0:NT], bank[5][0:ML_HEADS, 0:NT], gate_b[:, 1:2], None, ALU.add).then_inc(free[5], 1)
                    nc.vector.memset(R["crow"][:, :], 0.0).then_inc(r_v, 1)
                if k == 5:
                    dve.wait_ge(free[5], use("rows", 5) + 1)
                    dve.wait_ge(r_l, 1)
                    stt(R["lf"][:, 0:NT], R["xf"][:, 0:NT], 0.0, R["mrow"][:, 0:NT], ALU.min, ALU.subtract)\
                        .then_inc(r_v, 1)
                    dve.wait_ge(r_v, 2)
                    scan(R["bsum"], R["lf"], 0, C_SAMPLE, 0.0, (ALU.add, ALU.add), R["crow"]).then_inc(r_v, 1)
                    scan(R["bsum"], R["lf"], C_SAMPLE, NT, 0.0, (ALU.add, ALU.add), R["crow"]).then_inc(r_v, 1)
                if k == 6:
                    dve.wait_ge(r_v, 4)
                    tt(R["crow"][:, 0:NT], R["ig"][:, 0:NT], R["bsum"][:, 0:NT], ALU.subtract).then_inc(r_v, 1)
                    dve.wait_ge(r_v, 5)
                    scan(R["Mrow"], R["crow"], 0, C_SAMPLE, 0.0, (ALU.max, ALU.max), R["crow"]).then_inc(r_v, 1)
                    scan(R["Mrow"], R["crow"], C_SAMPLE, NT, gate_b[:, 2:3], (ALU.max, ALU.max), R["crow"])\
                        .then_inc(r_v, 1)
                    nc.vector.tensor_copy(R["Mrow"][:, NT:NT + 1], gate_b[:, 2:3]).then_inc(r_v, 1)
                if k == 7:
                    dve.wait_ge(r_v, 8)
                    tt(R["mrow"][:, 0:NT], R["bsum"][:, 0:NT], R["Mrow"][:, 0:NT], ALU.add).then_inc(r_v, 1)
                    nc.vector.memset(ccol[:, :, :], 0.0).then_inc(r_v, 1)
                    nc.vector.memset(emcol[:, :, :], 1.0).then_inc(r_v, 1)
                    nc.vector.memset(dsb[:, :], 1.0).then_inc(r_v, 1)
                    nc.vector.memset(hss[:, :], 1.0).then_inc(r_v, 1)
                    nc.vector.memset(qw[:, :, :], 0.0).then_inc(qw_z, 1)
                if k == 13:
                    dve.wait_ge(r_v, 13)
                    dve.wait_ge(full[6], use("rows", 6) + 1)
                    for t, (_, n) in enumerate(TOK):
                        nc.vector.tensor_copy(ccol[0:n, t, :], bank[6][0:n, 4 * t:4 * t + 4])\
                            .then_inc(free[6] if t == 2 else r_c, 1)
            steps(KT, big_units(U_ML + KT), big_units(U_ML + 2 * KT), row_hooks)
            mv_evict("ml0v", 0, 0, 0)

            def mlstm(phase, i, h):
                first = isinstance(h, int) and h == 0

                def hooks(k):
                    if k == 0:
                        dve.wait_ge(free[6], use("rows", 6) + 1)
                        ts_(Mh[:, :], R["Mrow"][:, :], ident[0:ML_HEADS, ds(h, 1)], None, ALU.mult).then_inc(mh_d, 1)
                    if k == 3:
                        dve.wait_ge(free[4], use(phase, 4, 0, i) + 1)
                        ts_(nML[:, 0:1], Mb[:, C_SAMPLE - 1:C_SAMPLE], -1.0, None, ALU.mult).then_inc(nml_s, 1)
                        ts_(nML[:, 1:2], Mb[:, NT - 1:NT], -1.0, None, ALU.mult).then_inc(nml_d, 1)
                        dve.wait_ge(nml_s, h + 1)
                        dve.wait_ge(nml_d, h + 1)
                        ts_(wtmp[:, 0:3], ccol[:, :, ds(h, 1)].rearrange("p t a -> p (t a)"), nML[:, 0:1], 0.0,
                            ALU.add, ALU.min).then_inc(wt_p, 1)
                        ts_(wtmp[:, 3:4], ccol[:, 2, ds(h, 1)], nML[:, 1:2], 0.0, ALU.add, ALU.min).then_inc(wt_d, 1)
                        for t, (at, w) in enumerate(MLW):
                            n = TOK[t][1]
                            ts_(E[0:n, at:at + w], Mb[0:n, NT - w:NT], ccol[0:n, t, ds(h, 1)], 0.0,
                                ALU.subtract, ALU.max).then_inc(e_d, 1)
                    if k == 5:
                        dve.wait_ge(wt_x, h + 1)
                        tt(wtmp[:, :], wtmp[:, :], c("rowmask"), ALU.mult).then_inc(wt_m, 1)
                        dve.wait_ge(wt_m, h + 1)
                        dve.wait_ge(full[6], use(phase, 6, 0, i) + 1)
                        ts_(kws[:, 0, :], bank[6][:, 0:256], wtmp[:, 0:1], None, ALU.mult).then_inc(kws_d, 1)
                        ts_(kws[:, 1, :], bank[6][:, 256:512], wtmp[:, 1:2], None, ALU.mult).then_inc(free[6], 1)
                        dve.wait_ge(full[7], use(phase, 7, 0, i) + 1)
                        ts_(kws[0:48, 2, :], bank[7][0:48, 0:256], wtmp[0:48, 2:3], None, ALU.mult).then_inc(kws_d, 1)
                        ts_(kws[0:48, 3, :], bank[7][0:48, 0:256], wtmp[0:48, 3:4], None, ALU.mult).then_inc(free[7], 1)
                        dve.wait_ge(wi_d, h + 1)
                        dve.wait_ge(qw_z, 1)
                        for d in range(2):
                            tt(qw[:, d, TAIL:48], mqT[:, d, C_SAMPLE:NT], wi[:, :], ALU.mult).then_inc(qw_d, 1)
                    if k == 7:
                        dve.wait_ge(full[5], use(phase, 5, 0, i) + 1)
                        dve.wait_ge(e_m, 2 * h + 2)
                        tt(Pt[:, 0:464], bank[5][:, 0:464], E[:, 0:464], ALU.mult).then_inc(p_d, 1)
                        tt(Pt[0:48, 464:512], bank[5][0:48, 464:512], E[0:48, 464:512], ALU.mult).then_inc(free[5], 1)
                        dve.wait_ge(full[4], use(phase, 4, 1, i) + 1)
                        nc.vector.tensor_copy(vtok[0:48, 2, :], bank[4][0:48, :]).then_inc(free[4], 1)
                    if k == 14:
                        dve.wait_ge(full[4], use(phase, 4, 2, i) + 1)
                        nc.vector.tensor_copy(dsb[:, 0:2], bank[4][:, 0:2]).then_inc(den_d, 1)
                        nc.vector.tensor_copy(dsb[0:48, 2:3], bank[4][0:48, 2:3]).then_inc(free[4], 1)
                        dve.wait_ge(den_d, h + 1)
                        dve.wait_ge(free[4], use(phase, 4, 2, i) + 1)
                        stt(dinv[:, :], dsb[:, :], -1.0, dsb[:, :], ALU.mult, ALU.max).then_inc(dab_d, 1)
                        dve.wait_ge(dab_d, h + 1)
                        tt(dinv[:, :], dinv[:, :], emcol[:, :, ds(h, 1)].rearrange("p t a -> p (t a)"),
                           ALU.max).then_inc(dmx_d, 1)
                        dve.wait_ge(dmx_d, h + 1)
                        nc.vector.reciprocal(dinv[:, :], dinv[:, :]).then_inc(din_d, 1)
                    if k == 19:
                        dve.wait_ge(hrs_d, h + 1)
                        tt(hfac[:, :], dinv[:, :], hss[:, :], ALU.mult).then_inc(hf_d, 1)
                        dve.wait_ge(hf_d, h + 1)
                        for t, (_, n) in enumerate(MQT):
                            b = 5 + t
                            ts_(hn[0:n, t, :], bank[b][0:n, :], hfac[0:n, t:t + 1], None, ALU.mult)\
                                .then_inc(free[b], 1)
                    if k == 24:
                        for e in range(4):
                            b = 4 + e
                            dve.wait_ge(full[b], use(phase, b, (3, 2, 3, 3)[e], i) + 1)
                            ts_(hT[:, ds(4 * h + e, 1), :], bank[b][:, 0:NQ], G[:, ds(G_MLO + 4 * h + e, 1)], None,
                                ALU.mult).then_inc(free[b], 1)
                    if k == 30:
                        dve.wait_ge(C0_in, 16 * (h + 1))
                        dve.wait_ge(dec_d, h + 1)
                        for d in range(2):
                            b = 5 + d
                            dve.wait_ge(full[b], use(phase, b, 4 + d, i) + 1)
                            stt(Cout[:, 2 + d, :], C0[:, d, :], decay[:, :], bank[b][:, :], ALU.mult, ALU.add)\
                                .then_inc(free[b], 1)
                        dve.wait_ge(full[7], use(phase, 7, 4, i) + 1)
                        nc.vector.tensor_copy(ncol[:, ds(2 * h, 2)], bank[7][:, 0:2]).then_inc(n_d, 1)
                        stt(ncol[:, ds(8 + 2 * h, 2)], G[:, ds(G_N0 + 2 * h, 2)], decay[:, :], bank[7][:, 2:4],
                            ALU.mult, ALU.add).then_inc(free[7], 1)
                return hooks

            with dve.Fori(0, 3) as h:
                qk = big_units(U_ML + 2 * KT + h * (2 * KT))
                v = big_units(U_ML + 3 * KT + h * (2 * KT))
                steps(KT, qk, v, mlstm("ml", h, h))
                qk_evict("ml", h, h + 1)
                steps(KT, v, big_units(U_ML + 4 * KT + h * (2 * KT)))
                mv_evict("ml", 1, h, h + 1)
                dve.wait_ge(Cs_out, 16 * h + 16)

            def silu(phase, i, g, b0=0):
                for ct in range(4):
                    dve.wait_ge(sg_d, 4 * g + ct + 1)
                    tt(gt[:, ct, :], bank[b0 + ct][:, 0:NQ], sg[:, ct, :], ALU.mult).then_inc(free[b0 + ct], 1)

            steps(KT, big_units(U_GATE), big_units(U_GATE + KT), mlstm("gate0", 0, 3))
            silu("gate0", 0, 0)
            with dve.Fori(0, 5) as g:
                odd, even, after = (big_units(U_GATE + n * KT + g * (2 * KT)) for n in (1, 2, 3))
                steps(KT, odd, even)
                silu("gates", g, 2 * g + 1, 4)
                steps(KT, even, after)
                silu("gates", g, 2 * g + 2)

            def mix(t):
                dve.wait_ge(mix_hi, t + 1)
                src = attnT[:, t, :] if t < 16 else hT[:, t - 16, :]
                tt(mlo[:, t, :], src, mhi[:, t, :].bitcast(f32), ALU.subtract).then_inc(mix_lo, 1)

            def last_gate(k):
                if 1 <= k <= 16:
                    mix(k - 1)
                if k == 6:
                    dve.wait_ge(full[0], use("nout", 0) + 1)
                    nc.vector.tensor_copy(nrow[:, :], bank[0][0:16, 0:P]).then_inc(free[0], 1)
            steps(KT, big_units(U_GATE + 11 * KT), big_units(U_OUT), last_gate)
            silu("gate11", 0, 11, 4)

            steps(KT, big_units(U_OUT), big_units(U_OUT + KT), lambda k: mix(16 + k) if k < 16 else None)

            def y_evict(phase, i, g):
                for ct in (1, 3):
                    dve.wait_ge(full[ct], use(phase, ct, 0, i) + 1)
                    if not (isinstance(g, int) and g == 0):
                        dve.wait_ge(full[6], use("out", 6, 0, i) + 1)
                    nc.vector.tensor_copy(yT[:, ct, :], bank[ct][:, 0:NQ]).then_inc(free[ct], 1)

            def add_rows(phase, i, g):
                for t, (_, n) in enumerate(QT):
                    b = 4 + t
                    dve.wait_ge(full[b], use(phase, b, 0, i) + 1)
                    tt(ytok[0:n, t, :], bank[b][0:n, :], xres[0:n, t, :], ALU.add).then_inc(free[b], 1)

            y_evict("out0", 0, 0)
            def out_hooks(g):
                def hooks(k):
                    if k == 4:
                        dve.wait_ge(xres_in, g * 48 + 48)
                        add_rows("out", g, g)
                return hooks

            with dve.Fori(0, 6) as g:
                steps(KT, big_units(U_OUT + KT + g * KT), big_units(U_OUT + 2 * KT + g * KT), out_hooks(g))
                y_evict("out", g, g + 1)
                dve.wait_ge(y_out, g * 48 + 48)
            steps(KT, big_units(U_OUT + 7 * KT), None, out_hooks(6))
            y_evict("out", 6, 7)
            dve.wait_ge(y_out, 7 * 48)
            dve.wait_ge(xres_in, 8 * 48)
            add_rows("outlast", 0, 7)

        @block.tensor
        def _(pe):
            mm, tr = nc.tensor.matmul, nc.tensor.transpose

            def mm3(out, w_hi, w_lo, m_hi, m_lo, start, stop, opens=False, **kw):
                ins = mm(out, w_hi, m_hi, start=start, stop=False, **kw)
                if opens:
                    ins.then_inc(unit_used, 1)
                mm(out, w_hi, m_lo, start=False, stop=False, **kw)
                return mm(out, w_lo, m_hi, start=False, stop=stop, **kw)

            def apart():
                pe.sem_inc(passed_pe, 1)

            def fill(phase, b, nth=0, i=0):
                before = use(phase, b, nth, i)
                if not (isinstance(before, int) and before == 0):
                    pe.wait_ge(free[b], before)

            pe.wait_ge(const_in, 16)
            pe.wait_ge(grows_in, 16 * 11)
            tr(bank[4][:, 0:G_ROWS], Grows[:, :], ident[0:G_ROWS, 0:G_ROWS]).then_inc(full[4], 1)

            def x_tile(k):
                b = 4 + k % 4
                fill("x", b, k // 4)
                for t, (c0, n) in enumerate(TOK):
                    if t == 0 and k % (KT // X_PARTS) == 0:
                        pe.wait_ge(xscaled, 3 + k // (KT // X_PARTS))
                    ins = tr(bank[b][:, c0:c0 + n], xt[t][0:n, k * P:(k + 1) * P], ident[0:n, 0:n])
                ins.then_inc(full[b], 1)

            def group(u, phase, nth, i, c0, hooks=lambda k: None, a_hi=xhi, a_lo=xlo, ready=None, x_ready=False,
                      queries=0, b0=0):
                n = NT - c0
                for k in range(KT):
                    pe.wait_ge(lo_done, u + k + 1)
                    if ready is not None:
                        pe.wait_ge(ready, k + 1)
                    if x_ready:
                        pe.wait_ge(free[4 + k % 4], use("x", 4 + k % 4, k // 4) + 1)
                    for ct in range(4):
                        if k == 0:
                            fill(phase, b0 + ct, nth, i)
                        s = slice(ct * P, ct * P + P)
                        skip = N_META if ct < queries else 0
                        mc = slice(0, NQ) if a_hi is mhi else slice(c0 + skip, NT)
                        ins = mm3(bank[b0 + ct][:, skip:n], whi[:, k % HL_SLOTS, s], wlo[:, k % HL_SLOTS, s],
                                  a_hi[:, k, mc], a_lo[:, k, mc], k == 0, k == KT - 1, k == 0 and ct == 0)
                        if k == KT - 1:
                            ins.then_inc(full[b0 + ct], 1)
                    if k < KT - 1:
                        ins.then_inc(unit_used, 1)
                    hooks(k)

            for k in range(4):
                x_tile(k)
            group(0, "cq", 0, 0, N_META, lambda k: x_tile(k + 4) if k + 4 < KT else None, x_ready=True)
            with pe.Fori(1, 3) as i:
                group(i * KT, "cq", 0, i, N_META)

            def cq_squares(k):
                if 2 <= k < 2 + KQ:
                    t = k - 2
                    if t == 0:
                        fill("ckv", 4)
                    pe.wait_ge(cq_sq, t + 1)
                    ins = mm(bank[4][:, 0:NQ], ones, sq3[:, t % 3, :], start=t == 0, stop=t == KQ - 1)
                    ins.then_inc(full[4] if t == KQ - 1 else cq_ssm, 1)
            group(U_CKV, "ckv", 0, 0, 0, cq_squares)

            for k in range(NAR_UNITS):
                pe.wait_ge(lo_done, U_NAR + k + 1)
                if k == 0:
                    fill("narrow", 0)
                for q in range(4):
                    s = slice(72 * q, 72 * q + 72)
                    kk = 4 * k + q
                    ins = mm3(bank[0][0:72, 0:NT], whi[:, k % HL_SLOTS, s], wlo[:, k % HL_SLOTS, s],
                              xhi[:, kk, :], xlo[:, kk, :], kk == 0, kk == KT - 1, kk == 0)
                ins.then_inc(full[0] if k == NAR_UNITS - 1 else unit_used, 1)
                if k == 2:
                    fill("latent", 5)
                    for t in range(KC):
                        pe.wait_ge(ck_sq, t + 1)
                        ins = mm(bank[5][:, 0:NT], ones, sq2[:, t % 2, 0:NT], start=t == 0, stop=t == KC - 1)
                        ins.then_inc(full[5] if t == KC - 1 else ck_ssm, 1)
                if k == 4:
                    pe.wait_ge(cache_in, 48)
                    fill("latent", 4)
                    for t in range(KC):
                        ins = tr(bank[4][:, t * P:t * P + P], cacher[:, t * P:t * P + P], ident)
                    ins.then_inc(full[4], 1)
                    fill("latent", 7)
                    tr(bank[7][:, 0:P], cacher[:, 512:640], ident).then_inc(full[7], 1)

            def q_units(n, phase, i, hooks):
                for k in range(KQ):
                    pe.wait_ge(lo_done, U_PAIR + n * PAIR_UNITS + k + 1)
                    if isinstance(n, int):
                        pe.wait_ge(cq_lo, k + 1)
                    for t in range(3):
                        if k == 0:
                            fill(phase, t, 0, i)

                        def cols(w):
                            return w[:, k % HL_SLOTS, P * t:P * t + P]
                        ins = mm3(bank[t][:, 0:NQ], cols(whi), cols(wlo), cqhi[:, k, :], cqlo[:, k, :],
                                  k == 0, k == KQ - 1, k == 0 and t == 0)
                        if k == KQ - 1:
                            ins.then_inc(full[t], 1)
                    if k < KQ - 1:
                        ins.then_inc(unit_used, 1)
                    hooks(k)

            def kv_units(n, phase, i, hooks):
                for k in range(KC):
                    slot = (KQ + k) % HL_SLOTS
                    pe.wait_ge(lo_done, U_PAIR + n * PAIR_UNITS + KQ + k + 1)
                    last = k == KC - 1
                    for h, b in ((0, 3), (1, 0)):
                        if k == 0:
                            fill(phase, b, (0, 1)[h], i)
                        s = slice(256 * h, 256 * h + P)
                        ins = mm3(bank[b][:, 0:NKV], whi[:, slot, s], wlo[:, slot, s], ckhi[:, k, :], cklo[:, k, :],
                                  k == 0, last, k == 0 and h == 0)
                        if last:
                            ins.then_inc(full[b], 1)

                    def vcols(w):
                        return w[:, slot, :].rearrange("p (h c) -> p h c", h=2)[:, :, NOPE:256]
                    for t, c0 in enumerate((0, P, 2 * P, NT)):
                        m = P
                        b, half = 1 + t // 2, t % 2
                        if k == 0 and half == 0:
                            fill(phase, b, 1, i)
                        out = bank[b][0:m, 256 * half:256 * half + 256].rearrange("p (h c) -> p h c", h=2)
                        cs = slice(c0, c0 + m)
                        mm(out, ckhi[:, k, cs], vcols(whi), start=k == 0 and half == 0, stop=False,
                           skip_group_check=True)
                        mm(out, cklo[:, k, cs], vcols(whi), start=False, stop=False, skip_group_check=True)
                        ins = mm(out, ckhi[:, k, cs], vcols(wlo), start=False, stop=last, skip_group_check=True)
                        if last and half == 1:
                            ins.then_inc(full[b], 1)
                    if not last:
                        ins.then_inc(unit_used, 1)
                    hooks(KQ + k)

            def q_squares(phase, i, n):
                first = phase == "bulk0"
                for t in range(3):
                    b = 4 + t
                    pe.wait_ge(q_sq, 3 * n + t + 1)
                    fill(phase, b, 0 if first else (2, 4, 3)[t], i)
                    mm(bank[b][:, 0:NQ], ones if t < 2 else blockones, sq3[:, t, :], start=True, stop=True)\
                        .then_inc(full[b], 1)
                pe.wait_ge(gsc_d, 3)
                fill(phase, 7, 0 if first else 3, i)
                mm(bank[7][:, 0:NQ], rotq[:, :], qp[:, :], start=True, stop=True).then_inc(full[7], 1)

            def latent(k):
                if k == 1:
                    pe.wait_ge(free[0], use("narrow", 0) + 1)
                    fill("latent", 6)
                    mm(bank[6][:, 0:NT], dup, nraw[0:64, :], start=True, stop=True).then_inc(full[6], 1)
                if k == 5:
                    pe.wait_ge(kp_sq, 1)
                    fill("latent", 6, 1)
                    mm(bank[6][:, 0:NT], blockones, sqk0, start=True, stop=True).then_inc(full[6], 1)
                    fill("latent", 7, 1)
                    pe.wait_ge(gsc_d, 4)
                    mm(bank[7][:, 0:NT], rope1[:, 0:P], kpr, start=True, stop=True).then_inc(full[7], 1)
                if k == 8:
                    pe.wait_ge(ck_n, KC)
                    for t, (c0, n) in enumerate(TOK):
                        b = 4 + t
                        fill("latent", b, (1, 1, 2)[t])
                        for f in range(KC):
                            ins = tr(bank[b][0:n, f * P:f * P + P], ckvf[:, f, c0:c0 + n], ident)
                        ins.then_inc(full[b], 1)
                if k == 10:
                    pe.wait_ge(kp_n, 1)
                    fill("latent", 7, 2)
                    for t, (c0, n) in enumerate(TOK):
                        ins = tr(bank[7][0:n, 64 * t:64 * t + 64], kpe_n[0:64, c0:c0 + n], ident[0:64, 0:64])
                    ins.then_inc(full[7], 1)
            q_units(0, "bulk0", 0, latent)
            pe.wait_ge(ck_lo, KC)
            pe.wait_ge(free[4], use("latent", 4) + 1)
            kv_units(0, "bulk0", 0, lambda k: q_squares("bulk0", 0, 0) if k == KQ + 1 else None)

            def k_squares(phase, i, j):
                for t in range(2):
                    b = 6 + t
                    pe.wait_ge(k_sq, 2 * j + t + 1)
                    fill(phase, b, 0, i)
                    mm(bank[b][:, 0:NKV], ones, sq2[:, t, :], start=True, stop=True).then_inc(full[b], 1)

            def scores(phase, i, j, h):
                if h == 0:
                    pe.wait_ge(q_fin, 2 * j + 2)
                    pe.wait_ge(qp_fin, j + 1)
                    pe.wait_ge(kp_st, 3)
                    pe.wait_ge(free[7], use("latent", 7) + 1)
                pe.wait_ge(k_fin, 2 * j + h + 1)
                fill(phase, 4, h, i)
                ind, neg = c("causal_ind"), c("causal_neg")
                for q0, at, keys in ((0, 0, N_META + P), (P, 144, C_SAMPLE)):
                    out = bank[4][:, at:at + keys]
                    mm(out, qn[:, h, q0:q0 + P], kn[:, h, 0:keys], start=True, stop=False)
                    mm(bank[4][:, at + keys - CHUNK:at + keys], ind, neg, start=False, stop=False)
                    ins = mm(out, qp[:, q0:q0 + P], kpe2[h][:, 0:keys], start=False, stop=True)
                ins.then_inc(full[4], 1)
                fill(phase, 5, h, i)
                for a, k0, w in ((0, 0, N_META), (N_META, 256, NKV - 256)):
                    out = bank[5][0:DEC, a:a + w]
                    mm(out, qn[:, h, SEQ:NQ], kn[:, h, k0:k0 + w], start=True, stop=False)
                    if a:
                        mm(bank[5][0:DEC, a:a + TAIL], ind[:, 0:DEC], neg[:, 0:TAIL], start=False, stop=False)
                    ins = mm(out, qp[:, SEQ:NQ], kpe2[h][:, k0:k0 + w], start=False, stop=True)
                ins.then_inc(full[5], 1)

            def transposes(phase, i, j, h):
                pe.wait_ge(pn, 6 * j + 3 * h + 3)
                fill(phase, 6, 1 + h, i)
                for at, a, m in ((0, 0, P), (128, 144, P), (256, 272, P)):
                    tr(bank[6][:, at:at + m], prob[:, a:a + P], ident)
                tr(bank[6][:, 384:416], prob[0:DEC, 480:608], ident[0:DEC, 0:DEC]).then_inc(full[6], 1)
                fill(phase, 7, 1 + h, i)
                tr(bank[7][0:TAIL, 0:128], prob[:, 128:144], ident)
                tr(bank[7][0:TAIL, 128:256], prob[:, 400:416], ident)
                tr(bank[7][0:TAIL, 256:288], prob[0:DEC, 416:432], ident[0:DEC, 0:DEC])
                tr(bank[7][0:48, 288:320], prob[0:DEC, 432:480], ident[0:DEC, 0:DEC]).then_inc(full[7], 1)

            def weighted(phase, i, j, h):
                pe.wait_ge(v_ev, j + 1)
                pe.wait_ge(free[6], use(phase, 6, 1 + h, i) + 1)
                pe.wait_ge(free[7], use(phase, 7, 1 + h, i) + 1)
                fill(phase, 5, 2 + h, i)
                vh = slice(P * h, P * h + P)
                for cols, parts in (
                        (slice(0, 128), ((0, P, 0), (1, TAIL, 416))),
                        (slice(128, 256), ((0, P, 128), (1, P, 256), (2, TAIL, 544))),
                        (slice(256, 288), ((0, TAIL, 672), (2, 48, 704), (3, P, 384)))):
                    w = cols.stop - cols.start
                    for n, (t, k, at) in enumerate(parts):
                        ins = mm(bank[5][:, cols], vt[0:k, t, vh], probT[0:k, at:at + w], start=n == 0,
                                 stop=n == len(parts) - 1)
                ins.then_inc(full[5], 1)

            def attention(phase, i, j):
                def hooks(k):
                    if k == 1:
                        k_squares(phase, i, j)
                    if k == 5:
                        scores(phase, i, j, 0)
                    if k == 8:
                        scores(phase, i, j, 1)
                    if k == 9:
                        transposes(phase, i, j, 0)
                    if k == 11:
                        weighted(phase, i, j, 0)
                    if k == 12:
                        transposes(phase, i, j, 1)
                    if k == 13:
                        weighted(phase, i, j, 1)
                    if k == 14 and phase == "step":
                        q_squares(phase, i, j + 1)
                return hooks

            with pe.Fori(0, 7) as j:
                q_units(j + 1, "step", j, attention("step", j, j))
                kv_units(j + 1, "step", j, attention("step", j, j))
            group(U_ML, "ml0qk", 0, 0, 0, attention("ml0qk", 0, 7), queries=2)

            def row_hooks(k):
                if k == 1:
                    for b, a in ((4, 64), (5, 68)):
                        fill("rows", b)
                        mm(bank[b][0:ML_HEADS, 0:NT], ident[0:72, a:a + 4], nraw[:, :], start=True, stop=True)\
                            .then_inc(full[b], 1)
                if k == 9:
                    pe.wait_ge(r_v, 9)
                    fill("rows", 6)
                    for t, (c0, n) in enumerate(TOK):
                        ins = tr(bank[6][0:n, 4 * t:4 * t + 4], R4["crow"][:, c0:c0 + n], ident[0:4, 0:4])
                    ins.then_inc(full[6], 1)
                    fill("rows", 7)
                    for t, (q0, n) in enumerate(MQT):
                        ins = tr(bank[7][0:n, 4 * t:4 * t + 4], R4["mrow"][:, N_META + q0:N_META + q0 + n],
                                 ident[0:4, 0:4])
                    ins.then_inc(full[7], 1)
            R4 = rows
            group(U_ML + KT, "ml0v", 0, 0, 0, row_hooks)

            def mlstm(phase, i, h):
                blocks = [slice(at, at + w) for at, w in MLW]

                def hooks(k):
                    if k == 1:
                        pe.wait_ge(mh_d, h + 1)
                        fill(phase, 4, 0, i)
                        mm(bank[4][:, 0:NT + 1], ones[0:ML_HEADS, :], Mh[:, :], start=True, stop=True)\
                            .then_inc(full[4], 1)
                        qk_ready(h)
                        fill(phase, 6, 0, i)
                        for t in range(2):
                            for d in range(2):
                                ins = tr(bank[6][:, 256 * t + P * d:256 * t + P * d + P],
                                         mkT[:, d, TOK[t][0]:TOK[t][0] + P], ident)
                        ins.then_inc(full[6], 1)
                        fill(phase, 7, 0, i)
                        apart()
                        for d in range(2):
                            ins = tr(bank[7][0:48, P * d:P * d + P], mkT[:, d, 256:NT], ident)
                        ins.then_inc(full[7], 1)
                    if k == 3:
                        fill(phase, 5, 0, i)
                        for t, (c0, n) in enumerate(TOK):
                            for d in range(2):
                                ins = mm(bank[5][0:n, blocks[t]], mkT[:, d, c0:c0 + n],
                                         mqT[:, d, NT - MLW[t][1]:NT], start=d == 0, stop=d == 1)
                        ins.then_inc(full[5], 1)
                    if k == 6:
                        for t, b, nth in ((0, 6, 1), (1, 7, 1), (2, 4, 1)):
                            c0, n = TOK[t]
                            fill(phase, b, nth, i)
                            apart()
                            for e in range(4):
                                ins = tr(bank[b][0:n, P * e:P * e + P], mvT[:, e, c0:c0 + n], ident)
                            ins.then_inc(full[b], 1)
                    if k == 12:
                        pe.wait_ge(p_d, h + 1)
                        pe.wait_ge(free[5], use(phase, 5, 0, i) + 1)
                        pe.wait_ge(free[4], use(phase, 4, 1, i) + 1)
                        pe.wait_ge(free[6], use(phase, 6, 1, i) + 1)
                        pe.wait_ge(free[7], use(phase, 7, 1, i) + 1)
                        pe.wait_ge(qw_d, 2 * h + 2)
                        pe.wait_ge(C0_in, 16 * (h + 1))
                        for q, (q0, m) in enumerate(MQT):
                            b = 5 + q
                            fill(phase, b, (1, 2, 2)[q], i)
                            for t in range(q + 1):
                                at = MLW[t][0] + q0 - (NQ - MLW[t][1])
                                n = TOK[t][1]
                                ins = mm(bank[b][0:m, :], Pt[0:n, at:at + m], vtok[0:n, t, :], start=t == 0,
                                         stop=t == q and q < 2)
                            if q == 2:
                                for d in range(2):
                                    ins = mm(bank[b][0:m, :], qw[:, d, :], C0[:, d, :], start=False, stop=d == 1)
                            ins.then_inc(full[b], 1)
                        fill(phase, 4, 2, i)
                        for q, (q0, m) in enumerate(MQT):
                            m = P if q == 0 else m
                            for t in range(q + 1):
                                at = MLW[t][0] + q0 - (NQ - MLW[t][1])
                                n = TOK[t][1]
                                ins = mm(bank[4][0:m, q:q + 1], Pt[0:n, at:at + m], ones[0:n, 0:1], start=t == 0,
                                         stop=t == q and q < 2)
                            if q == 2:
                                for d in range(2):
                                    ins = mm(bank[4][0:m, q:q + 1], qw[:, d, :], G[:, ds(G_N0 + 2 * h + d, 1)],
                                             start=False, stop=d == 1)
                        ins.then_inc(full[4], 1)
                    if k == 22:
                        for q in range(3):
                            pe.wait_ge(free[5 + q], use(phase, 5 + q, (1, 2, 2)[q], i) + 1)
                        for e in range(4):
                            b = 4 + e
                            fill(phase, b, (3, 2, 3, 3)[e], i)
                            for q, (q0, m) in enumerate(MQT):
                                ins = tr(bank[b][:, q0:q0 + m], hn[0:m, q, P * e:P * e + P], ident[0:m, 0:m])
                            ins.then_inc(full[b], 1)
                    if k == 25:
                        pe.wait_ge(kws_d, 2 * h + 2)
                        for d in range(2):
                            b = 5 + d
                            fill(phase, b, 3 + d, i)
                            for t in range(3):
                                n = TOK[t][1]
                                ins = mm(bank[b][:, :], kws[0:n, t, P * d:P * d + P], vtok[0:n, t, :],
                                         start=t == 0, stop=t == 2)
                            ins.then_inc(full[b], 1)
                    if k == 28:
                        for d in range(2):
                            b = 5 + d
                            fill(phase, b, 4 + d, i)
                            mm(bank[b][:, :], kws[0:48, 3, P * d:P * d + P], vtok[0:48, 2, :], start=True, stop=True)\
                                .then_inc(full[b], 1)
                        fill(phase, 7, 4, i)
                        for d in range(2):
                            for t in range(3):
                                n = TOK[t][1]
                                mm(bank[7][:, d:d + 1], kws[0:n, t, P * d:P * d + P], ones[0:n, 0:1],
                                   start=t == 0, stop=t == 2)
                        for d in range(2):
                            ins = mm(bank[7][:, 2 + d:3 + d], kws[0:48, 3, P * d:P * d + P], ones[0:48, 0:1],
                                     start=True, stop=True)
                        ins.then_inc(full[7], 1)
                return hooks

            def qk_ready(h):
                for b in range(4):
                    pe.wait_ge(free[b], use("ml0v", b) + 1 + 2 * h)

            with pe.Fori(0, 3) as h:
                group(U_ML + 2 * KT + h * (2 * KT), "ml", 0, h, 0, mlstm("ml", h, h), queries=2)
                group(U_ML + 3 * KT + h * (2 * KT), "ml", 1, h, 0)
            group(U_GATE, "gate0", 0, 0, N_META, mlstm("gate0", 0, 3))
            with pe.Fori(0, 5) as g:
                group(U_GATE + KT + g * (2 * KT), "gates", 0, g, N_META, b0=4)
                group(U_GATE + 2 * KT + g * (2 * KT), "gates", 0, g, N_META)

            def normalisers(k):
                if k == 4:
                    pe.wait_ge(free[7], use("gates", 7))
                    fill("nout", 0)
                    tr(bank[0][0:16, 0:P], ncol[:, :], ident).then_inc(full[0], 1)
            group(U_GATE + 11 * KT, "gate11", 0, 0, N_META, normalisers, b0=4)
            group(U_OUT, "out0", 0, 0, N_META, a_hi=mhi, a_lo=mlo, ready=mix_lo)

            def y_rows(phase, i):
                for b in range(4):
                    pe.wait_ge(free[b], use(phase, b, 0, i) if phase == "out" else use("outlast", b))
                for t, (q0, m) in enumerate(QT):
                    b = 4 + t
                    fill(phase, b, 0, i)
                    for ct in range(4):
                        ins = tr(bank[b][0:m, ct * P:ct * P + P], yT[:, ct, q0:q0 + m], ident)
                    ins.then_inc(full[b], 1)

            with pe.Fori(0, 7) as g:
                group(U_OUT + KT + g * KT, "out", 0, g, N_META,
                      lambda k: y_rows("out", g) if k == 2 else None, a_hi=mhi, a_lo=mlo)
            y_rows("outlast", 0)

        @block.gpsimd
        def _(pool):
            tt, ts_ = nc.gpsimd.tensor_tensor, nc.gpsimd.tensor_scalar

            def apart():
                pool.sem_inc(passed_pool, 1)

            def rows_of(v, n):
                return v.rearrange("(r c) -> r c", c=P) if n > 1 else v.rearrange("(a c) -> a c", a=1)
            pool.dma_start(Grows[G_X:G_X + 32, :], rows_of(norm_gain, 32)).then_inc(grows_in, 16)
            pool.dma_start(Grows[G_QA:G_QA + 12, :], rows_of(q_a, 12)).then_inc(grows_in, 16)
            pool.dma_start(Grows[G_KVA:G_KVA + 4, :], rows_of(kv_a, 4)).then_inc(grows_in, 16)
            pool.dma_start(Grows[G_MLO:G_MLO + 16, :], ml_out.rearrange("h (r c) -> (h r) c", c=P)).then_inc(grows_in, 16)
            pool.dma_start(Grows[G_QN:G_QN + 1, :], rows_of(q_nope, 1)).then_inc(grows_in, 16)
            pool.dma_start(Grows[G_KN:G_KN + 1, :], rows_of(k_nope, 1)).then_inc(grows_in, 16)
            for half in range(2):
                s = slice(64 * half, 64 * half + 64)
                pool.dma_start(Grows[G_QR:G_QR + 1, s], rows_of(q_rope, 1)).then_inc(grows_in, 16)
                pool.dma_start(Grows[G_KR:G_KR + 1, s], rows_of(k_rope, 1)).then_inc(grows_in, 16)
            pool.dma_start(Grows[G_N0:G_N0 + 8, :], state_n[0].rearrange("h (r c) -> (h r) c", c=P)).then_inc(grows_in, 16)
            pool.dma_start(con[:, :], consts).then_inc(const_in, 16)
            pool.dma_start(gate_b[:, 0:1], b_ig.rearrange("(h a) -> h a", a=1)).then_inc(gb_in, 16)
            pool.dma_start(gate_b[:, 1:2], b_fg.rearrange("(h a) -> h a", a=1)).then_inc(gb_in, 16)
            pool.dma_start(gate_b[:, 2:3], state_m.rearrange("a h -> h a")).then_inc(gb_in, 16)
            for b in range(4, 8):
                pool.wait_ge(full[b], use("cq", b))
            pool.dma_start(cacher[:, 0:512], cache_ckv[0]).then_inc(cache_in, 16)
            pool.dma_start(cacher[:, 512:576], cache_kpe[0]).then_inc(cache_in, 16)
            pool.dma_start(cacher[:, 576:640], cache_kpe[0]).then_inc(cache_in, 16)

            for ct in range(4):
                pool.wait_ge(free[ct], use("ckv", ct))
            for t in range(KQ):
                if t >= 3:
                    pool.wait_ge(cq_ssm, t - 2)
                tt(sq3[:, t % 3, :], cqraw[:, t, :], cqraw[:, t, :], ALU.mult).then_inc(cq_sq, 1)
            for ct in range(4):
                pool.wait_ge(free[ct], use("narrow", ct) if ct else use("ckv", 0) + 1)
            pool.wait_ge(full[4], use("ckv", 4) + 1)
            for t in range(KC):
                if t >= 2:
                    pool.wait_ge(ck_ssm, t - 1)
                tt(sq2[:, t % 2, 0:NT], ckvf[:, t, :], ckvf[:, t, :], ALU.mult).then_inc(ck_sq, 1)
            pool.wait_ge(free[6], use("latent", 6) + 1)
            pool.wait_ge(full[5], use("latent", 5) + 1)
            tt(sqk0, kpr, kpr, ALU.mult).then_inc(kp_sq, 1)
            pool.wait_ge(kp_c, 1)
            pool.wait_ge(free[7], use("latent", 7, 1) + 1)
            tt(rope1[:, :], rope1[:, :], rope2[:, :], ALU.add).then_inc(kp_a, 1)
            pool.wait_ge(kp_a, 1)
            pool.wait_ge(kp_rs, 1)
            tt(kpe_n, rope1[:, :], rs2[:, 1, 0:NT], ALU.mult).then_inc(kp_n, 1)
            def q_square(phase, i, n):
                for t in range(3):
                    pool.wait_ge(free[t], use(phase, t, 0, i) + 1)
                    src = qn[:, t, :] if t < 2 else qp[:, :]
                    tt(sq3[:, t, :], src, src, ALU.mult).then_inc(q_sq, 1)

            def k_square(phase, i, n):
                for t, b in ((0, 3), (1, 0)):
                    pool.wait_ge(free[b], use(phase, b, (0, 1)[t], i) + 1)
                    for q in range(3):
                        pool.wait_ge(full[4 + q], use(phase, 4 + q, (0 if phase == "bulk0" else (2, 4, 3)[q]), i) + 1)
                    tt(sq2[:, t, :], kn[:, t, :], kn[:, t, :], ALU.mult).then_inc(k_sq, 1)

            def q_turn(phase, i, n):
                pool.wait_ge(qp_c, n + 1)
                pool.wait_ge(free[7], use(phase, 7, 0 if phase == "bulk0" else 3, i) + 1)
                tt(rope1[:, 0:NQ], rope1[:, 0:NQ], rope2[:, 0:NQ], ALU.add).then_inc(qp_a, 1)
                pool.wait_ge(qp_a, n + 1)
                pool.wait_ge(q_rs, 3 * n + 3)
                tt(qp[:, :], rope1[:, 0:NQ], rs3[:, 2, :], ALU.mult).then_inc(qp_fin, 1)

            def norm_probs(phase, i, j, h):
                pool.wait_ge(free[4], use(phase, 4, h, i) + 1)
                apart()
                ts_(prob[:, 0:144], prob[:, 0:144], pinv[:, 0:1], None, ALU.mult).then_inc(pn, 1)
                ts_(prob[:, 144:416], prob[:, 144:416], pinv[:, 1:2], None, ALU.mult).then_inc(pn, 1)
                pool.wait_ge(free[5], use(phase, 5, h, i) + 1)
                apart()
                ts_(prob[0:DEC, 416:608], prob[0:DEC, 416:608], pinv[0:DEC, 2:3], None, ALU.mult).then_inc(pn, 1)

            q_square("bulk0", 0, 0)
            pool.wait_ge(kp_rows, 1)
            pool.wait_ge(free[7], use("latent", 7, 2) + 1)
            pool.dma_start(kpe_p[0, 0:128, :], kout[:, 0:64]).then_inc(kp_out, 16)
            pool.dma_start(kpe_p[0, 128:256, :], kout[:, 64:128]).then_inc(kp_out, 16)
            pool.dma_start(kpe_p[0, 256:272, :], kout[0:TAIL, 128:192]).then_inc(kp_out, 16)
            pool.dma_start(kpe_s[0, :, :], kout[TAIL:48, 128:192]).then_inc(kp_out, 16)
            pool.wait_ge(free[6], use("latent", 6, 2) + 1)
            pool.dma_start(ckv_p[0, 256:272, :], orow[0:TAIL, 0:512]).then_inc(ck_tail_out, 16)
            pool.dma_start(ckv_s[0, :, :], orow[TAIL:48, 0:512]).then_inc(ck_tail_out, 16)
            k_square("bulk0", 0, 0)
            q_turn("bulk0", 0, 0)
            with pool.Fori(0, 7) as j:
                norm_probs("step", j, j, 0)
                norm_probs("step", j, j, 1)
                q_square("step", j, j + 1)
                k_square("step", j, j + 1)
                q_turn("step", j, j + 1)
            norm_probs("ml0qk", 0, 7, 0)
            norm_probs("ml0qk", 0, 7, 1)

            for h in range(2):
                pool.wait_ge(free[5], use("ml0qk", 5, 2 + h) + 1)
            pool.dma_start(mask[:, :], mlmask).then_inc(mask_in, 16)
            pool.wait_ge(r_v, 9)
            pool.dma_start(m_p.rearrange("a h -> h a"), rows["mrow"][:, C_SAMPLE - 1:C_SAMPLE]).then_inc(m_out, 16)
            pool.dma_start(m_s.rearrange("a h -> h a"), rows["mrow"][:, NT - 1:NT]).then_inc(m_out, 16)

            def mlstm(phase, i, h):
                pool.dma_start(C0[:, :, :], state_C[0, ds(h, 1), :, :].rearrange("a (d p) e -> p (a d) e", p=P))\
                    .then_inc(C0_in, 16)
                pool.wait_ge(mask_in, 16)
                pool.wait_ge(e_x, 2 * h + 2)
                tt(E[:, 0:464], E[:, 0:464], mask[:, 0:464], ALU.mult).then_inc(e_m, 1)
                tt(E[0:48, 464:512], E[0:48, 464:512], mask[0:48, 464:512], ALU.mult).then_inc(e_m, 1)
                for d in range(2):
                    pool.wait_ge(free[5 + d], use(phase, 5 + d, 4 + d, i) + 1)
                    apart()
                pool.dma_start(C_s[0, ds(h, 1), :, :].rearrange("a (d p) e -> p (a d) e", p=P),
                               Cout[:, 2:4, :]).then_inc(Cs_out, 16)

            with pool.Fori(0, 3) as h:
                mlstm("ml", h, h)
                pool.wait_ge(Cs_out, 16 * h + 16)
                apart()
            mlstm("gate0", 0, 3)

            def apply(phase, i, dst, at, src, b0=0):
                for ct in range(4):
                    pool.wait_ge(free[b0 + ct], use(phase, b0 + ct, 0, i) + 1)
                    tt(dst[:, ds(at + ct, 1), :], dst[:, ds(at + ct, 1), :], src[:, ct:ct + 1, :], ALU.mult)\
                        .then_inc(gm_d, 1)

            apply("gate0", 0, attnT, 0, gt)
            apply("gates", 0, attnT, 4, gt, 4)
            apply("gates", 0, attnT, 8, gt)
            apply("gates", 1, attnT, 12, gt, 4)
            apply("gates", 1, hT, 0, sg)
            apply("gates", 2, hT, 4, sg, 4)
            apply("gates", 2, hT, 8, sg)
            apply("gates", 3, hT, 12, sg, 4)
            apply("gates", 3, hT, 0, gt)
            apply("gates", 4, hT, 4, gt, 4)
            apply("gates", 4, hT, 8, gt)
            pool.wait_ge(free[0], use("nout", 0) + 1)
            pool.dma_start(n_p[0].rearrange("h (r c) -> (h r) c", c=P), nrow[0:8, :]).then_inc(n_out, 16)
            pool.dma_start(n_s[0].rearrange("h (r c) -> (h r) c", c=P), nrow[8:16, :]).then_inc(n_out, 16)
            apply("gate11", 0, hT, 12, gt, 4)

            def fetch_x(g):
                cs = ds(g * 512, 512)
                pool.dma_start(xres[:, 0, :], x_prompt[0, 0:128, cs]).then_inc(xres_in, 16)
                pool.dma_start(xres[:, 1, :], x_prompt[0, 128:256, cs]).then_inc(xres_in, 16)
                pool.dma_start(xres[0:DEC, 2, :], x_sample[0, :, cs]).then_inc(xres_in, 16)

            def store_y(phase, i, g):
                cs = ds(g * 512, 512)
                for t, dst in enumerate((y_p[0, 0:128, cs], y_p[0, 128:256, cs], y_s[0, :, cs])):
                    pool.wait_ge(free[4 + t], use(phase, 4 + t, 0, i) + 1)
                    apart()
                    pool.dma_start(dst, ytok[0:QT[t][1], t, :]).then_inc(y_out, 16)

            pool.wait_ge(n_out, 32)
            fetch_x(0)
            with pool.Fori(0, 7) as g:
                store_y("out", g, g)
                fetch_x(g + 1)
            store_y("outlast", 0, 7)
            pool.wait_ge(y_out, 8 * 48)
            pool.wait_ge(Cp_out, 4 * 16)
            pool.wait_ge(Cs_out, 4 * 16)
            pool.wait_ge(m_out, 32)
            pool.wait_ge(ck_out, 32)
            pool.wait_ge(ck_tail_out, 32)
            pool.wait_ge(kp_out, 4 * 16)


_INS = ["x_prompt", "x_sample", "cache_ckv", "cache_kpe", "state_C", "state_n", "state_m", "meta_tokens",
        "norm_gain", "w_in", "b_igate", "b_fgate", "q_a_norm", "w_q_up", "q_nope_norm", "q_rope_norm",
        "kv_a_norm", "k_rope_norm", "w_kv_up", "k_nope_norm", "ml_out_norm", "w_out"]
_OUTS = [(1, SEQ, D_MODEL), (1, DEC, D_MODEL), (1, N_META + SEQ, KV_LORA), (1, N_META + SEQ, ROPE),
         (1, ML_HEADS, DQK, DV), (1, ML_HEADS, DQK), (1, ML_HEADS), (1, DEC, KV_LORA), (1, DEC, ROPE),
         (1, ML_HEADS, DQK, DV), (1, ML_HEADS, DQK), (1, ML_HEADS)]


def kernel(**inputs):
    import concourse.bacc as bacc
    from concourse.bass_utils import run_bass_kernel_spmd

    nc = bacc.Bacc("TRN2", target_bir_lowering=False, num_devices=1)
    arrays, args = {}, []
    table, mask = shape_constants()
    for name, a in [(n, inputs[n]) for n in _INS] + [("shape_table", table), ("mlstm_mask", mask)]:
        a = np.ascontiguousarray(a)
        arrays[f"in_{name}_dram"] = a
        args.append(nc.dram_tensor(f"in_{name}_dram", a.shape, mybir.dt.from_np(a.dtype),
                                   kind="ExternalInput").ap())
    for i, shape in enumerate(_OUTS):
        args.append(nc.dram_tensor(f"out_{i}_dram", shape, mybir.dt.float32, kind="ExternalOutput").ap())
    hymba_step(nc, *args)
    r = run_bass_kernel_spmd(nc, [arrays], core_ids=[0])
    return tuple(r.results[0][f"out_{i}_dram"] for i in range(len(_OUTS)))
```
